# Optimizing a Trainium2 kernel written in Bass

```python
import jax
import jax.numpy as jnp
from jax import lax
import numpy as np

D_MODEL = 1024
BATCH = 1
SEQ = 256
DEPTH = 2

GRID_W = 64
HEAD_DIM = 64
NORM_EPS = 1e-6
RW_HEADS = 8
RW_DIM = RW_HEADS * HEAD_DIM
DECAY_RANK = 64
ICLR_RANK = 64
GATE_RANK = 128
RWKV_GN_EPS = 64e-5
RW_IN = 3 * RW_DIM + DECAY_RANK + ICLR_RANK + GATE_RANK
ATT_HEADS = 8
ATT_KV_HEADS = 2
ATT_DIM = ATT_HEADS * HEAD_DIM
ATT_KV_DIM = ATT_KV_HEADS * HEAD_DIM
ATT_IN = ATT_DIM + 2 * ATT_KV_DIM
Q_BLOCK = 128
ROPE_THETA = 10000.0
E_IN = RW_IN + ATT_IN
GLA_HEADS = 4
GLA_DK = D_MODEL // 2
GLA_DV = D_MODEL
GLA_DKH = GLA_DK // GLA_HEADS
GLA_DVH = GLA_DV // GLA_HEADS
GLA_GATE_RANK = 16
GLA_GATE_NORM = 16.0
GLA_CHUNK = 64
O_IN = 2 * GLA_DK + GLA_DV + GLA_GATE_RANK + GLA_DV
D_FF = 2816
N_EXPERTS = 8
TOP_K = 2
D_FF_EXPERT = 3584
MOE_BLOCK = 128
N_EVEN = (DEPTH + 1) // 2
N_ODD = DEPTH // 2

kernel_name = 'hybrid_rwkv7_gqa_gla_moe_encoder'

def rms_norm(x, g, eps=NORM_EPS):
    xf = x.astype(jnp.float32)
    y = xf * lax.rsqrt(jnp.mean(xf * xf, axis=-1, keepdims=True) + eps)
    return (y * g.astype(jnp.float32)).astype(x.dtype)

def swiglu(h, w_gate, w_up, w_down):
    return (jax.nn.silu(h @ w_gate) * (h @ w_up)) @ w_down

def centred_shift(x):
    prev = jnp.pad(x, ((0, 0), (1, 0), (0, 0)))[:, :-1]
    nxt = jnp.pad(x, ((0, 0), (0, 1), (0, 0)))[:, 1:]
    return 0.5 * (prev + nxt)

def rwkv7_scan(r, w, k, v, a, b, reverse):
    Bn, S, H, N = r.shape

    def step(state, inp):
        r_t, w_t, k_t, v_t, a_t, b_t = inp
        sa = jnp.einsum('bhvk,bhk->bhv', state, a_t)
        new = state * w_t[:, :, None, :] + sa[..., None] * b_t[:, :, None, :] + v_t[..., None] * k_t[:, :, None, :]
        read = state if reverse else new
        return new, jnp.einsum('bhvk,bhk->bhv', read, r_t)

    xs = tuple(jnp.moveaxis(t, 1, 0) for t in (r, w, k, v, a, b))
    init = jnp.zeros((Bn, H, N, N), jnp.float32)
    _, out = lax.scan(step, init, xs, reverse=reverse)
    return jnp.moveaxis(out, 0, 1)

def rwkv7_mixer(p, shift_mu, w0_f, w_up_f, w0_b, w_up_b, a0_f, a_up_f, a0_b, a_up_b, g_up, k_k, k_a, r_k, gn_w, gn_b):
    Bn, S, _ = p.shape
    p = p + (centred_shift(p) - p) * shift_mu
    o1 = 3 * RW_DIM
    o2 = o1 + DECAY_RANK
    o3 = o2 + ICLR_RANK
    r = p[..., :RW_DIM]
    k = p[..., RW_DIM:2 * RW_DIM]
    v = p[..., 2 * RW_DIM:o1]
    wd = jnp.tanh(p[..., o1:o2])
    ad = p[..., o2:o3]
    g = jax.nn.sigmoid(p[..., o3:]) @ g_up

    def heads(t):
        return t.reshape(Bn, S, RW_HEADS, HEAD_DIM).astype(jnp.float32)

    def per_head(c):
        return c.reshape(RW_HEADS, HEAD_DIM).astype(jnp.float32)

    rh, kh, vh = heads(r), heads(k), heads(v)
    kk = kh * per_head(k_k)
    kk = kk / jnp.maximum(jnp.sqrt(jnp.sum(kk * kk, axis=-1, keepdims=True)), 1e-12)

    def direction(w0, w_up, a0, a_up, reverse):
        z = (w0 + wd @ w_up).astype(jnp.float32)
        w = heads(jnp.exp(-jnp.exp(-jax.nn.softplus(-z) - 0.5)))
        a = heads(jax.nn.sigmoid((a0 + ad @ a_up).astype(jnp.float32)))
        kd = kh * (1.0 + (a - 1.0) * per_head(k_a))
        return rwkv7_scan(rh, w, kd, vh, -kk, kk * a, reverse), kd

    y_f, k_fwd = direction(w0_f, w_up_f, a0_f, a_up_f, False)
    y_b, _ = direction(w0_b, w_up_b, a0_b, a_up_b, True)
    y = y_f + y_b
    mean = jnp.mean(y, axis=-1, keepdims=True)
    var = jnp.mean(jnp.square(y - mean), axis=-1, keepdims=True)
    y = ((y - mean) * lax.rsqrt(var + RWKV_GN_EPS)).reshape(Bn, S, RW_DIM)
    y = y * gn_w.astype(jnp.float32) + gn_b.astype(jnp.float32)
    bonus = jnp.sum(rh * k_fwd * per_head(r_k), axis=-1, keepdims=True) * vh
    y = (y + bonus.reshape(Bn, S, RW_DIM)) * g.astype(jnp.float32)
    return y.astype(p.dtype)

def axial_rope_tables(S):
    rows = S // GRID_W
    row = jnp.repeat(jnp.arange(rows), GRID_W).astype(jnp.float32)
    col = jnp.tile(jnp.arange(GRID_W), rows).astype(jnp.float32)
    half = HEAD_DIM // 2
    freq = ROPE_THETA ** (-jnp.arange(0, half, 2, dtype=jnp.float32) / half)
    ang = jnp.concatenate([row[:, None] * freq, col[:, None] * freq], axis=-1)
    return jnp.cos(ang), jnp.sin(ang)

def apply_rope(x, cos, sin):
    xp = x.reshape(x.shape[:-1] + (HEAD_DIM // 2, 2))
    x0, x1 = xp[..., 0], xp[..., 1]
    c = cos[None, :, None, :]
    s = sin[None, :, None, :]
    return jnp.stack([x0 * c - x1 * s, x0 * s + x1 * c], axis=-1).reshape(x.shape)

def gqa_axial_attention(p, q_norm, k_norm):
    Bn, S, _ = p.shape
    G = ATT_HEADS // ATT_KV_HEADS
    q = p[..., :ATT_DIM].reshape(Bn, S, ATT_HEADS, HEAD_DIM)
    k = p[..., ATT_DIM:ATT_DIM + ATT_KV_DIM].reshape(Bn, S, ATT_KV_HEADS, HEAD_DIM)
    v = p[..., ATT_DIM + ATT_KV_DIM:].reshape(Bn, S, ATT_KV_HEADS, HEAD_DIM)
    cos, sin = axial_rope_tables(S)
    q = apply_rope(rms_norm(q, q_norm).astype(jnp.float32), cos, sin) * (HEAD_DIM ** -0.5)
    k = apply_rope(rms_norm(k, k_norm).astype(jnp.float32), cos, sin)
    nb = S // Q_BLOCK
    qb = q.reshape(Bn, nb, Q_BLOCK, ATT_KV_HEADS, G, HEAD_DIM).transpose(1, 0, 3, 4, 2, 5)

    def block(q_blk):
        s = jnp.einsum('bkgqd,bskd->bkgqs', q_blk, k)
        pr = jax.nn.softmax(s, axis=-1).astype(v.dtype)
        return jnp.einsum('bkgqs,bskd->bqkgd', pr, v)

    o = lax.map(block, qb)
    return o.transpose(1, 0, 2, 3, 4, 5).reshape(Bn, S, ATT_DIM).astype(p.dtype)

def gla_chunked(q, k, v, g, strict):
    Bn, H, S, dk = q.shape
    dv = v.shape[-1]
    C = GLA_CHUNK
    n = S // C
    q = q.reshape(Bn, H, n, C, dk)
    k = k.reshape(Bn, H, n, C, dk)
    g = g.reshape(Bn, H, n, C, dk)
    v = v.reshape(Bn, H, n, C, dv)
    b = jnp.cumsum(g, axis=3)
    b_mid = b[:, :, :, C // 2:C // 2 + 1]
    b_last = b[:, :, :, C - 1:C]
    att = jnp.einsum('bhnid,bhnjd->bhnij', q * jnp.exp(b - b_mid), k * jnp.exp(b_mid - b))
    mask = jnp.tril(jnp.ones((C, C), dtype=bool), k=-1 if strict else 0)
    att = jnp.where(mask, att, 0.0)
    o = jnp.einsum('bhnij,bhnjv->bhniv', att, v)
    kv = jnp.einsum('bhncd,bhncv->bhndv', k * jnp.exp(b_last - b), v)
    dec = jnp.exp(b_last[:, :, :, 0, :])

    def step(state, inp):
        d, kv_n = inp
        return state * d[..., None] + kv_n, state

    init = jnp.zeros((Bn, H, dk, dv), jnp.float32)
    _, states = lax.scan(step, init, (jnp.moveaxis(dec, 2, 0), jnp.moveaxis(kv, 2, 0)))
    states = jnp.moveaxis(states, 0, 2)
    o = o + jnp.einsum('bhncd,bhndv->bhncv', q * jnp.exp(b), states)
    return o.reshape(Bn, H, S, dv)

def gla_mixer(p, gate_up_f, gate_bias_f, gate_up_b, gate_bias_b, out_norm):
    Bn, S, _ = p.shape
    o1 = GLA_DK
    o2 = 2 * GLA_DK
    o3 = o2 + GLA_DV
    o4 = o3 + GLA_GATE_RANK
    gd = p[..., o3:o4]
    og = p[..., o4:]

    def heads(t, d):
        return t.reshape(Bn, S, GLA_HEADS, d).transpose(0, 2, 1, 3).astype(jnp.float32)

    qh = heads(p[..., :o1], GLA_DKH) * (GLA_DKH ** -0.5)
    kh = heads(p[..., o1:o2], GLA_DKH)
    vh = heads(p[..., o2:o3], GLA_DVH)

    def log_gate(up, bias):
        return heads(jax.nn.log_sigmoid((gd @ up + bias).astype(jnp.float32)) / GLA_GATE_NORM, GLA_DKH)

    def flip(t):
        return jnp.flip(t, axis=2)

    o_f = gla_chunked(qh, kh, vh, log_gate(gate_up_f, gate_bias_f), strict=False)
    o_b = flip(gla_chunked(flip(qh), flip(kh), flip(vh), flip(log_gate(gate_up_b, gate_bias_b)), strict=True))
    o = rms_norm(o_f + o_b, out_norm)
    o = o.transpose(0, 2, 1, 3).reshape(Bn, S, GLA_DV).astype(p.dtype)
    return o * jax.nn.silu(og)

def moe_swiglu(h, router, w_gate, w_up, w_down):
    Bn, S, D = h.shape
    T = Bn * S
    A = T * TOP_K
    hf = h.reshape(T, D)
    logits = (hf @ router).astype(jnp.float32)
    top_val, top_idx = lax.top_k(logits, TOP_K)
    gates = jax.nn.softmax(top_val, axis=-1)
    e_flat = top_idx.reshape(A)
    tok_flat = jnp.repeat(jnp.arange(T, dtype=jnp.int32), TOP_K)
    g_flat = gates.reshape(A)
    order = jnp.argsort(e_flat)
    e_sorted = e_flat[order]
    counts = jnp.zeros((N_EXPERTS,), jnp.int32).at[e_flat].add(1)
    padded = (counts + MOE_BLOCK - 1) // MOE_BLOCK * MOE_BLOCK
    start = jnp.cumsum(counts) - counts
    ends = jnp.cumsum(padded)
    pstart = ends - padded
    dest = pstart[e_sorted] + jnp.arange(A, dtype=jnp.int32) - start[e_sorted]
    P = (A + MOE_BLOCK - 1) // MOE_BLOCK * MOE_BLOCK + N_EXPERTS * MOE_BLOCK
    nb = P // MOE_BLOCK
    row_tok = jnp.zeros((P,), jnp.int32).at[dest].set(tok_flat[order])
    row_gate = jnp.zeros((P,), jnp.float32).at[dest].set(g_flat[order])
    blk_start = jnp.arange(nb, dtype=jnp.int32) * MOE_BLOCK
    blk_exp = jnp.minimum(jnp.searchsorted(ends, blk_start, side='right'), N_EXPERTS - 1)
    xb = hf[row_tok].reshape(nb, MOE_BLOCK, D)

    def expert_block(inp):
        x_blk, e = inp
        return (jax.nn.silu(x_blk @ w_gate[e]) * (x_blk @ w_up[e])) @ w_down[e]

    yb = lax.map(expert_block, (xb, blk_exp)).reshape(P, D)
    y = jnp.zeros((T, D), h.dtype).at[row_tok].add((yb * row_gate[:, None]).astype(h.dtype))
    return y.reshape(Bn, S, D)

def even_layer(x, norm1, w_in, shift_mu, w0_f, w_up_f, w0_b, w_up_b, a0_f, a_up_f, a0_b, a_up_b, g_up,
               k_k, k_a, r_k, gn_w, gn_b, q_norm, k_norm, w_out, norm2, ffn_gate, ffn_up, ffn_down):
    p = rms_norm(x, norm1) @ w_in
    y_a = rwkv7_mixer(p[..., :RW_IN], shift_mu, w0_f, w_up_f, w0_b, w_up_b, a0_f, a_up_f, a0_b, a_up_b,
                      g_up, k_k, k_a, r_k, gn_w, gn_b)
    y_b = gqa_axial_attention(p[..., RW_IN:], q_norm, k_norm)
    x = x + jnp.concatenate([y_a, y_b], axis=-1) @ w_out
    return x + swiglu(rms_norm(x, norm2), ffn_gate, ffn_up, ffn_down)

def odd_layer(x, norm1, w_in, gate_up_f, gate_bias_f, gate_up_b, gate_bias_b, out_norm, w_out,
              norm2, router, exp_gate, exp_up, exp_down):
    p = rms_norm(x, norm1) @ w_in
    x = x + gla_mixer(p, gate_up_f, gate_bias_f, gate_up_b, gate_bias_b, out_norm) @ w_out
    return x + moe_swiglu(rms_norm(x, norm2), router, exp_gate, exp_up, exp_down)

def setup_inputs(seed: int = 0) -> dict:
    key = jax.random.key(seed)
    ks = iter(jax.random.split(key, 48))
    D = D_MODEL
    NE, NO = N_EVEN, N_ODD

    def nrm(shape, scale):
        return scale * jax.random.normal(next(ks), shape, jnp.float32)

    def gain(shape):
        return 1.0 + nrm(shape, 0.02)

    def unif(shape, lo, hi):
        return jax.random.uniform(next(ks), shape, jnp.float32, lo, hi)

    return {
        'x': nrm((BATCH, SEQ, D), 1.0),
        'e_norm1': gain((NE, D)),
        'e_w_in': nrm((NE, D, E_IN), D ** -0.5),
        'e_shift_mu': unif((NE, RW_IN), 0.0, 1.0),
        'e_w0_f': unif((NE, RW_DIM), -6.0, -1.0),
        'e_w_up_f': nrm((NE, DECAY_RANK, RW_DIM), 0.1),
        'e_w0_b': unif((NE, RW_DIM), -6.0, -1.0),
        'e_w_up_b': nrm((NE, DECAY_RANK, RW_DIM), 0.1),
        'e_a0_f': nrm((NE, RW_DIM), 0.1),
        'e_a_up_f': nrm((NE, ICLR_RANK, RW_DIM), 0.1),
        'e_a0_b': nrm((NE, RW_DIM), 0.1),
        'e_a_up_b': nrm((NE, ICLR_RANK, RW_DIM), 0.1),
        'e_g_up': nrm((NE, GATE_RANK, RW_DIM), GATE_RANK ** -0.5),
        'e_k_k': 0.85 + nrm((NE, RW_DIM), 0.02),
        'e_k_a': gain((NE, RW_DIM)),
        'e_r_k': nrm((NE, RW_DIM), 0.1),
        'e_gn_w': gain((NE, RW_DIM)),
        'e_gn_b': nrm((NE, RW_DIM), 0.02),
        'e_q_norm': gain((NE, HEAD_DIM)),
        'e_k_norm': gain((NE, HEAD_DIM)),
        'e_w_out': nrm((NE, RW_DIM + ATT_DIM, D), (RW_DIM + ATT_DIM) ** -0.5),
        'e_norm2': gain((NE, D)),
        'e_ffn_gate': nrm((NE, D, D_FF), D ** -0.5),
        'e_ffn_up': nrm((NE, D, D_FF), D ** -0.5),
        'e_ffn_down': nrm((NE, D_FF, D), D_FF ** -0.5),
        'o_norm1': gain((NO, D)),
        'o_w_in': nrm((NO, D, O_IN), D ** -0.5),
        'o_gate_up_f': nrm((NO, GLA_GATE_RANK, GLA_DK), GLA_GATE_RANK ** -0.5),
        'o_gate_bias_f': nrm((NO, GLA_DK), 0.1),
        'o_gate_up_b': nrm((NO, GLA_GATE_RANK, GLA_DK), GLA_GATE_RANK ** -0.5),
        'o_gate_bias_b': nrm((NO, GLA_DK), 0.1),
        'o_out_norm': gain((NO, GLA_DVH)),
        'o_w_out': nrm((NO, GLA_DV, D), GLA_DV ** -0.5),
        'o_norm2': gain((NO, D)),
        'o_router': nrm((NO, D, N_EXPERTS), D ** -0.5),
        'o_exp_gate': nrm((NO, N_EXPERTS, D, D_FF_EXPERT), D ** -0.5),
        'o_exp_up': nrm((NO, N_EXPERTS, D, D_FF_EXPERT), D ** -0.5),
        'o_exp_down': nrm((NO, N_EXPERTS, D_FF_EXPERT, D), D_FF_EXPERT ** -0.5),
    }

def reference(x, e_norm1, e_w_in, e_shift_mu, e_w0_f, e_w_up_f, e_w0_b, e_w_up_b, e_a0_f, e_a_up_f,
              e_a0_b, e_a_up_b, e_g_up, e_k_k, e_k_a, e_r_k, e_gn_w, e_gn_b, e_q_norm, e_k_norm, e_w_out,
              e_norm2, e_ffn_gate, e_ffn_up, e_ffn_down, o_norm1, o_w_in, o_gate_up_f, o_gate_bias_f,
              o_gate_up_b, o_gate_bias_b, o_out_norm, o_w_out, o_norm2, o_router, o_exp_gate, o_exp_up,
              o_exp_down):
    for i in range(DEPTH):
        j = i // 2
        if i % 2 == 0:
            x = even_layer(x, e_norm1[j], e_w_in[j], e_shift_mu[j], e_w0_f[j], e_w_up_f[j], e_w0_b[j],
                           e_w_up_b[j], e_a0_f[j], e_a_up_f[j], e_a0_b[j], e_a_up_b[j], e_g_up[j], e_k_k[j],
                           e_k_a[j], e_r_k[j], e_gn_w[j], e_gn_b[j], e_q_norm[j], e_k_norm[j], e_w_out[j],
                           e_norm2[j], e_ffn_gate[j], e_ffn_up[j], e_ffn_down[j])
        else:
            x = odd_layer(x, o_norm1[j], o_w_in[j], o_gate_up_f[j], o_gate_bias_f[j], o_gate_up_b[j],
                          o_gate_bias_b[j], o_out_norm[j], o_w_out[j], o_norm2[j], o_router[j],
                          o_exp_gate[j], o_exp_up[j], o_exp_down[j])
    return x


_drawn_inputs = setup_inputs


def setup_inputs(seed=0):
    import zlib

    import numpy as np

    out = dict(_drawn_inputs(seed))
    spreads = {}
    factors = {'e_gn_w': 2.817,
     'e_gn_b': 3.39,
     'e_q_norm': 4.673,
     'e_k_norm': 8.0,
     'e_k_k': 3.034,
     'e_norm2': 2.849,
     'o_gate_bias_f': 2.973,
     'o_gate_bias_b': 2.781,
     'o_out_norm': 3.324,
     'o_norm2': 3.164}
    for name, (base, spread) in spreads.items():
        noise = np.random.default_rng([zlib.crc32(name.encode()), seed]).standard_normal(out[name].shape)
        drawn = base * np.exp(spread * noise) if base else spread * noise
        out[name] = jnp.asarray(drawn.astype(out[name].dtype))
    for name, factor in factors.items():
        out[name] = (out[name] * factor).astype(out[name].dtype)
    return out
```

```python
import concourse.bass as bass
from concourse import mybir
from contextlib import ExitStack
import numpy as np

D, S = 1024, 256
P = 128
KT = D // P
TT = S // P
HD = 64
RW = 512
RT = RW // P
C = 64
NCH = S // C
RW_IN = 3 * RW + 64 + 64 + 128
ATT = 512
FF = 2816
FT = FF // P
E = 8
FE = 3584
FET = FE // P
CAP = 96
PASSES = -(-S // CAP)
GH = 4
GRANK = 16
RING = 7
GROUP = 3
EPS = 1e-6
GN_EPS = 64e-5
DECAY_C = float(np.exp(-0.5))
KK_SCALE = float(2.0 ** 20)

G_IN0 = 0
N_IN0 = 7
G_OUT0 = G_IN0 + N_IN0
N_OUT0 = 3
G_FFN = G_OUT0 + N_OUT0
G_IN1 = G_FFN + FT
N_IN1 = 8
G_OUT1 = G_IN1 + N_IN1
N_OUT1 = 3
G_MOE = G_OUT1 + N_OUT1

LEVELS = [1, 2, 4, 8, 16, 32]


def layout(parts):
    at, out = 0, {}
    for name, n in parts:
        out[name] = (at, at + n)
        at += n
    return out, at


CONST, N_CONST = layout(
    [("ident", P), ("headsum", P), ("ones", P), ("rot", P), ("before", P), ("cos", S), ("sin", S)]
    + [(f"level{b}", 2 * C) for b in LEVELS]
    + [("level1_t", 2 * C), ("strict", 2 * C), ("read", 2 * C), ("ident64", C), ("slots", CAP), ("experts", E), ("reset", C)]
)
PARAM, N_PARAM = layout(
    [("e_norm1", KT), ("mu", 14), ("w0_f", RT), ("w0_b", RT), ("a0_f", RT), ("a0_b", RT), ("k_k", RT), ("k_a", RT),
     ("r_k", RT), ("gn_w", RT), ("gn_b", RT), ("q_norm", 1), ("k_norm", 1), ("e_norm2", KT), ("o_norm1", KT),
     ("bias_f", GH), ("bias_b", GH), ("out_norm", 2), ("o_norm2", KT), ("eps", 1), ("gn_eps", 1), ("kk_bias", 1), ("one", 1)]
)
SMALL, N_SMALL = layout(
    [("up_f", RW), ("up_b", RW), ("g_up", RW), ("router", KT * E), ("w_gd", KT * GRANK)]
)
A_, R_, B_, K_ = 0, 2048, 4096, 6144
V_, GATE_, BONUS_, TEMP_ = 8192, 9216, 10240, 11264
N_SCRATCH = TEMP_ + 11264


def program(nc, io, stop=99):
    f32, i32, u32 = mybir.dt.float32, mybir.dt.int32, mybir.dt.uint32
    ACT = mybir.ActivationFunctionType
    ALU = mybir.AluOpType
    AX = mybir.AxisListType.X
    mul, add, sub = ALU.mult, ALU.add, ALU.subtract
    ctx = ExitStack()

    def sb(name, shape, dt=f32):
        return ctx.enter_context(nc.sbuf_tensor(name, shape, dt))

    def sem(name):
        return ctx.enter_context(nc.semaphore(name))

    with ctx:
        ring = sb("ring", [P, RING, GROUP, KT, P])
        xT = sb("xT", [P, KT, S])
        xn = sb("xn", [P, KT, S])
        const = sb("const", [P, N_CONST])
        param = sb("param", [P, N_PARAM])
        small = sb("small", [P, N_SMALL])
        rstd = sb("rstd", [P, S])
        scratch = sb("scratch", [P, N_SCRATCH])
        ps = [ctx.enter_context(nc.psum_tensor(f"bank{i}", [P, 512], f32)) for i in range(8)]

        def cst(name):
            a, b = CONST[name]
            return const[:, a:b]

        def par(name, i=0):
            a = PARAM[name][0] + i
            return param[:, a:a + 1]

        def sml(name):
            a, b = SMALL[name]
            return small[:, a:b]

        def area(at, *shape):
            n = int(np.prod(shape))
            v = scratch[:, at:at + n]
            if len(shape) == 1:
                return v
            names = "abcde"[:len(shape)]
            return v.rearrange(f"p ({' '.join(names)}) -> p {' '.join(names)}", **dict(zip(names, shape)))

        def two(b, n=2):
            return ps[b][:, :].rearrange("p (a b) -> p a b", a=n)

        ident = cst("ident")

        consts_loaded, x_loaded = sem("consts_loaded"), sem("x_loaded")
        slot_loaded = [sem(f"slot_loaded{i}") for i in range(RING)]
        group_started = sem("group_started")
        dve_order, act_order = sem("dve_order"), sem("act_order")
        squares_ready, sum_ready, rstd_ready, xn_ready = (sem(n) for n in ("squares_ready", "sum_ready", "rstd_ready", "xn_ready"))

        dve_steps, act_steps = [0], [0]

        def dve_then(dve, instruction):
            instruction.then_inc(dve_order, 1)
            dve_steps[0] += 1
            dve.wait_ge(dve_order, dve_steps[0])

        def act_then(act, instruction):
            instruction.then_inc(act_order, 1)
            act_steps[0] += 1
            act.wait_ge(act_order, act_steps[0])

        def load_group(sp, g, src, tiles=GROUP):
            if g >= RING:
                sp.wait_ge(group_started, g - RING + 2)
            sp.dma_start(ring[:, g % RING, 0:tiles].rearrange("p a k n -> p (a k n)"), src).then_inc(slot_loaded[g % RING], 16)

        stream = ([(io["w_in0"][i], min(3, 20 - 3 * i)) for i in range(N_IN0)]
                  + [(io["w_out0"][i], min(3, 8 - 3 * i)) for i in range(N_OUT0)]
                  + [(io["w_ffn"][i], 3) for i in range(FT)]
                  + [(io["w_in1"][i], 3) for i in range(N_IN1)]
                  + [(io["w_out1"][i], min(3, 8 - 3 * i)) for i in range(N_OUT1)])
        stream += [(io["w_moe"][0, i], 3) for i in range(RING)]

        def load_ahead(sp, first, last):
            for g in range(first + RING, last + RING):
                load_group(sp, g, stream[g][0][:, 0:stream[g][1] * D], stream[g][1])

        def group_ready(pe, g):
            pe.wait_ge(slot_loaded[g % RING], 16 * (g // RING + 1))

        def weights(g, t):
            return ring[:, g % RING, t]

        def norm_squares(dve, n, squares):
            for j in range(4):
                nc.vector.tensor_tensor(squares[:, 2 * j:2 * j + 2], xT[:, 2 * j:2 * j + 2], xT[:, 2 * j:2 * j + 2], mul)\
                    .then_inc(squares_ready, 1)

        def norm_sum(pe, n, squares):
            for k in range(KT):
                if k % 2 == 0:
                    pe.wait_ge(squares_ready, 4 * n + k // 2 + 1)
                last = nc.tensor.matmul(ps[7][:, 0:S], cst("ones"), squares[:, k], start=(k == 0), stop=(k == KT - 1))
            last.then_inc(sum_ready, 1)

        def norm_rstd(act, n):
            act.wait_ge(sum_ready, n + 1)
            act_then(act, nc.scalar.activation(rstd[:, :], ps[7][:, 0:S], ACT.Ln, scale=1.0 / D, bias=par("eps")))
            nc.scalar.activation(rstd[:, :], rstd[:, :], ACT.Exp, scale=-0.5).then_inc(rstd_ready, 1)

        def norm_scale(dve, n, gain):
            dve.wait_ge(rstd_ready, n + 1)
            for k in range(KT):
                nc.vector.scalar_tensor_tensor(xn[:, k], xT[:, k], par(gain, k), rstd[:, :], mul, mul).then_inc(xn_ready, 1)

        x_tok = area(0, TT, D)
        squares0 = area(2048, KT, S)
        proj = area(0, 14, S + 2)
        qk = area(3616, 5, S)
        v_tok = area(4896, TT, P)
        shift_sum = area(5152, 2, S)
        r_in, k_in, v_in = area(TEMP_, RT, S), area(TEMP_ + 1024, RT, S), area(V_, RT, S)
        low = area(TEMP_ + 2048, S)
        gate_low = area(TEMP_ + 2304, S)
        shifted = [r_in[:, i] for i in range(4)] + [k_in[:, i] for i in range(4)] + [v_in[:, i] for i in range(4)] + [low, gate_low]
        x_transposed, xT_ready, proj_ready, proj_copied = (sem(n) for n in ("x_transposed", "xT_ready", "proj_ready", "proj_copied"))

        with nc.Block(no_gpsimd_drain=True) as block:
            @block.sync
            def _(sp):
                for t in range(TT):
                    sp.dma_start(x_tok[:, t], io["x"][t * P:(t + 1) * P, :]).then_inc(x_loaded, 16)
                sp.dma_start(const[:, :], io["const"]).then_inc(consts_loaded, 16)
                sp.dma_start(param[:, :], io["param"]).then_inc(consts_loaded, 16)
                sp.dma_start(small[:, :], io["small"]).then_inc(consts_loaded, 16)
                for g in range(RING):
                    load_group(sp, g, stream[g][0][:, 0:stream[g][1] * D], stream[g][1])
                load_ahead(sp, G_IN0, G_IN0 + N_IN0 - 1)

            @block.tensor
            def _(pe):
                pe.wait_ge(consts_loaded, 48)
                pe.wait_ge(x_loaded, 32)
                for k in range(KT):
                    for t in range(TT):
                        last = nc.tensor.transpose(ps[k // 2][:, (k % 2) * S + t * P:(k % 2) * S + (t + 1) * P],
                                                   x_tok[:, t, k * P:(k + 1) * P], ident)
                    if k % 2:
                        last.then_inc(x_transposed, 1)
                norm_sum(pe, 0, squares0)
                for j in range(10):
                    if j >= 4:
                        pe.wait_ge(proj_copied, j - 3)
                    for i in (2 * j, 2 * j + 1):
                        g = i // GROUP
                        if i % GROUP == 0:
                            group_ready(pe, g)
                        w = weights(g, i % GROUP)
                        if i < 19:
                            for k in range(KT):
                                if i == 0:
                                    pe.wait_ge(xn_ready, k + 1)
                                last = nc.tensor.matmul(ps[j % 4][:, (i % 2) * S:(i % 2 + 1) * S], w[:, k], xn[:, k],
                                                        start=(k == 0), stop=(k == KT - 1))
                                if i % GROUP == 0 and k == 0:
                                    last.then_inc(group_started, 1)
                        else:
                            for t in range(TT):
                                for k in range(KT):
                                    last = nc.tensor.matmul(ps[j % 4][:, S + t * P:S + (t + 1) * P], xn[:, k, t * P:(t + 1) * P],
                                                            w[:, k], start=(k == 0), stop=(k == KT - 1))
                    last.then_inc(proj_ready, 1)

            @block.scalar
            def _(act):
                act.wait_ge(consts_loaded, 48)
                norm_rstd(act, 0)
                for j in range(10):
                    act.wait_ge(proj_ready, j + 1)
                    if j < 7:
                        dst = proj[:, 2 * j:2 * j + 2, 1:S + 1]
                    elif j < 9:
                        dst = qk[:, 2 * (j - 7):2 * (j - 7) + 2]
                    else:
                        dst = area(3616 + 4 * S, 2, S)
                    nc.scalar.activation(dst, two(j % 4), ACT.Copy).then_inc(proj_copied, 1)

            @block.vector
            def _(dve):
                dve.wait_ge(consts_loaded, 48)
                for j in range(4):
                    dve.wait_ge(x_transposed, j + 1)
                    nc.vector.tensor_copy(xT[:, 2 * j:2 * j + 2], two(j)).then_inc(xT_ready, 1)
                dve.wait_ge(xT_ready, 4)
                norm_squares(dve, 0, squares0)
                norm_scale(dve, 0, "e_norm1")
                dve_then(dve, nc.vector.memset(proj[:, :, 0:1], 0.0))
                dve_then(dve, nc.vector.memset(proj[:, :, S + 1:S + 2], 0.0))
                for j in range(7):
                    dve.wait_ge(proj_copied, j + 1)
                    pair = proj[:, 2 * j:2 * j + 2]
                    dve_then(dve, nc.vector.tensor_tensor(shift_sum, pair[:, :, 0:S], pair[:, :, 2:S + 2], add))
                    dve_then(dve, nc.vector.scalar_tensor_tensor(shift_sum, shift_sum, 0.5, pair[:, :, 1:S + 1], mul, sub))
                    for i in range(2):
                        dve_then(dve, nc.vector.scalar_tensor_tensor(shifted[2 * j + i], shift_sum[:, i], par("mu", 2 * j + i),
                                                                     pair[:, i, 1:S + 1], mul, add))
        if stop <= 1:
            return

        sq_qk, rstd_qk = area(0, 5 * S), area(5 * S, 5 * S)
        rope = area(5664, 5, S)
        probs, probs_t = area(2560, 2, 2, S), area(6944, 2, 2, S)
        stats = area(7968, 3, 16)
        yT = xn
        (qk_sq_ready, qk_sum_ready, qk_rstd_ready, qk_normed, rotated, rope_ready, scores_ready, max_ready, exp_ready,
         probs_ready, probs_turned, turned_copied, heads_ready, heads_copied) = (
            sem(n) for n in ("qk_sq_ready", "qk_sum_ready", "qk_rstd_ready", "qk_normed", "rotated", "rope_ready", "scores_ready",
                             "max_ready", "exp_ready", "probs_ready", "probs_turned", "turned_copied", "heads_ready", "heads_copied"))
        UNITS = 8
        QK_SPANS = [(0, 512), (512, 1024), (1024, 1280)]
        qk_flat, rope_flat = area(3616, 5 * S), area(5664, 5 * S)

        with nc.Block(no_gpsimd_drain=True) as block:
            @block.vector
            def _(dve):
                nc.vector.tensor_tensor(sq_qk, qk_flat, qk_flat, mul).then_inc(qk_sq_ready, 1)
                dve.wait_ge(qk_rstd_ready, 3)
                for i in range(5):
                    nc.vector.scalar_tensor_tensor(qk[:, i], qk[:, i], par("q_norm" if i < 4 else "k_norm"),
                                                   rstd_qk[:, i * S:(i + 1) * S], mul, mul).then_inc(qk_normed, 1)
                dve.wait_ge(qk_normed, 5)
                dve_then(dve, nc.vector.tensor_tensor(rope, qk, cst("cos").unsqueeze(1).to_broadcast([P, 5, S]), mul))
                for n, (a, b) in enumerate(QK_SPANS):
                    dve.wait_ge(rotated, n + 1)
                    w = (b - a) // S
                    dve_then(dve, nc.vector.tensor_tensor(sq_qk[:, a:b].rearrange("p (a b) -> p a b", b=S),
                                                          ps[3 + n][:, 0:b - a].rearrange("p (a b) -> p a b", b=S),
                                                          cst("sin").unsqueeze(1).to_broadcast([P, w, S]), mul))
                nc.vector.tensor_tensor(rope_flat, rope_flat, sq_qk, add).then_inc(rope_ready, 1)

                def maximum(u):
                    dve.wait_ge(scores_ready, u + 1)
                    dve_then(dve, nc.vector.tensor_reduce(stats[:, 0, 2 * u:2 * u + 2], two(u % 4), AX, ALU.max))
                    nc.vector.tensor_scalar(stats[:, 0, 2 * u:2 * u + 2], stats[:, 0, 2 * u:2 * u + 2], -HD ** -0.5, None, mul)\
                        .then_inc(max_ready, 1)

                def normalise(u):
                    dve.wait_ge(exp_ready, 2 * u + 2)
                    dve_then(dve, nc.vector.reciprocal(stats[:, 2, 2 * u:2 * u + 2], stats[:, 1, 2 * u:2 * u + 2]))
                    for q in range(2):
                        nc.vector.tensor_scalar(probs[:, u % 2, q], probs[:, u % 2, q], stats[:, 2, 2 * u + q:2 * u + q + 1], None, mul)\
                            .then_inc(probs_ready, 1)

                for u in range(UNITS + 1):
                    if u < UNITS:
                        maximum(u)
                    if u >= 1:
                        normalise(u - 1)

            @block.scalar
            def _(act):
                for n, (a, b) in enumerate(QK_SPANS):
                    act.wait_ge(qk_sum_ready, n + 1)
                    act_then(act, nc.scalar.activation(rstd_qk[:, a:b], ps[n][:, 0:b - a], ACT.Ln, scale=1.0 / HD, bias=par("eps")))
                for n, (a, b) in enumerate(QK_SPANS):
                    nc.scalar.activation(rstd_qk[:, a:b], rstd_qk[:, a:b], ACT.Exp, scale=-0.5).then_inc(qk_rstd_ready, 1)

                def exponentials(u):
                    act.wait_ge(max_ready, u + 1)
                    if u >= 2:
                        act.wait_ge(probs_turned, u - 1)
                    for q in range(2):
                        nc.scalar.activation(probs[:, u % 2, q], ps[u % 4][:, q * S:(q + 1) * S], ACT.Exp, scale=HD ** -0.5,
                                             bias=stats[:, 0, 2 * u + q:2 * u + q + 1],
                                             accum_out=stats[:, 1, 2 * u + q:2 * u + q + 1]).then_inc(exp_ready, 1)

                def copy_turned(u):
                    act.wait_ge(probs_turned, u + 1)
                    if u >= 2:
                        act.wait_ge(heads_ready, u - 1)
                    nc.scalar.activation(probs_t[:, u % 2], two(4 + u % 2), ACT.Copy).then_inc(turned_copied, 1)

                def copy_heads(i):
                    act.wait_ge(heads_ready, 2 * i + 2)
                    nc.scalar.activation(yT[:, 4 + i], ps[6 + i % 2][:, 0:S], ACT.Copy).then_inc(heads_copied, 1)

                for u in range(UNITS + 2):
                    if u < UNITS:
                        exponentials(u)
                    if 1 <= u <= UNITS:
                        copy_turned(u - 1)
                    if u >= 3 and u % 2:
                        copy_heads((u - 3) // 2)

            @block.tensor
            def _(pe):
                pe.wait_ge(qk_sq_ready, 1)
                for n, (a, b) in enumerate(QK_SPANS):
                    nc.tensor.matmul(ps[n][:, 0:b - a], cst("headsum"), sq_qk[:, a:b], start=True, stop=True).then_inc(qk_sum_ready, 1)
                pe.wait_ge(qk_normed, 5)
                for n, (a, b) in enumerate(QK_SPANS):
                    nc.tensor.matmul(ps[3 + n][:, 0:b - a], cst("rot"), qk_flat[:, a:b], start=True, stop=True).then_inc(rotated, 1)
                pe.wait_ge(rope_ready, 1)

                def scores(u):
                    i, h = u // 2, u % 2
                    if u >= 4:
                        pe.wait_ge(exp_ready, 2 * (u - 3))
                    for q in range(2):
                        last = nc.tensor.matmul(ps[u % 4][:, q * S:(q + 1) * S], rope[HD * h:HD * (h + 1), i, q * P:(q + 1) * P],
                                                rope[HD * h:HD * (h + 1), 4], start=True, stop=True)
                    last.then_inc(scores_ready, 1)

                def turn(u):
                    pe.wait_ge(probs_ready, 2 * u + 2)
                    if u >= 2:
                        pe.wait_ge(turned_copied, u - 1)
                    for q in range(2):
                        for t in range(TT):
                            last = nc.tensor.transpose(ps[4 + u % 2][:, t * S + q * P:t * S + (q + 1) * P],
                                                       probs[:, u % 2, q, t * P:(t + 1) * P], ident)
                    last.then_inc(probs_turned, 1)

                def weigh(u):
                    i, h = u // 2, u % 2
                    pe.wait_ge(turned_copied, u + 1)
                    if i >= 2 and h == 0:
                        pe.wait_ge(heads_copied, i - 1)
                    for t in range(TT):
                        last = nc.tensor.matmul(ps[6 + i % 2][HD * h:HD * (h + 1), 0:S], v_tok[:, t, HD * h:HD * (h + 1)],
                                                probs_t[:, u % 2, t], start=(t == 0), stop=(t == TT - 1))
                    last.then_inc(heads_ready, 1)

                for u in range(UNITS + 2):
                    if u < UNITS:
                        scores(u)
                    if 1 <= u <= UNITS:
                        turn(u - 1)
                    if u >= 2:
                        weigh(u - 2)
        if stop <= 2:
            return

        A, R, B, K = (area(at, 2, RT, S) for at in (A_, R_, B_, K_))
        gate, bonus = area(GATE_, RT, S), area(BONUS_, RT, S)
        rate = area(TEMP_ + 3072, 2, RT, S)
        sig = area(TEMP_ + 5120, 2, RT, S)
        run = area(TEMP_ + 7168, 2, RT, S)
        kk = area(TEMP_ + 9216, RT, S)
        reset = area(TEMP_ + 10240, RT * S)
        cols = sb("cols", [P, 4, 2, RT, NCH])
        mid, tail = cols[:, 0], cols[:, 1]
        factor = cols[:, 2].rearrange("p d t c -> p (d t c)")[:, 0:24].rearrange("p (s d t) -> p s d t", s=3, d=2)
        one_less_ka = cols[:, 3, 0, 0]

        def flat(v):
            return v.rearrange("p a b -> p (a b)")

        def halves(v, n):
            return v[:, 2 * n:2 * n + 2]

        def chunks(v):
            return v.rearrange("p d t (c n) -> p (d t c) n", n=C)

        (low_ready, ranks_ready, sig_ready, kk_sq_ready, kk_sum_ready, kk_floor_ready, kk_scale_ready, gate_done, gate_copied,
         run_ready, scales_ready, bonus_in, bonus_sum) = (
            sem(n) for n in ("low_ready", "ranks_ready", "sig_ready", "kk_sq_ready", "kk_sum_ready", "kk_floor_ready",
                             "kk_scale_ready", "gate_done", "gate_copied", "run_ready", "scales_ready", "bonus_in", "bonus_sum"))
        kk_sq, kk_scale = run[:, 0], run[:, 1]

        with nc.Block(no_gpsimd_drain=True) as block:
            @block.scalar
            def _(act):
                nc.scalar.activation(low[0:64, :], low[0:64, :], ACT.Tanh).then_inc(low_ready, 1)
                nc.scalar.activation(gate_low, gate_low, ACT.Sigmoid).then_inc(low_ready, 1)
                act.wait_ge(ranks_ready, 1)
                for d in range(2):
                    for i in range(RT):
                        nc.scalar.activation(sig[:, d, i], ps[2 * d + i // 2][:, (i % 2) * S:(i % 2 + 1) * S], ACT.Sigmoid,
                                             bias=par("w0_b" if d else "w0_f", i)).then_inc(sig_ready, 1)
                act.wait_ge(ranks_ready, 2)
                for d in range(2):
                    for i in range(RT):
                        nc.scalar.activation(rate[:, d, i], ps[4 + 2 * d + i // 2][:, (i % 2) * S:(i % 2 + 1) * S], ACT.Sigmoid,
                                             bias=par("a0_b" if d else "a0_f", i)).then_inc(sig_ready, 1)
                act.wait_ge(gate_done, 1)
                for n in range(2):
                    nc.scalar.activation(halves(gate, n), two(n), ACT.Copy).then_inc(gate_copied, 1)
                act.wait_ge(kk_floor_ready, 1)
                act_then(act, nc.scalar.activation(flat(kk_scale), flat(kk_scale), ACT.Ln, scale=KK_SCALE))
                nc.scalar.activation(flat(kk_scale), flat(kk_scale), ACT.Exp, scale=-0.5, bias=par("kk_bias")).then_inc(kk_scale_ready, 1)
                act.wait_ge(run_ready, 1)
                for out, src, s in ((R[:, 0], run[:, 0], -DECAY_C), (A[:, 1], run[:, 1], DECAY_C), (A[:, 0], sig[:, 0], -DECAY_C)):
                    nc.scalar.activation(flat(out), flat(src), ACT.Exp, scale=s).then_inc(scales_ready, 1)
                act.wait_ge(scales_ready, 3)
                nc.scalar.activation(flat(run[:, 0]), flat(run[:, 0]), ACT.Exp, scale=DECAY_C).then_inc(scales_ready, 1)
                nc.scalar.activation(flat(sig[:, 1]), flat(sig[:, 1]), ACT.Exp, scale=-DECAY_C).then_inc(scales_ready, 1)
                nc.scalar.activation(factor, factor, ACT.Exp, scale=-DECAY_C).then_inc(scales_ready, 1)

            @block.tensor
            def _(pe):
                pe.wait_ge(low_ready, 2)
                for d in range(2):
                    up = sml("up_b" if d else "up_f")
                    for i in range(RT):
                        last = nc.tensor.matmul(ps[2 * d + i // 2][:, (i % 2) * S:(i % 2 + 1) * S], up[0:64, i * P:(i + 1) * P],
                                                low[0:64, :], start=True, stop=True)
                last.then_inc(ranks_ready, 1)
                for d in range(2):
                    up = sml("up_b" if d else "up_f")
                    for i in range(RT):
                        last = nc.tensor.matmul(ps[4 + 2 * d + i // 2][:, (i % 2) * S:(i % 2 + 1) * S], up[64:128, i * P:(i + 1) * P],
                                                low[64:128, :], start=True, stop=True)
                last.then_inc(ranks_ready, 1)
                pe.wait_ge(sig_ready, 8)
                pe.wait_ge(kk_sq_ready, 1)
                for n in range(2):
                    last = nc.tensor.matmul(ps[2 + n][:, :], cst("headsum"), halves(kk_sq, n), start=True, stop=True)
                last.then_inc(kk_sum_ready, 1)
                for i in range(RT):
                    last = nc.tensor.matmul(ps[i // 2][:, (i % 2) * S:(i % 2 + 1) * S], sml("g_up")[:, i * P:(i + 1) * P], gate_low,
                                            start=True, stop=True)
                last.then_inc(gate_done, 1)
                pe.wait_ge(sig_ready, 16)
                pe.wait_ge(bonus_in, 4)
                for n in range(2):
                    nc.tensor.matmul(ps[4 + n][:, :], cst("headsum"), halves(kk_sq, n), start=True, stop=True).then_inc(bonus_sum, 1)

            @block.vector
            def _(dve):
                for i in range(RT):
                    dve_then(dve, nc.vector.tensor_scalar(kk[:, i], k_in[:, i], par("k_k", i), None, mul))
                nc.vector.tensor_tensor(flat(kk_sq), flat(kk), flat(kk), mul).then_inc(kk_sq_ready, 1)
                dve_then(dve, nc.vector.tensor_copy(reset.rearrange("p (a b) -> p a b", b=C),
                                                    cst("reset").unsqueeze(1).to_broadcast([P, RT * NCH, C])))
                a = PARAM["k_a"][0]
                dve_then(dve, nc.vector.tensor_scalar(one_less_ka, param[:, a:a + RT], -1.0, 1.0, mul, add))
                dve.wait_ge(kk_sum_ready, 1)
                for n in range(2):
                    last = nc.vector.tensor_scalar(halves(kk_scale, n), two(2 + n), 1e-24, None, ALU.max)
                last.then_inc(kk_floor_ready, 1)
                dve.wait_ge(sig_ready, 16)
                for d in range(2):
                    for i in range(RT):
                        dve_then(dve, nc.vector.tensor_scalar(K[:, d, i], rate[:, d, i], par("k_a", i), one_less_ka[:, i:i + 1], mul, add))
                    dve_then(dve, nc.vector.tensor_tensor(flat(K[:, d]), flat(K[:, d]), flat(k_in), mul))
                for i in range(RT):
                    nc.vector.scalar_tensor_tensor(kk_sq[:, i], r_in[:, i], par("r_k", i), K[:, 0, i], mul, mul).then_inc(bonus_in, 1)
                dve.wait_ge(kk_scale_ready, 1)
                dve_then(dve, nc.vector.tensor_tensor(flat(kk), flat(kk), flat(kk_scale), mul))
                for n in range(2):
                    dve.wait_ge(bonus_sum, n + 1)
                    dve_then(dve, nc.vector.tensor_tensor(halves(bonus, n), two(4 + n), halves(v_in, n), mul))
                for d in range(2):
                    dve_then(dve, nc.vector.tensor_tensor_scan(flat(run[:, d]), reset, flat(sig[:, d]), 0.0, mul, add))
                ends = run.rearrange("p d t (c n) -> p d t c n", n=C)
                dve_then(dve, nc.vector.tensor_copy(mid, ends[:, :, :, :, C // 2 - 1]))
                dve_then(dve, nc.vector.tensor_tensor(tail, ends[:, :, :, :, C - 1], mid, sub))
                for s in range(3):
                    dve_then(dve, nc.vector.tensor_tensor(factor[:, s, 0], tail[:, 0, :, s], mid[:, 0, :, s + 1], add))
                    dve_then(dve, nc.vector.tensor_tensor(factor[:, s, 1], mid[:, 1, :, 3 - s], tail[:, 1, :, 2 - s], add))
                dve_then(dve, nc.vector.tensor_tensor(chunks(run), chunks(run),
                                                      mid.rearrange("p d t c -> p (d t c)").unsqueeze(2).to_broadcast([P, 32, C]), sub))
                nc.vector.tensor_tensor(chunks(sig), chunks(run), chunks(sig), sub).then_inc(run_ready, 1)
                for d in range(2):
                    dve_then(dve, nc.vector.tensor_tensor(flat(B[:, d]), flat(kk), flat(rate[:, d]), mul))
                dve.wait_ge(scales_ready, 3)
                dve_then(dve, nc.vector.tensor_tensor(flat(R[:, 0]), flat(R[:, 0]), flat(r_in), mul))
                dve_then(dve, nc.vector.tensor_tensor(flat(R[:, 1]), flat(A[:, 1]), flat(r_in), mul))
                for d in range(2):
                    dve_then(dve, nc.vector.scalar_tensor_tensor(flat(A[:, d]), flat(A[:, d]), -1.0, flat(kk), mul, mul))
                dve.wait_ge(scales_ready, 5)
                for d, scale in ((0, run[:, 0]), (1, sig[:, 1])):
                    dve_then(dve, nc.vector.tensor_tensor(flat(B[:, d]), flat(B[:, d]), flat(scale), mul))
                    dve_then(dve, nc.vector.tensor_tensor(flat(K[:, d]), flat(K[:, d]), flat(scale), mul))
        if stop <= 3:
            return

        def tile8(at):
            return area(at, 8, C)

        slots = []
        for q in range(2):
            at = TEMP_ + q * 9 * 512
            slots.append({n: tile8(at + 512 * j) for j, n in enumerate(("X", "XT", "MT", "AK", "RB", "RK", "Bt", "Kt", "Vt"))})
        state = [tile8(TEMP_ + 9216), tile8(TEMP_ + 9728)]
        W, U = tile8(TEMP_ + 10240), tile8(TEMP_ + 10752)
        product = [W, U]
        yA = yT[:, 0:RT]
        SYSTEMS = [(d, t, h) for d in range(2) for t in range(RT) for h in range(2)]
        names = ("grams_ready", "grams_taken_dve", "grams_taken_act", "w_ready", "w_copied", "u_ready", "u_copied", "y_ready",
                 "y_taken", "s_ready", "state_ready")
        (grams_ready, grams_taken_dve, grams_taken_act, w_ready, w_copied, u_ready, u_copied, y_ready, y_taken, s_ready,
         state_ready) = (sem(n) for n in names)
        inverse_ready = [sem(f"inverse_ready{q}") for q in range(2)]
        product_ready = [sem(f"product_ready{q}") for q in range(2)]
        product_masked = [sem(f"product_masked{q}") for q in range(2)]
        blocks_ready = [sem(f"blocks_ready{q}") for q in range(2)]

        def both(name):
            return cst(name).rearrange("p (d n) -> p d n", d=2).unsqueeze(2).to_broadcast([P, 2, RT, C])

        def dirs(v):
            return v.rearrange("p (d t) n -> p d t n", d=2)

        def bank8(b):
            return ps[b][:, :].rearrange("p (a n) -> p a n", n=C)

        eye = cst("ident64").unsqueeze(1).to_broadcast([P, 8, C])

        with nc.Block(no_gpsimd_drain=True) as block:
            @block.tensor
            def _(pe):
                def chunk(v, s, d, t, h):
                    c = s if d == 0 else NCH - 1 - s
                    return v[HD * h:HD * (h + 1), d, t, c * C:(c + 1) * C]

                def v_chunk(s, d, t, h):
                    c = s if d == 0 else NCH - 1 - s
                    return v_in[HD * h:HD * (h + 1), t, c * C:(c + 1) * C]

                def grams(s):
                    def product_of(bank, left, right):
                        for d, t, h in SYSTEMS:
                            last = nc.tensor.matmul(bank8(bank)[HD * h:HD * (h + 1), RT * d + t], left(d, t, h), right(d, t, h),
                                                    start=True, stop=True)
                        last.then_inc(grams_ready, 1)

                    a, r, b, k = (lambda d, t, h, v=v: chunk(v, s, d, t, h) for v in (A, R, B, K))
                    turn = lambda d, t, h: ident[HD * h:HD * (h + 1), HD * h:HD * (h + 1)]
                    v = lambda d, t, h: v_chunk(s, d, t, h)
                    steps = [(a, b, "dve", 1), (b, a, "act", 1), (k, a, "dve", 2), (b, r, "dve", 3), (k, r, "dve", 4),
                             (b, turn, "act", 2), (k, turn, "act", 3), (v, turn, "act", 4)]
                    for bank, (left, right, taker, n) in enumerate(steps):
                        if s % 2:
                            pe.wait_ge(grams_taken_dve if taker == "dve" else grams_taken_act, 4 * (s - 1) + n)
                        product_of(bank, left, right)

                def levels(s):
                    pe.wait_ge(grams_taken_dve, 4 * (s + 2))
                    pe.wait_ge(grams_taken_act, 4 * (s + 2))
                    for n in range(1, len(LEVELS)):
                        done = len(LEVELS) * (s // 2)
                        for q in range(2):
                            o = slots[q]
                            pe.wait_ge(inverse_ready[q], done + n)
                            for d, t, h in SYSTEMS:
                                p = slice(HD * h, HD * (h + 1))
                                last = nc.tensor.matmul(bank8(3 * q)[p, RT * d + t], o["MT"][p, RT * d + t], o["X"][p, RT * d + t],
                                                        start=True, stop=True)
                            last.then_inc(product_ready[q], 1)
                        for q in range(2):
                            o = slots[q]
                            pe.wait_ge(product_masked[q], (len(LEVELS) - 1) * (s // 2) + n)
                            for d, t, h in SYSTEMS:
                                p = slice(HD * h, HD * (h + 1))
                                last = nc.tensor.matmul(bank8(3 * q + 2)[p, RT * d + t], product[q][p, RT * d + t],
                                                        o["XT"][p, RT * d + t], start=True, stop=True)
                            if n < len(LEVELS) - 1:
                                for d, t, h in SYSTEMS:
                                    p = slice(HD * h, HD * (h + 1))
                                    last = nc.tensor.matmul(bank8(3 * q + 1)[p, RT * d + t], o["XT"][p, RT * d + t],
                                                            product[q][p, RT * d + t], start=True, stop=True)
                            last.then_inc(blocks_ready[q], 1)

                def recur(s):
                    o, now = slots[s % 2], state[s % 2]
                    pe.wait_ge(inverse_ready[s % 2], len(LEVELS) * (s // 2 + 1))
                    if s:
                        pe.wait_ge(state_ready, s)
                    for d, t, h in SYSTEMS:
                        p, j = slice(HD * h, HD * (h + 1)), RT * d + t
                        if s:
                            nc.tensor.matmul(bank8(6)[p, j], chunk(A, s, d, t, h), now[p, j], start=True, stop=False)
                        last = nc.tensor.matmul(bank8(6)[p, j], o["AK"][p, j], o["Vt"][p, j], start=(s == 0), stop=True)
                    last.then_inc(w_ready, 1)
                    pe.wait_ge(w_copied, s + 1)
                    for d, t, h in SYSTEMS:
                        p, j = slice(HD * h, HD * (h + 1)), RT * d + t
                        last = nc.tensor.matmul(bank8(7)[p, j], o["XT"][p, j], W[p, j], start=True, stop=True)
                    last.then_inc(u_ready, 1)
                    pe.wait_ge(u_copied, s + 1)
                    if s < NCH - 1:
                        for d, t, h in SYSTEMS:
                            p, j = slice(HD * h, HD * (h + 1)), RT * d + t
                            nc.tensor.matmul(bank8(1)[p, j], o["Bt"][p, j], U[p, j], start=True, stop=False)
                            last = nc.tensor.matmul(bank8(1)[p, j], o["Kt"][p, j], o["Vt"][p, j], start=False, stop=True)
                        last.then_inc(s_ready, 1)
                    if s:
                        pe.wait_ge(y_taken, s)
                    for d, t, h in SYSTEMS:
                        p, j = slice(HD * h, HD * (h + 1)), RT * d + t
                        if s:
                            nc.tensor.matmul(bank8(0)[p, j], now[p, j], chunk(R, s, d, t, h), start=True, stop=False)
                        nc.tensor.matmul(bank8(0)[p, j], U[p, j], o["RB"][p, j], start=(s == 0), stop=False)
                        last = nc.tensor.matmul(bank8(0)[p, j], o["Vt"][p, j], o["RK"][p, j], start=False, stop=True)
                    last.then_inc(y_ready, 1)

                for s in range(0, NCH, 2):
                    if s:
                        pe.wait_ge(y_taken, s)
                        pe.wait_ge(state_ready, s)
                    grams(s)
                    grams(s + 1)
                    levels(s)
                    recur(s)
                    recur(s + 1)

            @block.scalar
            def _(act):
                for s in range(0, NCH, 2):
                    for q in range(2):
                        o = slots[q]
                        for n, (name, bank) in enumerate((("MT", 1), ("Bt", 5), ("Kt", 6), ("Vt", 7))):
                            act.wait_ge(grams_ready, 8 * (s + q) + bank + 1)
                            nc.scalar.activation(o[name], bank8(bank), ACT.Copy).then_inc(grams_taken_act, 1)
                    for r in (s, s + 1):
                        act.wait_ge(w_ready, r + 1)
                        nc.scalar.activation(W, bank8(6), ACT.Copy).then_inc(w_copied, 1)
                        act.wait_ge(u_ready, r + 1)
                        nc.scalar.activation(U, bank8(7), ACT.Copy).then_inc(u_copied, 1)

            @block.vector
            def _(dve):
                def y_out(s):
                    dve.wait_ge(y_ready, s + 1)
                    for d, c in ((0, s), (1, NCH - 1 - s)):
                        out, src = yA[:, :, c * C:(c + 1) * C], bank8(0)[:, RT * d:RT * (d + 1)]
                        if s < 2:
                            last = nc.vector.tensor_copy(out, src)
                        else:
                            last = nc.vector.tensor_tensor(out, out, src, add)
                    last.then_inc(y_taken, 1)

                for s in range(0, NCH, 2):
                    for q in range(2):
                        o = slots[q]
                        base = 8 * (s + q)
                        dve.wait_ge(grams_ready, base + 1)
                        nc.vector.tensor_tensor(dirs(o["X"]), dirs(bank8(0)), both("level1"), mul).then_inc(grams_taken_dve, 1)
                        for n, (name, bank, mask) in enumerate((("AK", 2, "strict"), ("RB", 3, "read"), ("RK", 4, "read"))):
                            dve.wait_ge(grams_ready, base + bank + 1)
                            nc.vector.tensor_tensor(dirs(o[name]), dirs(bank8(bank)), both(mask), mul).then_inc(grams_taken_dve, 1)
                        dve.wait_ge(grams_taken_dve, 4 * (s + q + 1))
                        dve_then(dve, nc.vector.tensor_tensor(o["X"], o["X"], eye, add))
                        dve.wait_ge(grams_taken_act, 4 * (s + q) + 1)
                        dve_then(dve, nc.vector.tensor_tensor(dirs(o["XT"]), dirs(o["MT"]), both("level1_t"), mul))
                        nc.vector.tensor_tensor(o["XT"], o["XT"], eye, add).then_inc(inverse_ready[q], 1)
                    for n in range(1, len(LEVELS)):
                        done = (len(LEVELS) - 1) * (s // 2)
                        for q in range(2):
                            dve.wait_ge(product_ready[q], done + n)
                            nc.vector.tensor_tensor(dirs(product[q]), dirs(bank8(3 * q)), both(f"level{LEVELS[n]}"), mul)\
                                .then_inc(product_masked[q], 1)
                        for q in range(2):
                            o = slots[q]
                            dve.wait_ge(blocks_ready[q], done + n)
                            if n < len(LEVELS) - 1:
                                nc.vector.tensor_tensor(o["X"], o["X"], bank8(3 * q + 1), add)
                            nc.vector.tensor_tensor(o["XT"], o["XT"], bank8(3 * q + 2), add).then_inc(inverse_ready[q], 1)
                    for r in (s, s + 1):
                        if r < NCH - 1:
                            dve.wait_ge(s_ready, r + 1)
                            scale = factor[:, r].rearrange("p d t -> p (d t)").unsqueeze(2).to_broadcast([P, 8, C])
                            new = state[(r + 1) % 2]
                            if r == 0:
                                nc.vector.tensor_tensor(new, bank8(1), scale, mul).then_inc(state_ready, 1)
                            else:
                                dve_then(dve, nc.vector.tensor_tensor(new, bank8(1), state[r % 2], add))
                                nc.vector.tensor_tensor(new, new, scale, mul).then_inc(state_ready, 1)
                        y_out(r)
        if stop <= 4:
            return

        y_sq, y_rstd = area(A_, RT, S), area(R_, RT, S)
        (mean_ready, centred, var_ready, y_rstd_ready) = (sem(n) for n in ("mean_ready", "centred", "var_ready", "y_rstd_ready"))
        with nc.Block(no_gpsimd_drain=True) as block:
            @block.tensor
            def _(pe):
                for n in range(2):
                    nc.tensor.matmul(ps[n][:, :], cst("headsum"), halves(yA, n), start=True, stop=True).then_inc(mean_ready, 1)
                for n in range(2):
                    pe.wait_ge(centred, n + 1)
                    nc.tensor.matmul(ps[2 + n][:, :], cst("headsum"), halves(y_sq, n), start=True, stop=True).then_inc(var_ready, 1)

            @block.scalar
            def _(act):
                for n in range(2):
                    act.wait_ge(var_ready, n + 1)
                    act_then(act, nc.scalar.activation(halves(y_rstd, n), two(2 + n), ACT.Ln, scale=1.0 / HD, bias=par("gn_eps")))
                for n in range(2):
                    nc.scalar.activation(halves(y_rstd, n), halves(y_rstd, n), ACT.Exp, scale=-0.5).then_inc(y_rstd_ready, 1)

            @block.vector
            def _(dve):
                for n in range(2):
                    dve.wait_ge(mean_ready, n + 1)
                    dve_then(dve, nc.vector.scalar_tensor_tensor(halves(yA, n), two(n), -1.0 / HD, halves(yA, n), mul, add))
                    nc.vector.tensor_tensor(halves(y_sq, n), halves(yA, n), halves(yA, n), mul).then_inc(centred, 1)
                for n in range(2):
                    dve.wait_ge(y_rstd_ready, n + 1)
                    y = halves(yA, n)
                    dve_then(dve, nc.vector.tensor_tensor(y, y, halves(y_rstd, n), mul))
                    for i in (2 * n, 2 * n + 1):
                        dve_then(dve, nc.vector.tensor_scalar(yA[:, i], yA[:, i], par("gn_w", i), par("gn_b", i), mul, add))
                    dve_then(dve, nc.vector.tensor_tensor(y, y, halves(bonus, n), add))
                    dve_then(dve, nc.vector.tensor_tensor(y, y, halves(gate, n), mul))
        if stop <= 5:
            return

        out_ready, out_added = sem("out_ready"), sem("out_added")

        def project_out(pe, first_group, use):
            for j in range(KT):
                g = first_group + j // GROUP
                if j % GROUP == 0:
                    group_ready(pe, g)
                w = weights(g, j % GROUP)
                for k in range(KT):
                    last = nc.tensor.matmul(ps[j // 2][:, (j % 2) * S:(j % 2 + 1) * S], w[:, k], yT[:, k], start=(k == 0), stop=(k == KT - 1))
                    if j % GROUP == 0 and k == 0:
                        last.then_inc(group_started, 1)
                if j % 2:
                    last.then_inc(out_ready, 1)

        def add_out(dve, use, squares):
            for n in range(4):
                dve.wait_ge(out_ready, 4 * use + n + 1)
                x = xT[:, 2 * n:2 * n + 2]
                nc.vector.tensor_tensor(x, x, two(n), add).then_inc(out_added, 1)
                dve.wait_ge(out_added, 8 * use + n + 1)
                nc.vector.tensor_tensor(squares[:, 2 * n:2 * n + 2], x, x, mul).then_inc(squares_ready, 1)

        PAIR_BANK = [4, 5, 6, 7, 4, 5, 6]
        LEAD = 3
        squares1 = area(0, KT, S)
        silu_f, hidden_f = area(2048, RING, S), area(2048 + RING * S, RING, S)
        (pair_ready, silu_ready, hidden_ready, ffn_done) = (sem(n) for n in ("pair_ready", "silu_ready", "hidden_ready", "ffn_done"))

        def gate_up_tile(pe, slot, j, x, n, ready):
            bank = ps[PAIR_BANK[j]]
            for m in range(2):
                for k in range(KT):
                    last = nc.tensor.matmul(bank[:, m * n:(m + 1) * n], ring[:, slot, m, k], x[:, k], start=(k == 0), stop=(k == KT - 1))
            last.then_inc(ready, 1)

        with nc.Block(no_gpsimd_drain=True) as block:
            @block.sync
            def _(sp):
                load_ahead(sp, G_IN0 + N_IN0 - 1, G_FFN + FT - 1)

            @block.tensor
            def _(pe):
                project_out(pe, G_OUT0, 0)
                norm_sum(pe, 1, squares1)
                pe.wait_ge(xn_ready, 2 * KT)
                pe.wait_ge(hidden_ready, LEAD)
                pe.wait_ge(rstd_ready, 2)

                def pair(i, t, j):
                    g = G_FFN + j
                    pe.wait_ge(slot_loaded[g % RING], (i + (g // RING + 1)) * 16)
                    pe.wait_ge(hidden_ready, t + (LEAD - 2))
                    gate_up_tile(pe, g % RING, j, xn, S, pair_ready)

                def down(t, j):
                    pe.wait_ge(hidden_ready, t + (LEAD + 1))
                    for k in range(KT):
                        last = nc.tensor.matmul(ps[k // 2][:, (k % 2) * S:(k % 2 + 1) * S], ring[:, (G_FFN + j) % RING, 2, k],
                                                hidden_f[:, j], start=False, stop=False, skip_group_check=True)
                        if k == 0:
                            last.then_inc(group_started, 1)
                    return last

                pair(0, 0, 0)
                with pe.Fori(0, FT // RING) as i:
                    for j in range(RING):
                        t = i * RING + j
                        pair(i if j + 1 < RING else i + 1, t + 1, (j + 1) % RING)
                        down(t, j)
                down(FT - 1, 0).then_inc(ffn_done, 1)

            @block.scalar
            def _(act):
                norm_rstd(act, 1)

                def silu(t, j):
                    act.wait_ge(pair_ready, t + 1)
                    nc.scalar.activation(silu_f[:, j], ps[PAIR_BANK[j]][:, 0:S], ACT.Silu).then_inc(silu_ready, 1)

                with act.Fori(0, FT // RING) as i:
                    for j in range(RING):
                        silu(i * RING + j, j)
                silu(FT - 1, 0)

            @block.vector
            def _(dve):
                add_out(dve, 0, squares1)
                for n in range(4):
                    dve.wait_ge(out_added, 4)
                    zero = nc.vector.memset(ps[n][:, :], 0.0)
                    if n:
                        zero.then_inc(hidden_ready, 1)
                norm_scale(dve, 1, "e_norm2")

                def product_tile(t, j):
                    dve.wait_ge(silu_ready, t + 1)
                    nc.vector.tensor_tensor(hidden_f[:, j], silu_f[:, j], ps[PAIR_BANK[j]][:, S:2 * S], mul).then_inc(hidden_ready, 1)

                with dve.Fori(0, FT // RING) as i:
                    for j in range(RING):
                        product_tile(i * RING + j, j)
                product_tile(FT - 1, 0)
                dve.wait_ge(ffn_done, 1)
                for n in range(4):
                    x = xT[:, 2 * n:2 * n + 2]
                    nc.vector.tensor_tensor(x, x, two(n), add).then_inc(out_added, 1)
        if stop <= 6:
            return

        q1, k1 = area(0, GH, S), area(1024, GH, S)
        v1 = area(2048, TT, D)
        swish = area(4096, KT, S)
        G = area(6144, 2, GH, S)
        run1 = area(8192, 2, GH, S)
        squares2 = area(10240, KT, S)
        reset1, low1 = area(20480, GH * S), area(21504, S)
        gate_up = small[0:GRANK, 0:2 * RW]
        (gates_loaded, proj1_ready, proj1_copied, low1_copied, z_ready, z_copied) = (
            sem(n) for n in ("gates_loaded", "proj1_ready", "proj1_copied", "low1_copied", "z_ready", "z_copied"))

        with nc.Block(no_gpsimd_drain=True) as block:
            @block.sync
            def _(sp):
                sp.dma_start(gate_up, io["gate_up"]).then_inc(gates_loaded, 16)
                load_ahead(sp, G_FFN + FT - 1, G_OUT1 - 1)

            @block.tensor
            def _(pe):
                norm_sum(pe, 2, squares2)
                pe.wait_ge(xn_ready, 3 * KT)
                for k in range(KT):
                    last = nc.tensor.matmul(ps[4][0:GRANK, 0:S], sml("w_gd")[:, k * GRANK:(k + 1) * GRANK], xn[:, k],
                                            start=(k == 0), stop=(k == KT - 1))
                last.then_inc(proj1_ready, 1)
                for j in range(12):
                    if j >= 4:
                        pe.wait_ge(proj1_copied, j - 3)
                    for i in (2 * j, 2 * j + 1):
                        g = G_IN1 + i // GROUP
                        if i % GROUP == 0:
                            group_ready(pe, g)
                        w = weights(g, i % GROUP)
                        if 8 <= i < 16:
                            for t in range(TT):
                                for k in range(KT):
                                    last = nc.tensor.matmul(ps[j % 4][:, (i % 2) * S + t * P:(i % 2) * S + (t + 1) * P],
                                                            xn[:, k, t * P:(t + 1) * P], w[:, k], start=(k == 0), stop=(k == KT - 1))
                                    if i % GROUP == 0 and k == 0 and t == 0:
                                        last.then_inc(group_started, 1)
                        else:
                            for k in range(KT):
                                last = nc.tensor.matmul(ps[j % 4][:, (i % 2) * S:(i % 2 + 1) * S], w[:, k], xn[:, k],
                                                        start=(k == 0), stop=(k == KT - 1))
                                if i % GROUP == 0 and k == 0:
                                    last.then_inc(group_started, 1)
                    last.then_inc(proj1_ready, 1)
                    if 1 <= j <= 4:
                        pe.wait_ge(low1_copied, 1)
                        pe.wait_ge(gates_loaded, 16)
                        if j >= 3:
                            pe.wait_ge(z_copied, 2 * (j - 2))
                        d, n = (j - 1) // 2, (j - 1) % 2
                        for h in (2 * n, 2 * n + 1):
                            last = nc.tensor.matmul(ps[5 + n][:, (h % 2) * S:(h % 2 + 1) * S],
                                                    gate_up[:, d * RW + h * P:d * RW + (h + 1) * P], low1[0:GRANK, :], start=True, stop=True)
                        last.then_inc(z_ready, 1)

            @block.scalar
            def _(act):
                norm_rstd(act, 2)
                act.wait_ge(proj1_ready, 1)
                nc.scalar.activation(low1[0:GRANK, :], ps[4][0:GRANK, 0:S], ACT.Copy).then_inc(low1_copied, 1)

                def z_copy(m):
                    d, n = m // 2, m % 2
                    act.wait_ge(z_ready, m + 1)
                    for h in (2 * n, 2 * n + 1):
                        nc.scalar.activation(G[:, d, h], ps[5 + n][:, (h % 2) * S:(h % 2 + 1) * S], ACT.Identity,
                                             bias=par("bias_b" if d else "bias_f", h)).then_inc(z_copied, 1)

                for j in range(12):
                    act.wait_ge(proj1_ready, j + 2)
                    func = ACT.Copy
                    if j < 2:
                        dst, src = q1[:, 2 * j:2 * j + 2], two(j % 4)
                    elif j < 4:
                        dst, src = k1[:, 2 * (j - 2):2 * (j - 2) + 2], two(j % 4)
                    elif j < 8:
                        dst = v1[:, :, 2 * (j - 4) * P:2 * (j - 3) * P].rearrange("p t (i n) -> p i t n", i=2)
                        src = ps[j % 4][:, :].rearrange("p (i t n) -> p i t n", i=2, t=2)
                    else:
                        dst, src, func = swish[:, 2 * (j - 8):2 * (j - 8) + 2], two(j % 4), ACT.Silu
                    nc.scalar.activation(dst, src, func).then_inc(proj1_copied, 1)
                    if 1 <= j <= 4:
                        z_copy(j - 1)

            @block.vector
            def _(dve):
                dve.wait_ge(out_added, 8)
                norm_squares(dve, 2, squares2)
                norm_scale(dve, 2, "o_norm1")
                nc.vector.tensor_copy(reset1.rearrange("p (a b) -> p a b", b=C), cst("reset").unsqueeze(1).to_broadcast([P, GH * NCH, C]))
        if stop <= 7:
            return

        Q1, K1 = area(10240, 2, GH, S), area(12288, 2, GH, S)
        states = area(14336, 3, 2, GH, 2 * P)
        K_tok = area(6144, TT, 2, GH, P)
        att = area(8192, TT, 2, GH, C)
        o_sq, o_rstd = area(0, KT, S), area(2048, GH, S)
        G8, run8 = area(6144, 2 * GH * S), area(8192, 2 * GH * S)
        GS = 1.0 / 16
        (abs_ready, log_ready, run1_ready, scales1_ready, qk1_ready, k1_turned, k1_copied, att_ready, att_masked, add1_ready,
         states_ready, o_ready, o_copied, o_sq_ready, o_sum_ready, o_rstd_ready, mixed1) = (
            sem(n) for n in ("abs_ready", "log_ready", "run1_ready", "scales1_ready", "qk1_ready", "k1_turned", "k1_copied", "att_ready",
                             "att_masked", "add1_ready", "states_ready", "o_ready", "o_copied", "o_sq_ready", "o_sum_ready",
                             "o_rstd_ready", "mixed1"))

        with nc.Block(no_gpsimd_drain=True) as block:
            @block.vector
            def _(dve):
                dve_then(dve, nc.vector.tensor_scalar(run8, G8, -1.0, None, mul))
                nc.vector.tensor_tensor(run8, run8, G8, ALU.min).then_inc(abs_ready, 1)
                dve.wait_ge(log_ready, 1)
                dve_then(dve, nc.vector.scalar_tensor_tensor(G8, G8, 0.0, run8, ALU.min, sub))
                for d in range(2):
                    dve_then(dve, nc.vector.tensor_tensor_scan(flat(run1[:, d]), reset1, flat(G[:, d]), 0.0, mul, add))
                nc.vector.tensor_tensor(G8, run8, G8, sub).then_inc(run1_ready, 1)
                dve.wait_ge(run1_ready, 1)
                L = run1.rearrange("p d t (c n) -> p d t c n", n=C)
                X = G.rearrange("p d t (c n) -> p d t c n", n=C)
                dve_then(dve, nc.vector.tensor_copy(mid[:, 0], L[:, 0, :, :, C // 2]))
                dve_then(dve, nc.vector.tensor_copy(mid[:, 1], X[:, 1, :, :, C // 2 - 1]))
                dve_then(dve, nc.vector.tensor_tensor(tail, L[:, :, :, :, C - 1], mid, sub))
                for s in range(3):
                    dve_then(dve, nc.vector.tensor_tensor(factor[:, s, 0], tail[:, 0, :, s], mid[:, 0, :, s + 1], add))
                    dve_then(dve, nc.vector.tensor_tensor(factor[:, s, 1], mid[:, 1, :, 3 - s], tail[:, 1, :, 2 - s], add))
                for d, v in ((0, run1), (1, G)):
                    w = v[:, d].rearrange("p t (c n) -> p (t c) n", n=C)
                    nc.vector.tensor_tensor(w, w, mid[:, d].rearrange("p t c -> p (t c)").unsqueeze(2).to_broadcast([P, 16, C]), sub)\
                        .then_inc(run1_ready, 1)
                dve.wait_ge(scales1_ready, 5)
                for d in range(2):
                    dve_then(dve, nc.vector.scalar_tensor_tensor(flat(Q1[:, d]), flat(Q1[:, d]), P ** -0.5, flat(q1), mul, mul))
                    nc.vector.tensor_tensor(flat(K1[:, d]), flat(K1[:, d]), flat(k1), mul).then_inc(qk1_ready, 1)
                dve_then(dve, nc.vector.memset(area(8192, 1024), 0.0))
                for t in range(TT):
                    dve.wait_ge(att_ready, t + 1)
                    for d in range(2):
                        last = nc.vector.copy_predicated(att[:, t, d], cst("read")[:, d * C:(d + 1) * C].bitcast(u32).unsqueeze(1).to_broadcast([P, GH, C]),
                                                         bank8(t)[:, GH * d:GH * (d + 1)])
                    last.then_inc(att_masked, 1)
                for s in range(3):
                    for n in range(4):
                        d, h = n // 2, 2 * (n % 2)
                        dve.wait_ge(add1_ready, 4 * s + n + 1)
                        new = states[:, s, d, h:h + 2]
                        scale = factor[:, s, d, h:h + 2].unsqueeze(2).to_broadcast([P, 2, 2 * P])
                        if s == 0:
                            nc.vector.tensor_tensor(new, two(4 + n), scale, mul).then_inc(states_ready, 1)
                        else:
                            dve_then(dve, nc.vector.tensor_tensor(new, two(4 + n), states[:, s - 1, d, h:h + 2], add))
                            nc.vector.tensor_tensor(new, new, scale, mul).then_inc(states_ready, 1)
                for n in range(4):
                    dve.wait_ge(o_copied, 4)
                    o = yT[:, 2 * n:2 * n + 2]
                    nc.vector.tensor_tensor(o_sq[:, 2 * n:2 * n + 2], o, o, mul).then_inc(o_sq_ready, 1)
                for h in range(GH):
                    dve.wait_ge(o_rstd_ready, h // 2 + 1)
                    for v in range(2):
                        dve_then(dve, nc.vector.scalar_tensor_tensor(yT[:, 2 * h + v], yT[:, 2 * h + v], par("out_norm", v), o_rstd[:, h], mul, mul))
                    o = yT[:, 2 * h:2 * h + 2]
                    nc.vector.tensor_tensor(o, o, swish[:, 2 * h:2 * h + 2], mul).then_inc(mixed1, 1)

            @block.scalar
            def _(act):
                act.wait_ge(abs_ready, 1)
                act_then(act, nc.scalar.activation(run8, run8, ACT.Exp))
                nc.scalar.activation(run8, run8, ACT.Ln, bias=par("one")).then_inc(log_ready, 1)
                act.wait_ge(run1_ready, 3)
                for out, src, s in ((Q1[:, 0], run1[:, 0], GS), (K1[:, 0], run1[:, 0], -GS), (Q1[:, 1], G[:, 1], -GS), (K1[:, 1], G[:, 1], GS)):
                    nc.scalar.activation(flat(out), flat(src), ACT.Exp, scale=s).then_inc(scales1_ready, 1)
                nc.scalar.activation(factor, factor, ACT.Exp, scale=GS).then_inc(scales1_ready, 1)
                for n in range(4):
                    act.wait_ge(k1_turned, n + 1)
                    nc.scalar.activation(K_tok[:, n // 2, n % 2], ps[2 + n][:, :].rearrange("p (h n) -> p h n", h=GH), ACT.Copy)\
                        .then_inc(k1_copied, 1)
                for n in range(4):
                    act.wait_ge(o_ready, n + 1)
                    dst = yT[:, 4 * (n % 2):4 * (n % 2) + 4].rearrange("p i (t b n) -> p i t b n", t=2, b=2)[:, :, :, n // 2]
                    nc.scalar.activation(dst, ps[n][:, :].rearrange("p (i t n) -> p i t n", i=4, t=2), ACT.Copy).then_inc(o_copied, 1)
                for n in range(2):
                    act.wait_ge(o_sum_ready, n + 1)
                    act_then(act, nc.scalar.activation(o_rstd[:, 2 * n:2 * n + 2], two(4 + n), ACT.Ln, scale=1.0 / (2 * P), bias=par("eps")))
                for n in range(2):
                    nc.scalar.activation(o_rstd[:, 2 * n:2 * n + 2], o_rstd[:, 2 * n:2 * n + 2], ACT.Exp, scale=-0.5).then_inc(o_rstd_ready, 1)

            @block.tensor
            def _(pe):
                pe.wait_ge(qk1_ready, 2)
                for t in range(TT):
                    for d in range(2):
                        for h in range(GH):
                            for b in range(2):
                                c = slice((2 * t + b) * C, (2 * t + b + 1) * C)
                                last = nc.tensor.matmul(bank8(t)[C * b:C * (b + 1), GH * d + h], K1[:, d, h, c], Q1[:, d, h, c], start=True, stop=True)
                    last.then_inc(att_ready, 1)
                for n in range(4):
                    for h in range(GH):
                        last = nc.tensor.transpose(ps[2 + n][:, h * P:(h + 1) * P], K1[:, n % 2, h, (n // 2) * P:(n // 2 + 1) * P], ident)
                    last.then_inc(k1_turned, 1)
                pe.wait_ge(k1_copied, 4)
                for s in range(3):
                    for n in range(4):
                        d = n // 2
                        c = s if d == 0 else NCH - 1 - s
                        rows = slice(C * (c % 2), C * (c % 2 + 1))
                        if s:
                            pe.wait_ge(states_ready, 4 * (s - 1) + n + 1)
                        for h in (2 * (n % 2), 2 * (n % 2) + 1):
                            last = nc.tensor.matmul(ps[4 + n][:, (h % 2) * S:(h % 2 + 1) * S], K_tok[rows, c // 2, d, h],
                                                    v1[rows, c // 2, h * 2 * P:(h + 1) * 2 * P], start=True, stop=True)
                        last.then_inc(add1_ready, 1)
                pe.wait_ge(att_masked, 2)
                pe.wait_ge(states_ready, 12)
                for n in range(4):
                    parity = n // 2
                    rows = slice(C * parity, C * (parity + 1))
                    for i in range(4 * (n % 2), 4 * (n % 2) + 4):
                        h, vt = i // 2, i % 2
                        for t in range(TT):
                            c = 2 * t + parity
                            out = ps[n][:, (i % 4) * P + t * C:(i % 4) * P + (t + 1) * C]
                            vs = slice(h * 2 * P + vt * P, h * 2 * P + (vt + 1) * P)
                            terms = [(v1[rows, t, vs], att[rows, t, d, h]) for d in range(2)]
                            if c:
                                terms.append((states[:, c - 1, 0, h, vt * P:(vt + 1) * P], Q1[:, 0, h, c * C:(c + 1) * C]))
                            if c < NCH - 1:
                                terms.append((states[:, NCH - 2 - c, 1, h, vt * P:(vt + 1) * P], Q1[:, 1, h, c * C:(c + 1) * C]))
                            for m, (left, right) in enumerate(terms):
                                last = nc.tensor.matmul(out, left, right, start=(m == 0), stop=(m == len(terms) - 1))
                    last.then_inc(o_ready, 1)
                for h in range(GH):
                    pe.wait_ge(o_sq_ready, h + 1)
                    for v in range(2):
                        last = nc.tensor.matmul(ps[4 + h // 2][:, (h % 2) * S:(h % 2 + 1) * S], cst("ones"), o_sq[:, 2 * h + v],
                                                start=(v == 0), stop=(v == 1))
                    if h % 2:
                        last.then_inc(o_sum_ready, 1)
        if stop <= 8:
            return

        squares3 = area(0, KT, S)
        x_tok1 = area(0, TT, D)
        logits, top_idx_f = area(11264, TT, E), area(11280, TT, E)
        top = area(11296, TT, E)
        top_idx = sb("top_idx", [P, TT, E], u32)
        gap = area(11312, 4, TT)
        chosen, weight, hot = area(11328, TT, E), area(11344, TT, E), area(11360, 2, TT, E)
        rank, counts = area(11392, TT, E), area(11408, E)
        most = area(11416, 1)
        more = sb("more", [P, PASSES], i32)
        (logits_ready, turned1, tok1_copied, gap_ready, gap_exp, chosen_ready, ranks1_ready, routed) = (
            sem(n) for n in ("logits_ready", "turned1", "tok1_copied", "gap_ready", "gap_exp", "chosen_ready", "ranks1_ready", "routed"))

        with nc.Block(no_gpsimd_drain=True) as block:
            @block.sync
            def _(sp):
                load_ahead(sp, G_OUT1 - 1, G_MOE - 1)

            @block.tensor
            def _(pe):
                project_out(pe, G_OUT1, 1)
                norm_sum(pe, 3, squares3)
                for t in range(TT):
                    for k in range(KT):
                        pe.wait_ge(xn_ready, 3 * KT + k + 1)
                        last = nc.tensor.matmul(ps[4][:, t * E:(t + 1) * E], xn[:, k, t * P:(t + 1) * P], sml("router")[:, k * E:(k + 1) * E],
                                                start=(k == 0), stop=(k == KT - 1))
                last.then_inc(logits_ready, 1)
                for n in range(4):
                    for k in range(4 * (n % 2), 4 * (n % 2) + 4):
                        last = nc.tensor.transpose(ps[n][:, (k % 4) * P:(k % 4 + 1) * P], xn[:, k, (n // 2) * P:(n // 2 + 1) * P], ident)
                    last.then_inc(turned1, 1)
                pe.wait_ge(chosen_ready, 1)
                nc.tensor.matmul(ps[5][:, 0:E], cst("before"), chosen[:, 0], start=True, stop=True)
                nc.tensor.matmul(ps[5][:, E:2 * E], cst("ones"), chosen[:, 0], start=True, stop=False)
                nc.tensor.matmul(ps[5][:, E:2 * E], cst("before"), chosen[:, 1], start=False, stop=True)
                nc.tensor.matmul(ps[5][:, 2 * E:3 * E], cst("ones"), chosen[:, 0], start=True, stop=False)
                nc.tensor.matmul(ps[5][:, 2 * E:3 * E], cst("ones"), chosen[:, 1], start=False, stop=True).then_inc(ranks1_ready, 1)

            @block.scalar
            def _(act):
                norm_rstd(act, 3)
                act.wait_ge(gap_ready, 1)
                nc.scalar.activation(gap[:, 1], gap[:, 0], ACT.Exp).then_inc(gap_exp, 1)
                for n in range(4):
                    act.wait_ge(turned1, n + 1)
                    nc.scalar.activation(x_tok1[:, n // 2, (n % 2) * 512:(n % 2 + 1) * 512], ps[n][:, :], ACT.Copy).then_inc(tok1_copied, 1)

            @block.vector
            def _(dve):
                add_out(dve, 1, squares3)
                norm_scale(dve, 3, "o_norm2")
                dve.wait_ge(logits_ready, 1)
                dve_then(dve, nc.vector.tensor_copy(logits.rearrange("p t e -> p (t e)"), ps[4][:, 0:TT * E]))
                for t in range(TT):
                    dve_then(dve, nc.vector.max(top[:, t], logits[:, t]))
                    dve_then(dve, nc.vector.max_index(top_idx[:, t], top[:, t], logits[:, t]))
                dve_then(dve, nc.vector.tensor_copy(top_idx_f, top_idx[:, :, :]))
                nc.vector.tensor_tensor(gap[:, 0], top[:, :, 1], top[:, :, 0], sub).then_inc(gap_ready, 1)
                for n in range(2):
                    for t in range(TT):
                        dve_then(dve, nc.vector.tensor_scalar(hot[:, n, t], cst("experts"), top_idx_f[:, t, n:n + 1], None, ALU.is_equal))
                nc.vector.tensor_tensor(chosen, hot[:, 0], hot[:, 1], add).then_inc(chosen_ready, 1)
                dve.wait_ge(gap_exp, 1)
                dve_then(dve, nc.vector.tensor_scalar(gap[:, 2], gap[:, 1], 1.0, None, add))
                dve_then(dve, nc.vector.reciprocal(gap[:, 2], gap[:, 2]))
                dve_then(dve, nc.vector.tensor_tensor(gap[:, 3], gap[:, 1], gap[:, 2], mul))
                for t in range(TT):
                    dve_then(dve, nc.vector.tensor_scalar(weight[:, t], hot[:, 0, t], gap[:, 2, t:t + 1], None, mul))
                    dve_then(dve, nc.vector.scalar_tensor_tensor(weight[:, t], hot[:, 1, t], gap[:, 3, t:t + 1], weight[:, t], mul, add))
                dve.wait_ge(ranks1_ready, 1)
                dve_then(dve, nc.vector.tensor_copy(rank.rearrange("p t e -> p (t e)"), ps[5][:, 0:2 * E]))
                dve_then(dve, nc.vector.tensor_copy(counts, ps[5][:, 2 * E:3 * E]))
                dve_then(dve, nc.vector.tensor_reduce(most, counts, AX, ALU.max))
                for p in range(PASSES):
                    last = nc.vector.tensor_scalar(more[:, p:p + 1], most, float(CAP * p), None, ALU.is_gt)
                last.then_inc(routed, 1)
        if stop <= 9:
            return

        place = area(2048, TT, E, CAP)
        placed_weight = area(3584, TT, E, CAP)
        back = area(5120, E, S)
        x_slots = area(7168, KT, CAP)
        silu_e, hidden_e = area(7936, RING, CAP), area(7936 + RING * CAP, RING, CAP)
        y_chan = area(9280, KT, CAP)
        y_slot = area(10240, D)
        place_flat, back_flat = area(2048, TT * E, CAP), area(5120, E * S)
        rank_p = area(11424, TT, E)
        (placed, back_turned, back_copied, gathered, x_slots_ready, pair_e_ready, silu_e_ready, hidden_e_ready, down_done,
         acc_copied, acc_zeroed, y_turned, y_slot_ready, scattered, x_added) = (
            sem(n) for n in ("placed", "back_turned", "back_copied", "gathered", "x_slots_ready", "pair_e_ready", "silu_e_ready",
                             "hidden_e_ready", "down_done", "acc_copied", "acc_zeroed", "y_turned", "y_slot_ready", "scattered",
                             "x_added"))
        w_moe = io["w_moe"].rearrange("e t p n -> (e t) p n")
        N_MOE = E * FET
        BODY = FET // RING

        class Pass:

            def __init__(self, p):
                self.p, self.tiles0, self.e0 = p, N_MOE * p, E * p
                self.g0 = G_MOE + self.tiles0

        def all_passes(eng, body):
            body(eng, Pass(0))
            for p in range(1, PASSES):
                with eng.If(eng.value_load(more[0:1, p:p + 1], min_val=0, max_val=1) > 0):
                    body(eng, Pass(p))

        def moe_loads(sp, at):
            p, tiles0, e0, g0 = at.p, at.tiles0, at.e0, at.g0
            first = 0
            if p == 0:
                load_ahead(sp, G_MOE - 1, G_MOE)
                first = 1
            with sp.Fori(first, N_MOE // RING) as i:
                for j in range(RING):
                    slot = (g0 + j) % RING
                    sp.wait_ge(group_started, i * RING + (g0 + j - RING + 2))
                    sp.dma_start(ring[:, slot].rearrange("p a k n -> p (a k n)"),
                                 w_moe[bass.ds(i * RING + j, 1)].rearrange("a p n -> (a p) n")).then_inc(slot_loaded[slot], 16)

        def moe_products(pe, at):
            p, tiles0, e0, g0 = at.p, at.tiles0, at.e0, at.g0
            for n in range(4):
                pe.wait_ge(placed, TT * (p + 1))
                for e in (2 * n, 2 * n + 1):
                    for t in range(TT):
                        last = nc.tensor.transpose(ps[2 + n][0:CAP, (e % 2) * S + t * P:(e % 2) * S + (t + 1) * P],
                                                   placed_weight[:, t, e], ident)
                last.then_inc(back_turned, 1)
            pe.wait_ge(back_copied, 4 * (p + 1))

            def pair(e, i, t, j):
                g = g0 + j
                pe.wait_ge(slot_loaded[g % RING], (e * BODY + i + (g // RING + 1)) * 16)
                pe.wait_ge(hidden_e_ready, e * FET + t + (tiles0 + LEAD - 2))
                gate_up_tile(pe, g % RING, j, x_slots, CAP, pair_e_ready)

            def down(e, t, j):
                pe.wait_ge(hidden_e_ready, e * FET + t + (tiles0 + LEAD + 1))
                for k in range(KT):
                    last = nc.tensor.matmul(ps[k // 4][:, (k % 4) * CAP:(k % 4 + 1) * CAP], ring[:, (g0 + j) % RING, 2, k],
                                            hidden_e[:, j], start=False, stop=False, skip_group_check=True)
                    if k == 0:
                        last.then_inc(group_started, 1)
                last.then_inc(down_done, 1)

            with pe.Fori(0, E) as e:
                pe.wait_ge(x_added, e * 4 + (4 * e0 + 1))
                for n in range(2):
                    for k in range(4 * n, 4 * n + 4):
                        for t in range(TT):
                            last = nc.tensor.matmul(ps[2 + n][:, (k % 4) * CAP:(k % 4 + 1) * CAP], x_tok1[:, t, k * P:(k + 1) * P],
                                                    place_flat[:, bass.ds(e + t * E, 1)].rearrange("p a n -> p (a n)"),
                                                    start=(t == 0), stop=(t == TT - 1))
                    last.then_inc(gathered, 1)
                pe.wait_ge(x_slots_ready, e * 2 + (2 * e0 + 2))
                pe.wait_ge(acc_zeroed, e + (e0 + 1))
                pair(e, 0, 0, 0)
                with pe.Fori(0, BODY - 1) as i:
                    for j in range(RING):
                        t = i * RING + j
                        pair(e, i if j + 1 < RING else i + 1, t + 1, (j + 1) % RING)
                        down(e, t, j)
                for j in range(RING):
                    t = (BODY - 1) * RING + j
                    if j + 1 < RING:
                        pair(e, BODY - 1, t + 1, j + 1)
                    down(e, t, j)
                for n in range(2):
                    pe.wait_ge(acc_copied, e * 2 + (2 * e0 + n + 1))
                    for k in range(4 * n, 4 * n + 4):
                        last = nc.tensor.transpose(ps[2 + n][0:CAP, (k % 4) * P:(k % 4 + 1) * P], y_chan[:, k], ident)
                    last.then_inc(y_turned, 1)
                for r in range(4):
                    if r == 0:
                        pe.wait_ge(y_slot_ready, e * 2 + (2 * e0 + 2))
                    if r >= 2:
                        pe.wait_ge(x_added, e * 4 + (4 * e0 + r))
                    for k in (2 * r, 2 * r + 1):
                        last = nc.tensor.matmul(ps[2 + r % 2][:, (k % 2) * S:(k % 2 + 1) * S], y_slot[0:CAP, k * P:(k + 1) * P],
                                                back_flat[0:CAP, bass.ds(e * S, S)], start=True, stop=True)
                    last.then_inc(scattered, 1)

        def moe_activations(act, at):
            p, tiles0, e0, g0 = at.p, at.tiles0, at.e0, at.g0
            for n in range(4):
                act.wait_ge(back_turned, 4 * p + n + 1)
                nc.scalar.activation(back[0:CAP, 2 * n:2 * n + 2], ps[2 + n][0:CAP, :].rearrange("p (a b) -> p a b", a=2), ACT.Copy)\
                    .then_inc(back_copied, 1)
            with act.Fori(0, E) as e:
                for n in range(2):
                    act.wait_ge(gathered, e * 2 + (2 * e0 + n + 1))
                    nc.scalar.activation(x_slots[:, 4 * n:4 * n + 4], ps[2 + n][:, 0:4 * CAP].rearrange("p (a b) -> p a b", a=4), ACT.Copy)\
                        .then_inc(x_slots_ready, 1)
                with act.Fori(0, BODY) as i:
                    for j in range(RING):
                        act.wait_ge(pair_e_ready, e * FET + i * RING + (tiles0 + j + 1))
                        nc.scalar.activation(silu_e[:, j], ps[PAIR_BANK[j]][:, 0:CAP], ACT.Silu).then_inc(silu_e_ready, 1)
                for n in range(2):
                    act.wait_ge(y_turned, e * 2 + (2 * e0 + n + 1))
                    nc.scalar.activation(y_slot[0:CAP, n * 512:(n + 1) * 512], ps[2 + n][0:CAP, :], ACT.Copy).then_inc(y_slot_ready, 1)

        def moe_elementwise(dve, at):
            p, tiles0, e0, g0 = at.p, at.tiles0, at.e0, at.g0
            dve_then(dve, nc.vector.tensor_scalar(rank_p, rank, float(CAP * p), None, sub))
            for t in range(TT):
                slots_b = cst("slots").unsqueeze(1).to_broadcast([P, E, CAP])
                dve_then(dve, nc.vector.tensor_tensor(place[:, t], slots_b, rank_p[:, t].unsqueeze(2).to_broadcast([P, E, CAP]), ALU.is_equal))
                dve_then(dve, nc.vector.tensor_tensor(place[:, t], place[:, t], chosen[:, t].unsqueeze(2).to_broadcast([P, E, CAP]), mul))
                nc.vector.tensor_tensor(placed_weight[:, t], place[:, t], weight[:, t].unsqueeze(2).to_broadcast([P, E, CAP]), mul)\
                    .then_inc(placed, 1)
            if p == 0:
                nc.vector.memset(ps[0][:, :], 0.0)
                nc.vector.memset(ps[1][:, :], 0.0).then_inc(acc_zeroed, 1)
                for n in range(LEAD + 1):
                    nc.vector.memset(area(11440 + n, 1), 0.0).then_inc(hidden_e_ready if n < LEAD else x_added, 1)
            with dve.Fori(0, E) as e:
                with dve.Fori(0, BODY) as i:
                    for j in range(RING):
                        dve.wait_ge(silu_e_ready, e * FET + i * RING + (tiles0 + j + 1))
                        nc.vector.tensor_tensor(hidden_e[:, j], silu_e[:, j], ps[PAIR_BANK[j]][:, CAP:2 * CAP], mul)\
                            .then_inc(hidden_e_ready, 1)
                dve.wait_ge(down_done, e * FET + (tiles0 + FET))
                for n in range(2):
                    nc.vector.tensor_copy(y_chan[:, 4 * n:4 * n + 4], ps[n][:, 0:4 * CAP].rearrange("p (a b) -> p a b", a=4))\
                        .then_inc(acc_copied, 1)
                dve.wait_ge(acc_copied, e * 2 + (2 * e0 + 2))
                nc.vector.memset(ps[0][:, :], 0.0)
                nc.vector.memset(ps[1][:, :], 0.0).then_inc(acc_zeroed, 1)
                for r in range(4):
                    dve.wait_ge(scattered, e * 4 + (4 * e0 + r + 1))
                    x = xT[:, 2 * r:2 * r + 2]
                    nc.vector.tensor_tensor(x, x, two(2 + r % 2), add).then_inc(x_added, 1)

        with nc.Block(no_gpsimd_drain=True) as block:
            @block.sync
            def _(sp):
                all_passes(sp, moe_loads)

            @block.tensor
            def _(pe):
                all_passes(pe, moe_products)

            @block.scalar
            def _(act):
                all_passes(act, moe_activations)

            @block.vector
            def _(dve):
                all_passes(dve, moe_elementwise)

        if stop <= 10:
            return

        y_tok = area(0, TT, D)
        (result_turned, result_copied, stored) = (sem(n) for n in ("result_turned", "result_copied", "stored"))
        with nc.Block(no_gpsimd_drain=True) as block:
            @block.tensor
            def _(pe):
                for n in range(4):
                    for k in range(4 * (n % 2), 4 * (n % 2) + 4):
                        last = nc.tensor.transpose(ps[n][:, (k % 4) * P:(k % 4 + 1) * P], xT[:, k, (n // 2) * P:(n // 2 + 1) * P], ident)
                    last.then_inc(result_turned, 1)

            @block.vector
            def _(dve):
                for n in range(4):
                    dve.wait_ge(result_turned, n + 1)
                    nc.vector.tensor_copy(y_tok[:, n // 2, (n % 2) * 512:(n % 2 + 1) * 512], ps[n][:, :]).then_inc(result_copied, 1)

            @block.sync
            def _(sp):
                for t in range(TT):
                    sp.wait_ge(result_copied, 2 * (t + 1))
                    sp.dma_start(io["out"][t * P:(t + 1) * P, :], y_tok[:, t]).then_inc(stored, 16)
                sp.wait_ge(stored, 32)


def _const():
    out = np.zeros((P, N_CONST), np.float32)

    def put(name, v):
        a, b = CONST[name]
        out[:, a:b] = v

    p = np.arange(P)
    put("ident", np.eye(P))
    put("headsum", (p[:, None] // HD == p[None] // HD))
    put("ones", 1.0)
    rot = np.zeros((P, P))
    even = p[::2]
    rot[even + 1, even] = -1.0
    rot[even, even + 1] = 1.0
    put("rot", rot)
    put("before", p[:, None] < p[None])
    t = np.arange(S)
    freq = (np.float32(10000.0) ** (-np.arange(0, HD // 2, 2, dtype=np.float32) / np.float32(HD // 2))).astype(np.float32)
    row, col = (t // 64).astype(np.float32), (t % 64).astype(np.float32)
    ang = np.concatenate([row[:, None] * freq, col[:, None] * freq], -1)
    ang = ang[:, (p % HD) // 2].T.astype(np.float64)
    put("cos", np.cos(ang))
    put("sin", np.sin(ang))
    r, c = (p % C)[:, None], np.arange(C)[None]
    low, up = r > c, r < c
    for b in LEVELS:
        pair = (r // (2 * b) == c // (2 * b)) & (r // b != c // b)
        put(f"level{b}", np.concatenate([pair & low, pair & up], 1))
        if b == 1:
            put("level1_t", np.concatenate([pair & up, pair & low], 1))
    put("strict", np.concatenate([up, low], 1))
    put("read", np.concatenate([r <= c, low], 1))
    put("ident64", r == c)
    put("slots", np.arange(CAP)[None])
    put("experts", np.arange(E)[None])
    put("reset", (c > 0) * np.ones((P, 1)))
    return out


def _tiles(w, size=P):
    k, n = w.shape
    return np.ascontiguousarray(w.reshape(k // P, P, n // P, P).transpose(2, 1, 0, 3)).reshape(n // P, P, k)


def _groups(tiles):
    n = -(-len(tiles) // GROUP)
    out = np.zeros((n * GROUP,) + tiles.shape[1:], tiles.dtype)
    out[:len(tiles)] = tiles
    return np.ascontiguousarray(out.reshape(n, GROUP, P, D).transpose(0, 2, 1, 3)).reshape(n, P, GROUP * D)


def _arrays(i):
    def col(v):
        return np.asarray(v).reshape(-1, P).T

    i = {k: np.asarray(v) for k, v in i.items()}
    param = np.zeros((P, N_PARAM), np.float32)

    def put(name, v):
        a, b = PARAM[name]
        param[:, a:b] = v

    for name, key in [("e_norm1", "e_norm1"), ("mu", "e_shift_mu"), ("w0_f", "e_w0_f"), ("w0_b", "e_w0_b"), ("a0_f", "e_a0_f"),
                      ("a0_b", "e_a0_b"), ("k_k", "e_k_k"), ("k_a", "e_k_a"), ("r_k", "e_r_k"), ("gn_w", "e_gn_w"), ("gn_b", "e_gn_b"),
                      ("e_norm2", "e_norm2"), ("o_norm1", "o_norm1"), ("bias_f", "o_gate_bias_f"), ("bias_b", "o_gate_bias_b"),
                      ("out_norm", "o_out_norm"), ("o_norm2", "o_norm2")]:
        put(name, col(i[key]))
    for name, key in [("q_norm", "e_q_norm"), ("k_norm", "e_k_norm")]:
        put(name, np.concatenate([i[key][0], i[key][0]])[:, None])
    put("eps", EPS)
    put("gn_eps", GN_EPS)
    put("kk_bias", 0.5 * np.log(KK_SCALE))
    put("one", 1.0)

    small = np.zeros((P, N_SMALL), np.float32)

    def puts(name, v):
        a, b = SMALL[name]
        small[:v.shape[0], a:b] = v

    puts("up_f", np.concatenate([i["e_w_up_f"][0], i["e_a_up_f"][0]]))
    puts("up_b", np.concatenate([i["e_w_up_b"][0], i["e_a_up_b"][0]]))
    puts("g_up", i["e_g_up"][0])
    puts("router", i["o_router"][0].reshape(KT, P, E).transpose(1, 0, 2).reshape(P, KT * E))
    w1 = i["o_w_in"][0]
    puts("w_gd", w1[:, 2048:2064].reshape(KT, P, GRANK).transpose(1, 0, 2).reshape(P, KT * GRANK))

    w0 = i["e_w_in"][0]
    q = w0[:, RW_IN:RW_IN + ATT].reshape(D, 2, 4, HD).transpose(0, 2, 1, 3).reshape(D, ATT)
    w0 = np.concatenate([w0[:, :RW_IN], q, w0[:, RW_IN + ATT:]], 1)
    wo0 = i["e_w_out"][0]
    att = wo0[RW:].reshape(2, 4, HD, D).transpose(1, 0, 2, 3).reshape(ATT, D)
    wo0 = np.concatenate([wo0[:RW], att], 0)
    w1 = np.concatenate([w1[:, :2048], w1[:, 2064:]], 1)
    down = i["e_ffn_down"][0].reshape(FT, P, D)
    ffn = np.stack([_tiles(i["e_ffn_gate"][0]), _tiles(i["e_ffn_up"][0]), down], 2).reshape(FT, P, GROUP * D)
    moe = np.empty((E, FET, P, GROUP, D), np.float32)
    for e in range(E):
        moe[e, :, :, 0] = _tiles(i["o_exp_gate"][0, e])
        moe[e, :, :, 1] = _tiles(i["o_exp_up"][0, e])
        moe[e, :, :, 2] = i["o_exp_down"][0, e].reshape(FET, P, D)
    return {"x": np.ascontiguousarray(i["x"][0]), "const": _const(), "param": param, "small": small,
            "gate_up": np.concatenate([i["o_gate_up_f"][0], i["o_gate_up_b"][0]], 1),
            "w_in0": _groups(_tiles(w0)), "w_out0": _groups(_tiles(wo0)), "w_ffn": ffn,
            "w_in1": _groups(_tiles(w1)), "w_out1": _groups(_tiles(i["o_w_out"][0])),
            "w_moe": moe.reshape(E, FET, P, GROUP * D)}


def kernel(**inputs):
    import concourse.bacc as _bacc
    from concourse.bass_utils import run_bass_kernel_spmd as _run

    nc = _bacc.Bacc("TRN2", target_bir_lowering=False, num_devices=1)
    arrays = _arrays(inputs)
    io = {n: nc.dram_tensor(f"in_{n}", a.shape, mybir.dt.float32, kind="ExternalInput").ap() for n, a in arrays.items()}
    io["out"] = nc.dram_tensor("out_y", (S, D), mybir.dt.float32, kind="ExternalOutput").ap()
    program(nc, io)
    r = _run(nc, [{f"in_{n}": a for n, a in arrays.items()}], core_ids=[0])
    return np.asarray(r.results[0]["out_y"]).reshape(1, S, D)
```

```python
import concourse.bass as bass
from concourse import mybir
from contextlib import ExitStack
import numpy as np

D, S = 1024, 256
P = 128
KT = D // P
TT = S // P
HD = 64
RW = 512
RT = RW // P
C = 64
NCH = S // C
RW_IN = 3 * RW + 64 + 64 + 128
ATT = 512
FF = 2816
FT = FF // P
E = 8
FE = 3584
FET = FE // P
CAP = 96
PASSES = -(-S // CAP)
GH = 4
GRANK = 16
RING = 4
GROUP = 3
EPS = 1e-6
GN_EPS = 64e-5
DECAY_C = float(np.exp(-0.5))
KK_SCALE = float(2.0 ** 20)

G_IN0 = 0
N_IN0 = 7
G_OUT0 = G_IN0 + N_IN0
N_OUT0 = 3
G_FFN = G_OUT0 + N_OUT0
G_IN1 = G_FFN + FT
N_IN1 = 8
G_OUT1 = G_IN1 + N_IN1
N_OUT1 = 3
G_MOE = G_OUT1 + N_OUT1

LEVELS = [1, 2, 4, 8, 16, 32]


def layout(parts):
    at, out = 0, {}
    for name, n in parts:
        out[name] = (at, at + n)
        at += n
    return out, at


CONST, N_CONST = layout(
    [("ident", P), ("headsum", P), ("ones", P), ("rot", P), ("before", P), ("cos", S), ("sin", S)]
    + [(f"level{b}", 2 * C) for b in LEVELS]
    + [("level1_t", 2 * C), ("strict", 2 * C), ("read", 2 * C), ("ident64", C), ("slots", CAP), ("experts", E), ("reset", C)]
)
PARAM, N_PARAM = layout(
    [("e_norm1", KT), ("mu", 14), ("w0_f", RT), ("w0_b", RT), ("a0_f", RT), ("a0_b", RT), ("k_k", RT), ("k_a", RT),
     ("r_k", RT), ("gn_w", RT), ("gn_b", RT), ("q_norm", 1), ("k_norm", 1), ("e_norm2", KT), ("o_norm1", KT),
     ("bias_f", GH), ("bias_b", GH), ("out_norm", 2), ("o_norm2", KT), ("eps", 1), ("gn_eps", 1), ("kk_bias", 1), ("one", 1)]
)
SMALL, N_SMALL = layout(
    [("up_f", RW), ("up_b", RW), ("g_up", RW), ("router", KT * E), ("w_gd", KT * GRANK)]
)
A_, R_, B_, K_ = 0, 2048, 4096, 6144
V_, GATE_, BONUS_, TEMP_ = 8192, 9216, 10240, 11264
X_HI, X_LO = 15360, 17408
W_HI = 19456
W_LO = W_HI + 2 * GROUP * D
N_SCRATCH = W_LO + 2 * GROUP * D
TOP = 229344

T_IN0 = 0
T_OUT0 = T_IN0 + 20
T_IN1 = T_OUT0 + KT
T_OUT1 = T_IN1 + 24


def program(nc, io, stop=99):
    f32, i32, u32, f32r = mybir.dt.float32, mybir.dt.int32, mybir.dt.uint32, mybir.dt.float32r
    ACT = mybir.ActivationFunctionType
    ALU = mybir.AluOpType
    AX = mybir.AxisListType.X
    mul, add, sub = ALU.mult, ALU.add, ALU.subtract
    ctx = ExitStack()

    def sb(name, shape, dt=f32):
        return ctx.enter_context(nc.sbuf_tensor(name, shape, dt))

    def sem(name):
        return ctx.enter_context(nc.semaphore(name))

    with ctx:
        ring = sb("ring", [P, RING, GROUP * D])
        xT = sb("xT", [P, KT, S])
        xn = sb("xn", [P, KT, S])
        const = sb("const", [P, N_CONST])
        param = sb("param", [P, N_PARAM])
        small = sb("small", [P, N_SMALL])
        rstd = sb("rstd", [P, S])
        scratch = nc.alloc_sbuf_tensor_at("scratch", [P, N_SCRATCH], f32, offset=TOP - 4 * N_SCRATCH)
        ps = [ctx.enter_context(nc.psum_tensor(f"bank{i}", [P, 512], f32)) for i in range(8)]

        def cst(name):
            a, b = CONST[name]
            return const[:, a:b]

        def par(name, i=0):
            a = PARAM[name][0] + i
            return param[:, a:a + 1]

        def sml(name):
            a, b = SMALL[name]
            return small[:, a:b]

        def area(at, *shape):
            n = int(np.prod(shape))
            v = scratch[:, at:at + n]
            if len(shape) == 1:
                return v
            names = "abcde"[:len(shape)]
            return v.rearrange(f"p ({' '.join(names)}) -> p {' '.join(names)}", **dict(zip(names, shape)))

        def two(b, n=2):
            return ps[b][:, :].rearrange("p (a b) -> p a b", a=n)

        def parts(name, at, shape):
            return tuple(nc.alloc_sbuf_tensor_at(f"{name}_{part}", [P] + shape, f32r, offset=TOP - 4 * (N_SCRATCH - a))
                         for part, a in zip(("high", "low"), at))

        x_split = parts("x", (X_HI, X_LO), [KT, S])
        w_split = parts("w", (W_HI, W_LO), [2, GROUP * D])

        def high_part(dst, src):
            return nc.scalar.activation(dst, src, ACT.Copy)

        def low_part(dst, src, high):
            return nc.vector.tensor_tensor(dst, src, high.bitcast(f32), sub)

        def split_product(out, left, right, start, stop, **flags):
            nc.tensor.matmul(out, left[0], right[0], start=start, stop=False, **flags)
            nc.tensor.matmul(out, left[0], right[1], start=False, stop=False, **flags)
            return nc.tensor.matmul(out, left[1], right[0], start=False, stop=stop, **flags)

        ident = cst("ident")

        consts_loaded, x_loaded = sem("consts_loaded"), sem("x_loaded")
        slot_loaded = [sem(f"slot_loaded{i}") for i in range(RING)]
        back_loaded = [sem(f"back_loaded{i}") for i in range(RING)]
        front_high, back_high, front_split, back_split = (sem(n) for n in ("front_high", "back_high", "front_split", "back_split"))
        tile_done = sem("tile_done")
        x_high_ready, x_split_ready = sem("x_high_ready"), sem("x_split_ready")
        dve_order, act_order = sem("dve_order"), sem("act_order")
        squares_ready, sum_ready, rstd_ready, xn_ready = (sem(n) for n in ("squares_ready", "sum_ready", "rstd_ready", "xn_ready"))

        dve_steps, act_steps = [0], [0]

        def dve_then(dve, instruction):
            instruction.then_inc(dve_order, 1)
            dve_steps[0] += 1
            dve.wait_ge(dve_order, dve_steps[0])

        def act_then(act, instruction):
            instruction.then_inc(act_order, 1)
            act_steps[0] += 1
            act.wait_ge(act_order, act_steps[0])

        def load_group(sp, g, src):
            if g >= RING:
                sp.wait_ge(back_split, g - RING + 1)
            if g < G_MOE:
                sp.dma_start(ring[:, g % RING], src).then_inc(slot_loaded[g % RING], 16)
            else:
                sp.dma_start(ring[:, g % RING, 0:2 * D], src[:, 0:2 * D]).then_inc(slot_loaded[g % RING], 16)
                sp.dma_start(ring[:, g % RING, 2 * D:], src[:, 2 * D:]).then_inc(back_loaded[g % RING], 16)

        stream = ([io["w_in0"][i] for i in range(N_IN0)] + [io["w_out0"][i] for i in range(N_OUT0)]
                  + [io["w_ffn"][i] for i in range(FT)] + [io["w_in1"][i] for i in range(N_IN1)]
                  + [io["w_out1"][i] for i in range(N_OUT1)] + [io["w_moe"][0, i] for i in range(RING)])

        def load_ahead(sp, first, last):
            for g in range(first + RING, last + RING):
                load_group(sp, g, stream[g])

        def piece(v, slot, n):
            return v[:, slot, n * D:(n + 1) * D]

        def tile_parts(g, n):
            return tuple(piece(v, g % 2, n).rearrange("p (k n) -> p k n", k=KT) for v in w_split)

        def tile_pair(g):
            return tuple(v[:, g % 2, 0:2 * D].rearrange("p (k m n) -> p k m n", k=KT, m=2) for v in w_split)

        def split_high(act, g, free=None):
            act.wait_ge(slot_loaded[g % RING], 16 * (g // RING + 1))
            if free:
                act.wait_ge(tile_done, free)
            for n in range(GROUP):
                high_part(piece(w_split[0], g % 2, n), piece(ring, g % RING, n)).then_inc(back_high if n == 2 else front_high, 1)

        def split_low(dve, g):
            for n in range(GROUP):
                if n < 2:
                    dve.wait_ge(front_high, 2 * g + n + 1)
                else:
                    dve.wait_ge(back_high, g + 1)
                last = low_part(piece(w_split[1], g % 2, n), piece(ring, g % RING, n), piece(w_split[0], g % 2, n))
                if n:
                    last.then_inc(back_split if n == 2 else front_split, 1)

        def tile_ready(pe, g, n):
            pe.wait_ge(back_split if n == 2 else front_split, g + 1)

        def x_high(act, m, src, xn_count=None):
            for j in range(4):
                if xn_count is not None:
                    act.wait_ge(xn_ready, xn_count + 2 * j + 2)
                high_part(x_split[0][:, 2 * j:2 * j + 2], src[:, 2 * j:2 * j + 2]).then_inc(x_high_ready, 1)

        def x_low(dve, m, src):
            for j in range(4):
                dve.wait_ge(x_high_ready, 4 * m + j + 1)
                two_tiles = slice(2 * j, 2 * j + 2)
                low_part(x_split[1][:, two_tiles], src[:, two_tiles], x_split[0][:, two_tiles]).then_inc(x_split_ready, 1)

        def x_parts(k):
            return tuple(v[:, k] for v in x_split)

        def norm_squares(dve, n, squares):
            for j in range(4):
                nc.vector.tensor_tensor(squares[:, 2 * j:2 * j + 2], xT[:, 2 * j:2 * j + 2], xT[:, 2 * j:2 * j + 2], mul)\
                    .then_inc(squares_ready, 1)

        def norm_sum(pe, n, squares):
            for k in range(KT):
                if k % 2 == 0:
                    pe.wait_ge(squares_ready, 4 * n + k // 2 + 1)
                last = nc.tensor.matmul(ps[7][:, 0:S], cst("ones"), squares[:, k], start=(k == 0), stop=(k == KT - 1))
            last.then_inc(sum_ready, 1)

        def norm_rstd(act, n):
            act.wait_ge(sum_ready, n + 1)
            act_then(act, nc.scalar.activation(rstd[:, :], ps[7][:, 0:S], ACT.Ln, scale=1.0 / D, bias=par("eps")))
            nc.scalar.activation(rstd[:, :], rstd[:, :], ACT.Exp, scale=-0.5).then_inc(rstd_ready, 1)

        def norm_scale(dve, n, gain):
            dve.wait_ge(rstd_ready, n + 1)
            for k in range(KT):
                nc.vector.scalar_tensor_tensor(xn[:, k], xT[:, k], par(gain, k), rstd[:, :], mul, mul).then_inc(xn_ready, 1)

        x_tok = area(0, TT, D)
        squares0 = area(2048, KT, S)
        proj = area(0, 14, S + 2)
        qk = area(3616, 5, S)
        v_tok = area(28672, TT, P)
        shift_sum = area(5152, 2, S)
        r_in, k_in, v_in = area(TEMP_, RT, S), area(TEMP_ + 1024, RT, S), area(V_, RT, S)
        low = area(TEMP_ + 2048, S)
        gate_low = area(TEMP_ + 2304, S)
        shifted = [r_in[:, i] for i in range(4)] + [k_in[:, i] for i in range(4)] + [v_in[:, i] for i in range(4)] + [low, gate_low]
        x_transposed, xT_ready, proj_copied = (sem(n) for n in ("x_transposed", "xT_ready", "proj_copied"))

        with nc.Block(no_gpsimd_drain=True) as block:
            @block.sync
            def _(sp):
                for t in range(TT):
                    sp.dma_start(x_tok[:, t], io["x"][t * P:(t + 1) * P, :]).then_inc(x_loaded, 16)
                sp.dma_start(const[:, :], io["const"]).then_inc(consts_loaded, 16)
                sp.dma_start(param[:, :], io["param"]).then_inc(consts_loaded, 16)
                sp.dma_start(small[:, :], io["small"]).then_inc(consts_loaded, 16)
                for g in range(RING):
                    load_group(sp, g, stream[g])
                load_ahead(sp, G_IN0, G_IN0 + N_IN0 - 1)

            @block.tensor
            def _(pe):
                pe.wait_ge(consts_loaded, 48)
                pe.wait_ge(x_loaded, 32)
                for k in range(KT):
                    for t in range(TT):
                        last = nc.tensor.transpose(ps[k // 2][:, (k % 2) * S + t * P:(k % 2) * S + (t + 1) * P],
                                                   x_tok[:, t, k * P:(k + 1) * P], ident)
                    if k % 2:
                        last.then_inc(x_transposed, 1)
                norm_sum(pe, 0, squares0)
                for i in range(20):
                    j, g, n = i // 2, i // GROUP, i % GROUP
                    if j >= 4 and i % 2 == 0:
                        pe.wait_ge(proj_copied, j - 3)
                    out = ps[j % 4][:, (i % 2) * S:(i % 2 + 1) * S]
                    if n != 1:
                        tile_ready(pe, g, n)
                    if i < 19:
                        w = tile_parts(g, n)
                        for k in range(KT):
                            if i == 0 and k % 2 == 0:
                                pe.wait_ge(x_split_ready, k // 2 + 1)
                            last = split_product(out, (w[0][:, k], w[1][:, k]), x_parts(k), k == 0, k == KT - 1)
                    else:
                        w = piece(ring, g % RING, n).rearrange("p (k n) -> p k n", k=KT)
                        for t in range(TT):
                            for k in range(KT):
                                last = nc.tensor.matmul(out[:, t * P:(t + 1) * P], xn[:, k, t * P:(t + 1) * P], w[:, k],
                                                        start=(k == 0), stop=(k == KT - 1))
                    last.then_inc(tile_done, 1)

            @block.scalar
            def _(act):
                act.wait_ge(consts_loaded, 48)
                norm_rstd(act, 0)
                split_high(act, 0)
                x_high(act, 0, xn, 0)
                split_high(act, 1)
                for j in range(10):
                    g = (2 * j + 1) // GROUP + 2
                    if g < N_IN0 and g > (2 * j - 1) // GROUP + 2:
                        split_high(act, g, GROUP * (g - 1))
                    act.wait_ge(tile_done, 2 * j + 2)
                    if j < 7:
                        dst = proj[:, 2 * j:2 * j + 2, 1:S + 1]
                    elif j < 9:
                        dst = qk[:, 2 * (j - 7):2 * (j - 7) + 2]
                    else:
                        nc.scalar.activation(qk[:, 4], ps[j % 4][:, 0:S], ACT.Copy)
                        nc.scalar.activation(v_tok.rearrange("p t n -> p (t n)"), ps[j % 4][:, S:2 * S], ACT.Copy)
                        break
                    nc.scalar.activation(dst, two(j % 4), ACT.Copy).then_inc(proj_copied, 1)

            @block.vector
            def _(dve):
                dve.wait_ge(consts_loaded, 48)
                for j in range(4):
                    dve.wait_ge(x_transposed, j + 1)
                    nc.vector.tensor_copy(xT[:, 2 * j:2 * j + 2], two(j)).then_inc(xT_ready, 1)
                dve.wait_ge(xT_ready, 4)
                norm_squares(dve, 0, squares0)
                norm_scale(dve, 0, "e_norm1")
                split_low(dve, 0)
                x_low(dve, 0, xn)
                split_low(dve, 1)
                dve_then(dve, nc.vector.memset(proj[:, :, 0:1], 0.0))
                dve_then(dve, nc.vector.memset(proj[:, :, S + 1:S + 2], 0.0))
                for j in range(7):
                    g = (2 * j + 1) // GROUP + 2
                    if g < N_IN0 and g > (2 * j - 1) // GROUP + 2:
                        split_low(dve, g)
                    dve.wait_ge(proj_copied, j + 1)
                    pair = proj[:, 2 * j:2 * j + 2]
                    dve_then(dve, nc.vector.tensor_tensor(shift_sum, pair[:, :, 0:S], pair[:, :, 2:S + 2], add))
                    dve_then(dve, nc.vector.scalar_tensor_tensor(shift_sum, shift_sum, 0.5, pair[:, :, 1:S + 1], mul, sub))
                    for i in range(2):
                        dve_then(dve, nc.vector.scalar_tensor_tensor(shifted[2 * j + i], shift_sum[:, i], par("mu", 2 * j + i),
                                                                     pair[:, i, 1:S + 1], mul, add))
        if stop <= 1:
            return


        sq_qk, rstd_qk, rope = area(22528, 5 * S), area(22528 + 5 * S, 5 * S), area(22528 + 10 * S, 5, S)
        probs, probs_t = area(26368, 2, 2, S), area(27392, 2, 2, S)
        stats = area(28416, 3, 16)
        yT = xn
        (qk_sq_ready, qk_sum_ready, qk_rstd_ready, qk_normed, rotated, rope_ready, scores_ready, max_ready, exp_ready,
         probs_ready, probs_turned, turned_copied, heads_ready, heads_copied) = (
            sem(n) for n in ("qk_sq_ready", "qk_sum_ready", "qk_rstd_ready", "qk_normed", "rotated", "rope_ready", "scores_ready",
                             "max_ready", "exp_ready", "probs_ready", "probs_turned", "turned_copied", "heads_ready", "heads_copied"))
        UNITS = 8
        QK_SPANS = [(0, 512), (512, 1024), (1024, 1280)]
        qk_flat, rope_flat = area(3616, 5 * S), area(22528 + 10 * S, 5 * S)


        A, R, B, K = (area(at, 2, RT, S) for at in (A_, R_, B_, K_))
        gate, bonus = area(GATE_, RT, S), area(BONUS_, RT, S)
        rate = area(TEMP_ + 3072, 2, RT, S)
        sig = area(TEMP_ + 5120, 2, RT, S)
        run = area(TEMP_ + 7168, 2, RT, S)
        kk = area(TEMP_ + 9216, RT, S)
        reset = area(TEMP_ + 10240, RT * S)
        cols = sb("cols", [P, 4, 2, RT, NCH])
        mid, tail = cols[:, 0], cols[:, 1]
        factor = cols[:, 2].rearrange("p d t c -> p (d t c)")[:, 0:24].rearrange("p (s d t) -> p s d t", s=3, d=2)
        one_less_ka = cols[:, 3, 0, 0]

        def flat(v):
            return v.rearrange("p a b -> p (a b)")

        def halves(v, n):
            return v[:, 2 * n:2 * n + 2]

        def chunks(v):
            return v.rearrange("p d t (c n) -> p (d t c) n", n=C)

        (low_ready, ranks_ready, sig_ready, kk_sq_ready, kk_sum_ready, kk_floor_ready, kk_scale_ready, gate_done, gate_copied,
         run_ready, scales_ready, bonus_in, bonus_sum) = (
            sem(n) for n in ("low_ready", "ranks_ready", "sig_ready", "kk_sq_ready", "kk_sum_ready", "kk_floor_ready",
                             "kk_scale_ready", "gate_done", "gate_copied", "run_ready", "scales_ready", "bonus_in", "bonus_sum"))
        kk_sq, kk_scale = run[:, 0], run[:, 1]

        with nc.Block(no_gpsimd_drain=True) as block:
            @block.vector
            def _(dve):
                nc.vector.tensor_tensor(sq_qk, qk_flat, qk_flat, mul).then_inc(qk_sq_ready, 1)
                for i in range(RT):
                    dve_then(dve, nc.vector.tensor_scalar(kk[:, i], k_in[:, i], par("k_k", i), None, mul))
                nc.vector.tensor_tensor(flat(kk_sq), flat(kk), flat(kk), mul).then_inc(kk_sq_ready, 1)
                dve.wait_ge(qk_rstd_ready, 3)
                for i in range(5):
                    nc.vector.scalar_tensor_tensor(qk[:, i], qk[:, i], par("q_norm" if i < 4 else "k_norm"),
                                                   rstd_qk[:, i * S:(i + 1) * S], mul, mul).then_inc(qk_normed, 1)
                dve.wait_ge(qk_normed, 5)
                dve_then(dve, nc.vector.tensor_tensor(rope, qk, cst("cos").unsqueeze(1).to_broadcast([P, 5, S]), mul))
                for n, (a, b) in enumerate(QK_SPANS):
                    dve.wait_ge(rotated, n + 1)
                    w = (b - a) // S
                    dve_then(dve, nc.vector.tensor_tensor(sq_qk[:, a:b].rearrange("p (a b) -> p a b", b=S),
                                                          ps[n][:, 0:b - a].rearrange("p (a b) -> p a b", b=S),
                                                          cst("sin").unsqueeze(1).to_broadcast([P, w, S]), mul))
                nc.vector.tensor_tensor(rope_flat, rope_flat, sq_qk, add).then_inc(rope_ready, 1)
                dve.wait_ge(kk_sum_ready, 1)
                for n in range(2):
                    last = nc.vector.tensor_scalar(halves(kk_scale, n), two(4 + n), 1e-24, None, ALU.max)
                last.then_inc(kk_floor_ready, 1)

                def maximum(u):
                    dve.wait_ge(scores_ready, u + 1)
                    dve_then(dve, nc.vector.tensor_reduce(stats[:, 0, 2 * u:2 * u + 2], two(u % 4), AX, ALU.max))
                    nc.vector.tensor_scalar(stats[:, 0, 2 * u:2 * u + 2], stats[:, 0, 2 * u:2 * u + 2], -HD ** -0.5, None, mul)\
                        .then_inc(max_ready, 1)

                def normalise(u):
                    dve.wait_ge(exp_ready, 2 * u + 2)
                    dve_then(dve, nc.vector.reciprocal(stats[:, 2, 2 * u:2 * u + 2], stats[:, 1, 2 * u:2 * u + 2]))
                    for q in range(2):
                        nc.vector.tensor_scalar(probs[:, u % 2, q], probs[:, u % 2, q], stats[:, 2, 2 * u + q:2 * u + q + 1], None, mul)\
                            .then_inc(probs_ready, 1)

                def attend(u):
                    if u < UNITS:
                        maximum(u)
                    if u >= 1:
                        normalise(u - 1)

                def keys(d):
                    for i in range(RT):
                        dve_then(dve, nc.vector.tensor_scalar(K[:, d, i], rate[:, d, i], par("k_a", i), one_less_ka[:, i:i + 1], mul, add))
                    dve_then(dve, nc.vector.tensor_tensor(flat(K[:, d]), flat(K[:, d]), flat(k_in), mul))

                a = PARAM["k_a"][0]
                dve_then(dve, nc.vector.tensor_scalar(one_less_ka, param[:, a:a + RT], -1.0, 1.0, mul, add))
                attend(0)
                dve_then(dve, nc.vector.tensor_copy(reset.rearrange("p (a b) -> p a b", b=C),
                                                    cst("reset").unsqueeze(1).to_broadcast([P, RT * NCH, C])))
                dve.wait_ge(sig_ready, 16)
                keys(0)
                attend(1)
                keys(1)
                for i in range(RT):
                    nc.vector.scalar_tensor_tensor(bonus[:, i], r_in[:, i], par("r_k", i), K[:, 0, i], mul, mul).then_inc(bonus_in, 1)
                attend(2)
                dve.wait_ge(kk_scale_ready, 1)
                dve_then(dve, nc.vector.tensor_tensor(flat(kk), flat(kk), flat(kk_scale), mul))
                for d in range(2):
                    dve_then(dve, nc.vector.tensor_tensor_scan(flat(run[:, d]), reset, flat(sig[:, d]), 0.0, mul, add))
                attend(3)
                ends = run.rearrange("p d t (c n) -> p d t c n", n=C)
                dve_then(dve, nc.vector.tensor_copy(mid, ends[:, :, :, :, C // 2 - 1]))
                dve_then(dve, nc.vector.tensor_tensor(tail, ends[:, :, :, :, C - 1], mid, sub))
                for s in range(3):
                    dve_then(dve, nc.vector.tensor_tensor(factor[:, s, 0], tail[:, 0, :, s], mid[:, 0, :, s + 1], add))
                    dve_then(dve, nc.vector.tensor_tensor(factor[:, s, 1], mid[:, 1, :, 3 - s], tail[:, 1, :, 2 - s], add))
                attend(4)
                dve_then(dve, nc.vector.tensor_tensor(chunks(run), chunks(run),
                                                      mid.rearrange("p d t c -> p (d t c)").unsqueeze(2).to_broadcast([P, 32, C]), sub))
                attend(5)
                nc.vector.tensor_tensor(chunks(sig), chunks(run), chunks(sig), sub).then_inc(run_ready, 1)
                attend(6)
                for d in range(2):
                    dve_then(dve, nc.vector.tensor_tensor(flat(B[:, d]), flat(kk), flat(rate[:, d]), mul))
                attend(7)
                dve.wait_ge(scales_ready, 3)
                dve_then(dve, nc.vector.tensor_tensor(flat(R[:, 0]), flat(R[:, 0]), flat(r_in), mul))
                dve_then(dve, nc.vector.tensor_tensor(flat(R[:, 1]), flat(A[:, 1]), flat(r_in), mul))
                attend(8)
                for d in range(2):
                    dve_then(dve, nc.vector.scalar_tensor_tensor(flat(A[:, d]), flat(A[:, d]), -1.0, flat(kk), mul, mul))
                dve.wait_ge(scales_ready, 5)
                for d, scale in ((0, run[:, 0]), (1, sig[:, 1])):
                    dve_then(dve, nc.vector.tensor_tensor(flat(B[:, d]), flat(B[:, d]), flat(scale), mul))
                    dve_then(dve, nc.vector.tensor_tensor(flat(K[:, d]), flat(K[:, d]), flat(scale), mul))
                for n in range(2):
                    dve.wait_ge(bonus_sum, n + 1)
                    dve_then(dve, nc.vector.tensor_tensor(halves(bonus, n), two(4 + n), halves(v_in, n), mul))

            @block.scalar
            def _(act):
                nc.scalar.activation(low[0:64, :], low[0:64, :], ACT.Tanh).then_inc(low_ready, 1)
                nc.scalar.activation(gate_low, gate_low, ACT.Sigmoid).then_inc(low_ready, 1)
                for n, (a, b) in enumerate(QK_SPANS):
                    act.wait_ge(qk_sum_ready, n + 1)
                    act_then(act, nc.scalar.activation(rstd_qk[:, a:b], ps[4 + n][:, 0:b - a], ACT.Ln, scale=1.0 / HD, bias=par("eps")))
                for n, (a, b) in enumerate(QK_SPANS):
                    nc.scalar.activation(rstd_qk[:, a:b], rstd_qk[:, a:b], ACT.Exp, scale=-0.5).then_inc(qk_rstd_ready, 1)
                act.wait_ge(ranks_ready, 1)
                for d in range(2):
                    for i in range(RT):
                        nc.scalar.activation(sig[:, d, i], ps[2 * d + i // 2][:, (i % 2) * S:(i % 2 + 1) * S], ACT.Sigmoid,
                                             bias=par("w0_b" if d else "w0_f", i)).then_inc(sig_ready, 1)
                act.wait_ge(ranks_ready, 2)
                for d in range(2):
                    for i in range(RT):
                        nc.scalar.activation(rate[:, d, i], ps[4 + 2 * d + i // 2][:, (i % 2) * S:(i % 2 + 1) * S], ACT.Sigmoid,
                                             bias=par("a0_b" if d else "a0_f", i)).then_inc(sig_ready, 1)
                act.wait_ge(gate_done, 1)
                for n in range(2):
                    nc.scalar.activation(halves(gate, n), two(6 + n), ACT.Copy).then_inc(gate_copied, 1)

                def exponentials(u):
                    act.wait_ge(max_ready, u + 1)
                    if u >= 2:
                        act.wait_ge(probs_turned, u - 1)
                    for q in range(2):
                        nc.scalar.activation(probs[:, u % 2, q], ps[u % 4][:, q * S:(q + 1) * S], ACT.Exp, scale=HD ** -0.5,
                                             bias=stats[:, 0, 2 * u + q:2 * u + q + 1],
                                             accum_out=stats[:, 1, 2 * u + q:2 * u + q + 1]).then_inc(exp_ready, 1)

                def copy_turned(u):
                    act.wait_ge(probs_turned, u + 1)
                    if u >= 2:
                        act.wait_ge(heads_ready, u - 1)
                    nc.scalar.activation(probs_t[:, u % 2], two(4 + u % 2), ACT.Copy).then_inc(turned_copied, 1)

                def copy_heads(i):
                    act.wait_ge(heads_ready, 2 * i + 2)
                    nc.scalar.activation(yT[:, 4 + i], ps[6 + i % 2][:, 0:S], ACT.Copy).then_inc(heads_copied, 1)

                for u in range(UNITS + 2):
                    if u < UNITS:
                        exponentials(u)
                    if 1 <= u <= UNITS:
                        copy_turned(u - 1)
                    if u >= 3 and u % 2:
                        copy_heads((u - 3) // 2)
                    if u == 0:
                        act.wait_ge(kk_floor_ready, 1)
                        act_then(act, nc.scalar.activation(flat(kk_scale), flat(kk_scale), ACT.Ln, scale=KK_SCALE))
                        nc.scalar.activation(flat(kk_scale), flat(kk_scale), ACT.Exp, scale=-0.5, bias=par("kk_bias")).then_inc(kk_scale_ready, 1)
                    if u == 6:
                        act.wait_ge(run_ready, 1)
                        for out, src, s in ((R[:, 0], run[:, 0], -DECAY_C), (A[:, 1], run[:, 1], DECAY_C), (A[:, 0], sig[:, 0], -DECAY_C)):
                            nc.scalar.activation(flat(out), flat(src), ACT.Exp, scale=s).then_inc(scales_ready, 1)
                    if u == 7:
                        act.wait_ge(scales_ready, 3)
                        nc.scalar.activation(flat(run[:, 0]), flat(run[:, 0]), ACT.Exp, scale=DECAY_C).then_inc(scales_ready, 1)
                        nc.scalar.activation(flat(sig[:, 1]), flat(sig[:, 1]), ACT.Exp, scale=-DECAY_C).then_inc(scales_ready, 1)
                        nc.scalar.activation(factor, factor, ACT.Exp, scale=-DECAY_C).then_inc(scales_ready, 1)

            @block.tensor
            def _(pe):
                def ranks(rows, bank):
                    for d in range(2):
                        up = sml("up_b" if d else "up_f")
                        for i in range(RT):
                            last = nc.tensor.matmul(ps[bank + 2 * d + i // 2][:, (i % 2) * S:(i % 2 + 1) * S], up[rows, i * P:(i + 1) * P],
                                                    low[rows, :], start=True, stop=True)
                    last.then_inc(ranks_ready, 1)

                pe.wait_ge(qk_sq_ready, 1)
                for n, (a, b) in enumerate(QK_SPANS):
                    nc.tensor.matmul(ps[4 + n][:, 0:b - a], cst("headsum"), sq_qk[:, a:b], start=True, stop=True).then_inc(qk_sum_ready, 1)
                pe.wait_ge(low_ready, 2)
                ranks(slice(0, 64), 0)
                pe.wait_ge(qk_rstd_ready, 1)
                ranks(slice(64, 128), 4)
                pe.wait_ge(sig_ready, 8)
                pe.wait_ge(qk_normed, 5)
                for n, (a, b) in enumerate(QK_SPANS):
                    nc.tensor.matmul(ps[n][:, 0:b - a], cst("rot"), qk_flat[:, a:b], start=True, stop=True).then_inc(rotated, 1)
                pe.wait_ge(sig_ready, 16)
                pe.wait_ge(kk_sq_ready, 1)
                for n in range(2):
                    last = nc.tensor.matmul(ps[4 + n][:, :], cst("headsum"), halves(kk_sq, n), start=True, stop=True)
                last.then_inc(kk_sum_ready, 1)
                for i in range(RT):
                    last = nc.tensor.matmul(ps[6 + i // 2][:, (i % 2) * S:(i % 2 + 1) * S], sml("g_up")[:, i * P:(i + 1) * P], gate_low,
                                            start=True, stop=True)
                last.then_inc(gate_done, 1)
                pe.wait_ge(rope_ready, 1)

                def scores(u):
                    i, h = u // 2, u % 2
                    if u >= 4:
                        pe.wait_ge(exp_ready, 2 * (u - 3))
                    for q in range(2):
                        last = nc.tensor.matmul(ps[u % 4][:, q * S:(q + 1) * S], rope[HD * h:HD * (h + 1), i, q * P:(q + 1) * P],
                                                rope[HD * h:HD * (h + 1), 4], start=True, stop=True)
                    last.then_inc(scores_ready, 1)

                def turn(u):
                    pe.wait_ge(probs_ready, 2 * u + 2)
                    if u >= 2:
                        pe.wait_ge(turned_copied, u - 1)
                    for q in range(2):
                        for t in range(TT):
                            last = nc.tensor.transpose(ps[4 + u % 2][:, t * S + q * P:t * S + (q + 1) * P],
                                                       probs[:, u % 2, q, t * P:(t + 1) * P], ident)
                    last.then_inc(probs_turned, 1)

                def weigh(u):
                    i, h = u // 2, u % 2
                    pe.wait_ge(turned_copied, u + 1)
                    if i >= 2 and h == 0:
                        pe.wait_ge(heads_copied, i - 1)
                    for t in range(TT):
                        last = nc.tensor.matmul(ps[6 + i % 2][HD * h:HD * (h + 1), 0:S], v_tok[:, t, HD * h:HD * (h + 1)],
                                                probs_t[:, u % 2, t], start=(t == 0), stop=(t == TT - 1))
                    last.then_inc(heads_ready, 1)

                for u in range(UNITS + 2):
                    if u < UNITS:
                        scores(u)
                    if u == 1:
                        pe.wait_ge(kk_floor_ready, 1)
                    if u == 2:
                        pe.wait_ge(gate_copied, 2)
                    if 1 <= u <= UNITS:
                        turn(u - 1)
                    if u >= 2:
                        weigh(u - 2)
                pe.wait_ge(turned_copied, UNITS)
                pe.wait_ge(bonus_in, 4)
                for n in range(2):
                    nc.tensor.matmul(ps[4 + n][:, :], cst("headsum"), halves(bonus, n), start=True, stop=True).then_inc(bonus_sum, 1)
        if stop <= 3:
            return

        def tile8(at):
            return area(at, 8, C)

        slots = []
        for q in range(2):
            at = TEMP_ + q * 9 * 512
            slots.append({n: tile8(at + 512 * j) for j, n in enumerate(("X", "XT", "MT", "AK", "RB", "RK", "Bt", "Kt", "Vt"))})
        state = [tile8(TEMP_ + 9216), tile8(TEMP_ + 9728)]
        W, U = tile8(TEMP_ + 10240), tile8(TEMP_ + 10752)
        product = [W, U]
        yA = yT[:, 0:RT]
        SYSTEMS = [(d, t, h) for d in range(2) for t in range(RT) for h in range(2)]
        names = ("grams_ready", "grams_taken_dve", "grams_taken_act", "w_ready", "w_copied", "u_ready", "u_copied", "y_ready",
                 "y_taken", "s_ready", "state_ready")
        (grams_ready, grams_taken_dve, grams_taken_act, w_ready, w_copied, u_ready, u_copied, y_ready, y_taken, s_ready,
         state_ready) = (sem(n) for n in names)
        inverse_ready = [sem(f"inverse_ready{q}") for q in range(2)]
        product_ready = [sem(f"product_ready{q}") for q in range(2)]
        product_masked = [sem(f"product_masked{q}") for q in range(2)]
        blocks_ready = [sem(f"blocks_ready{q}") for q in range(2)]

        def both(name):
            return cst(name).rearrange("p (d n) -> p d n", d=2).unsqueeze(2).to_broadcast([P, 2, RT, C])

        def dirs(v):
            return v.rearrange("p (d t) n -> p d t n", d=2)

        def bank8(b):
            return ps[b][:, :].rearrange("p (a n) -> p a n", n=C)

        eye = cst("ident64").unsqueeze(1).to_broadcast([P, 8, C])

        with nc.Block(no_gpsimd_drain=True) as block:
            @block.tensor
            def _(pe):
                def chunk(v, s, d, t, h):
                    c = s if d == 0 else NCH - 1 - s
                    return v[HD * h:HD * (h + 1), d, t, c * C:(c + 1) * C]

                def v_chunk(s, d, t, h):
                    c = s if d == 0 else NCH - 1 - s
                    return v_in[HD * h:HD * (h + 1), t, c * C:(c + 1) * C]

                def grams(s):
                    def product_of(bank, left, right):
                        for d, t, h in SYSTEMS:
                            last = nc.tensor.matmul(bank8(bank)[HD * h:HD * (h + 1), RT * d + t], left(d, t, h), right(d, t, h),
                                                    start=True, stop=True)
                        last.then_inc(grams_ready, 1)

                    a, r, b, k = (lambda d, t, h, v=v: chunk(v, s, d, t, h) for v in (A, R, B, K))
                    turn = lambda d, t, h: ident[HD * h:HD * (h + 1), HD * h:HD * (h + 1)]
                    v = lambda d, t, h: v_chunk(s, d, t, h)
                    steps = [(a, b, "dve", 1), (b, a, "act", 1), (k, a, "dve", 2), (b, r, "dve", 3), (k, r, "dve", 4),
                             (b, turn, "act", 2), (k, turn, "act", 3), (v, turn, "act", 4)]
                    for bank, (left, right, taker, n) in enumerate(steps):
                        if s % 2:
                            pe.wait_ge(grams_taken_dve if taker == "dve" else grams_taken_act, 4 * (s - 1) + n)
                        product_of(bank, left, right)

                def levels(s):
                    pe.wait_ge(grams_taken_dve, 4 * (s + 2))
                    pe.wait_ge(grams_taken_act, 4 * (s + 2))
                    for n in range(1, len(LEVELS)):
                        done = len(LEVELS) * (s // 2)
                        for q in range(2):
                            o = slots[q]
                            pe.wait_ge(inverse_ready[q], done + n)
                            for d, t, h in SYSTEMS:
                                p = slice(HD * h, HD * (h + 1))
                                last = nc.tensor.matmul(bank8(3 * q)[p, RT * d + t], o["MT"][p, RT * d + t], o["X"][p, RT * d + t],
                                                        start=True, stop=True)
                            last.then_inc(product_ready[q], 1)
                        for q in range(2):
                            o = slots[q]
                            pe.wait_ge(product_masked[q], (len(LEVELS) - 1) * (s // 2) + n)
                            for d, t, h in SYSTEMS:
                                p = slice(HD * h, HD * (h + 1))
                                last = nc.tensor.matmul(bank8(3 * q + 2)[p, RT * d + t], product[q][p, RT * d + t],
                                                        o["XT"][p, RT * d + t], start=True, stop=True)
                            if n < len(LEVELS) - 1:
                                for d, t, h in SYSTEMS:
                                    p = slice(HD * h, HD * (h + 1))
                                    last = nc.tensor.matmul(bank8(3 * q + 1)[p, RT * d + t], o["XT"][p, RT * d + t],
                                                            product[q][p, RT * d + t], start=True, stop=True)
                            last.then_inc(blocks_ready[q], 1)

                def recur(s):
                    o, now = slots[s % 2], state[s % 2]
                    pe.wait_ge(inverse_ready[s % 2], len(LEVELS) * (s // 2 + 1))
                    if s:
                        pe.wait_ge(state_ready, s)
                    for d, t, h in SYSTEMS:
                        p, j = slice(HD * h, HD * (h + 1)), RT * d + t
                        if s:
                            nc.tensor.matmul(bank8(6)[p, j], chunk(A, s, d, t, h), now[p, j], start=True, stop=False)
                        last = nc.tensor.matmul(bank8(6)[p, j], o["AK"][p, j], o["Vt"][p, j], start=(s == 0), stop=True)
                    last.then_inc(w_ready, 1)
                    pe.wait_ge(w_copied, s + 1)
                    for d, t, h in SYSTEMS:
                        p, j = slice(HD * h, HD * (h + 1)), RT * d + t
                        last = nc.tensor.matmul(bank8(7)[p, j], o["XT"][p, j], W[p, j], start=True, stop=True)
                    last.then_inc(u_ready, 1)
                    pe.wait_ge(u_copied, s + 1)
                    if s < NCH - 1:
                        for d, t, h in SYSTEMS:
                            p, j = slice(HD * h, HD * (h + 1)), RT * d + t
                            nc.tensor.matmul(bank8(1)[p, j], o["Bt"][p, j], U[p, j], start=True, stop=False)
                            last = nc.tensor.matmul(bank8(1)[p, j], o["Kt"][p, j], o["Vt"][p, j], start=False, stop=True)
                        last.then_inc(s_ready, 1)
                    if s:
                        pe.wait_ge(y_taken, s)
                    for d, t, h in SYSTEMS:
                        p, j = slice(HD * h, HD * (h + 1)), RT * d + t
                        if s:
                            nc.tensor.matmul(bank8(0)[p, j], now[p, j], chunk(R, s, d, t, h), start=True, stop=False)
                        nc.tensor.matmul(bank8(0)[p, j], U[p, j], o["RB"][p, j], start=(s == 0), stop=False)
                        last = nc.tensor.matmul(bank8(0)[p, j], o["Vt"][p, j], o["RK"][p, j], start=False, stop=True)
                    last.then_inc(y_ready, 1)

                for s in range(0, NCH, 2):
                    if s:
                        pe.wait_ge(y_taken, s)
                        pe.wait_ge(state_ready, s)
                    grams(s)
                    grams(s + 1)
                    levels(s)
                    recur(s)
                    recur(s + 1)

            @block.scalar
            def _(act):
                for s in range(0, NCH, 2):
                    for q in range(2):
                        o = slots[q]
                        for n, (name, bank) in enumerate((("MT", 1), ("Bt", 5), ("Kt", 6), ("Vt", 7))):
                            act.wait_ge(grams_ready, 8 * (s + q) + bank + 1)
                            nc.scalar.activation(o[name], bank8(bank), ACT.Copy).then_inc(grams_taken_act, 1)
                    for r in (s, s + 1):
                        act.wait_ge(w_ready, r + 1)
                        nc.scalar.activation(W, bank8(6), ACT.Copy).then_inc(w_copied, 1)
                        act.wait_ge(u_ready, r + 1)
                        nc.scalar.activation(U, bank8(7), ACT.Copy).then_inc(u_copied, 1)

            @block.vector
            def _(dve):
                def y_out(s):
                    dve.wait_ge(y_ready, s + 1)
                    for d, c in ((0, s), (1, NCH - 1 - s)):
                        out, src = yA[:, :, c * C:(c + 1) * C], bank8(0)[:, RT * d:RT * (d + 1)]
                        if s < 2:
                            last = nc.vector.tensor_copy(out, src)
                        else:
                            last = nc.vector.tensor_tensor(out, out, src, add)
                    last.then_inc(y_taken, 1)

                for s in range(0, NCH, 2):
                    for q in range(2):
                        o = slots[q]
                        base = 8 * (s + q)
                        dve.wait_ge(grams_ready, base + 1)
                        nc.vector.tensor_tensor(dirs(o["X"]), dirs(bank8(0)), both("level1"), mul).then_inc(grams_taken_dve, 1)
                        for n, (name, bank, mask) in enumerate((("AK", 2, "strict"), ("RB", 3, "read"), ("RK", 4, "read"))):
                            dve.wait_ge(grams_ready, base + bank + 1)
                            nc.vector.tensor_tensor(dirs(o[name]), dirs(bank8(bank)), both(mask), mul).then_inc(grams_taken_dve, 1)
                        dve.wait_ge(grams_taken_dve, 4 * (s + q + 1))
                        dve_then(dve, nc.vector.tensor_tensor(o["X"], o["X"], eye, add))
                        dve.wait_ge(grams_taken_act, 4 * (s + q) + 1)
                        dve_then(dve, nc.vector.tensor_tensor(dirs(o["XT"]), dirs(o["MT"]), both("level1_t"), mul))
                        nc.vector.tensor_tensor(o["XT"], o["XT"], eye, add).then_inc(inverse_ready[q], 1)
                    for n in range(1, len(LEVELS)):
                        done = (len(LEVELS) - 1) * (s // 2)
                        for q in range(2):
                            dve.wait_ge(product_ready[q], done + n)
                            nc.vector.tensor_tensor(dirs(product[q]), dirs(bank8(3 * q)), both(f"level{LEVELS[n]}"), mul)\
                                .then_inc(product_masked[q], 1)
                        for q in range(2):
                            o = slots[q]
                            dve.wait_ge(blocks_ready[q], done + n)
                            if n < len(LEVELS) - 1:
                                nc.vector.tensor_tensor(o["X"], o["X"], bank8(3 * q + 1), add)
                            nc.vector.tensor_tensor(o["XT"], o["XT"], bank8(3 * q + 2), add).then_inc(inverse_ready[q], 1)
                    for r in (s, s + 1):
                        if r < NCH - 1:
                            dve.wait_ge(s_ready, r + 1)
                            scale = factor[:, r].rearrange("p d t -> p (d t)").unsqueeze(2).to_broadcast([P, 8, C])
                            new = state[(r + 1) % 2]
                            if r == 0:
                                nc.vector.tensor_tensor(new, bank8(1), scale, mul).then_inc(state_ready, 1)
                            else:
                                dve_then(dve, nc.vector.tensor_tensor(new, bank8(1), state[r % 2], add))
                                nc.vector.tensor_tensor(new, new, scale, mul).then_inc(state_ready, 1)
                        y_out(r)
        if stop <= 4:
            return

        y_sq, y_rstd = area(A_, RT, S), area(R_, RT, S)
        (mean_ready, centred, var_ready, y_rstd_ready) = (sem(n) for n in ("mean_ready", "centred", "var_ready", "y_rstd_ready"))
        with nc.Block(no_gpsimd_drain=True) as block:
            @block.tensor
            def _(pe):
                for n in range(2):
                    nc.tensor.matmul(ps[n][:, :], cst("headsum"), halves(yA, n), start=True, stop=True).then_inc(mean_ready, 1)
                for n in range(2):
                    pe.wait_ge(centred, n + 1)
                    nc.tensor.matmul(ps[2 + n][:, :], cst("headsum"), halves(y_sq, n), start=True, stop=True).then_inc(var_ready, 1)

            @block.scalar
            def _(act):
                for n in range(2):
                    act.wait_ge(var_ready, n + 1)
                    act_then(act, nc.scalar.activation(halves(y_rstd, n), two(2 + n), ACT.Ln, scale=1.0 / HD, bias=par("gn_eps")))
                for n in range(2):
                    nc.scalar.activation(halves(y_rstd, n), halves(y_rstd, n), ACT.Exp, scale=-0.5).then_inc(y_rstd_ready, 1)

            @block.vector
            def _(dve):
                for n in range(2):
                    dve.wait_ge(mean_ready, n + 1)
                    dve_then(dve, nc.vector.scalar_tensor_tensor(halves(yA, n), two(n), -1.0 / HD, halves(yA, n), mul, add))
                    nc.vector.tensor_tensor(halves(y_sq, n), halves(yA, n), halves(yA, n), mul).then_inc(centred, 1)
                for n in range(2):
                    dve.wait_ge(y_rstd_ready, n + 1)
                    y = halves(yA, n)
                    dve_then(dve, nc.vector.tensor_tensor(y, y, halves(y_rstd, n), mul))
                    for i in (2 * n, 2 * n + 1):
                        dve_then(dve, nc.vector.tensor_scalar(yA[:, i], yA[:, i], par("gn_w", i), par("gn_b", i), mul, add))
                    dve_then(dve, nc.vector.tensor_tensor(y, y, halves(bonus, n), add))
                    dve_then(dve, nc.vector.tensor_tensor(y, y, halves(gate, n), mul))
        if stop <= 5:
            return

        out_added = sem("out_added")

        def project_out(pe, first_group, first_tile, m):
            for j in range(KT):
                g, n = first_group + j // GROUP, j % GROUP
                if n != 1:
                    tile_ready(pe, g, n)
                w = tile_parts(g, n)
                for k in range(KT):
                    if j == 0 and k % 2 == 0:
                        pe.wait_ge(x_split_ready, 4 * m + k // 2 + 1)
                    last = split_product(ps[j // 2][:, (j % 2) * S:(j % 2 + 1) * S], (w[0][:, k], w[1][:, k]), x_parts(k), k == 0, k == KT - 1)
                last.then_inc(tile_done, 1)

        def add_out(dve, use, first_tile, squares):
            for n in range(4):
                dve.wait_ge(tile_done, first_tile + 2 * n + 2)
                x = xT[:, 2 * n:2 * n + 2]
                nc.vector.tensor_tensor(x, x, two(n), add).then_inc(out_added, 1)
                dve.wait_ge(out_added, 8 * use + n + 1)
                nc.vector.tensor_tensor(squares[:, 2 * n:2 * n + 2], x, x, mul).then_inc(squares_ready, 1)

        PAIR_BANK = [4, 5, 6, 7]
        squares1 = area(0, KT, S)
        silu_f, hidden_f = area(2048, 2, S), area(2048 + 2 * S, 2, S)
        hidden_split = parts("hidden", (4096, 4096 + 2 * S), [2, S])
        (acc_zero, pair_done, silu_ready, product_done, hidden_high, hidden_ready, down_done) = (
            sem(n) for n in ("acc_zero", "pair_done", "silu_ready", "product_done", "hidden_high", "hidden_ready", "down_done"))

        with nc.Block(no_gpsimd_drain=True) as block:
            @block.sync
            def _(sp):
                load_ahead(sp, G_IN0 + N_IN0 - 1, G_FFN + FT)

            @block.tensor
            def _(pe):
                project_out(pe, G_OUT0, T_OUT0, 1)
                norm_sum(pe, 1, squares1)

                def pair(t, j):
                    w = tile_pair(G_FFN + j)
                    pe.wait_ge(front_split, t + (G_FFN + 1))
                    for m in range(2):
                        for k in range(KT):
                            last = split_product(ps[PAIR_BANK[j % 4]][:, m * S:(m + 1) * S], (w[0][:, k, m], w[1][:, k, m]), x_parts(k),
                                           k == 0, k == KT - 1)
                    last.then_inc(pair_done, 1)

                def down(t, j):
                    w = tile_parts(G_FFN + j, 2)
                    pe.wait_ge(back_split, t + (G_FFN + 1))
                    pe.wait_ge(hidden_ready, t + 1)
                    for k in range(KT):
                        last = split_product(ps[k // 2][:, (k % 2) * S:(k % 2 + 1) * S], (w[0][:, k], w[1][:, k]),
                                       (hidden_split[0][:, j % 2], hidden_split[1][:, j % 2]), False, False, skip_group_check=True)
                    last.then_inc(down_done, 1)

                pe.wait_ge(x_split_ready, 4 * 2 + 4)
                pair(0, 0)
                pe.wait_ge(acc_zero, 3)
                with pe.Fori(0, FT // 4) as i:
                    for j in range(4):
                        pair(i * 4 + (j + 1), j + 1)
                        down(i * 4 + j, j)
                pair(FT - 1, 1)
                down(FT - 2, 0)
                down(FT - 1, 1)

            @block.scalar
            def _(act):
                x_high(act, 1, yT)
                split_high(act, G_OUT0)
                split_high(act, G_OUT0 + 1)
                split_high(act, G_OUT0 + 2, T_OUT0 + 3)

                def pair_high(j, i=0):
                    g = G_FFN + j
                    act.wait_ge(slot_loaded[g % RING], i * 16 + 16 * (g // RING + 1))
                    for n in range(2):
                        high_part(piece(w_split[0], g % 2, n), piece(ring, g % RING, n)).then_inc(front_high, 1)

                def down_high(j):
                    g = G_FFN + j
                    high_part(piece(w_split[0], g % 2, 2), piece(ring, g % RING, 2)).then_inc(back_high, 1)

                def hidden(t, j):
                    act.wait_ge(pair_done, t + 1)
                    nc.scalar.activation(silu_f[:, j % 2], ps[PAIR_BANK[j % 4]][:, 0:S], ACT.Silu).then_inc(silu_ready, 1)
                    act.wait_ge(product_done, t + 1)
                    high_part(hidden_split[0][:, j % 2], hidden_f[:, j % 2]).then_inc(hidden_high, 1)

                act.wait_ge(tile_done, T_OUT0 + 2 * GROUP)
                pair_high(0)
                down_high(0)
                act.wait_ge(tile_done, T_OUT0 + KT)
                pair_high(1)
                norm_rstd(act, 1)
                x_high(act, 2, xn, KT)
                act.wait_ge(back_split, G_FFN)
                with act.Fori(0, FT // 4) as i:
                    for j in range(4):
                        t = i * 4 + j
                        hidden(t, j)
                        pair_high(j + 2, i)
                        act.wait_ge(down_done, t + 1)
                        down_high(j + 1)
                hidden(FT - 2, 0)
                act.wait_ge(down_done, FT - 1)
                down_high(1)
                hidden(FT - 1, 1)

            @block.vector
            def _(dve):
                x_low(dve, 1, yT)
                for n in range(N_OUT0):
                    split_low(dve, G_OUT0 + n)
                add_out(dve, 0, T_OUT0, squares1)

                def pair_low(t, j):
                    g = G_FFN + j
                    for n in range(2):
                        dve.wait_ge(front_high, t * 2 + (2 * G_FFN + n + 1))
                        last = low_part(piece(w_split[1], g % 2, n), piece(ring, g % RING, n), piece(w_split[0], g % 2, n))
                    last.then_inc(front_split, 1)

                def down_low(t, j):
                    g = G_FFN + j
                    dve.wait_ge(back_high, t + (G_FFN + 1))
                    low_part(piece(w_split[1], g % 2, 2), piece(ring, g % RING, 2), piece(w_split[0], g % 2, 2)).then_inc(back_split, 1)

                def hidden(t, j):
                    dve.wait_ge(silu_ready, t + 1)
                    nc.vector.tensor_tensor(hidden_f[:, j % 2], silu_f[:, j % 2], ps[PAIR_BANK[j % 4]][:, S:2 * S], mul)                        .then_inc(product_done, 1)
                    dve.wait_ge(hidden_high, t + 1)
                    low_part(hidden_split[1][:, j % 2], hidden_f[:, j % 2], hidden_split[0][:, j % 2]).then_inc(hidden_ready, 1)

                pair_low(0, 0)
                norm_scale(dve, 1, "e_norm2")
                x_low(dve, 2, xn)
                down_low(0, 0)
                pair_low(1, 1)
                dve.wait_ge(out_added, 4)
                for n in range(4):
                    nc.vector.memset(ps[n][:, :], 0.0).then_inc(acc_zero if n else down_done, 1)
                with dve.Fori(0, FT // 4) as i:
                    for j in range(4):
                        t = i * 4 + j
                        hidden(t, j)
                        pair_low(t + 2, j + 2)
                        down_low(t + 1, j + 1)
                hidden(FT - 2, 0)
                down_low(FT - 1, 1)
                hidden(FT - 1, 1)
                dve.wait_ge(down_done, FT + 1)
                for n in range(4):
                    x = xT[:, 2 * n:2 * n + 2]
                    nc.vector.tensor_tensor(x, x, two(n), add).then_inc(out_added, 1)
        if stop <= 6:
            return

        q1, k1 = area(0, GH, S), area(1024, GH, S)
        v1 = area(2048, TT, D)
        swish = area(4096, KT, S)
        G = area(6144, 2, GH, S)
        run1 = area(8192, 2, GH, S)
        squares2 = area(10240, KT, S)
        reset1, low1 = area(12288, GH * S), area(13312, S)
        gate_up = small[0:GRANK, 0:2 * RW]
        (gates_loaded, low1_ready, proj1_copied, low1_copied, z_ready, z_copied) = (
            sem(n) for n in ("gates_loaded", "low1_ready", "proj1_copied", "low1_copied", "z_ready", "z_copied"))

        Q1, K1 = area(10240, 2, GH, S), area(12288, 2, GH, S)
        G8, run8 = area(6144, 2 * GH * S), area(8192, 2 * GH * S)
        GS = 1.0 / 16
        abs_ready, log_ready, run1_ready, scales1_ready, qk1_ready = (
            sem(n) for n in ("abs_ready", "log_ready", "run1_ready", "scales1_ready", "qk1_ready"))
        fills = []
        for i in range(4):
            fills += [("v", 3 * i, i), ("q", 3 * i + 2, i)]
        fills += [("k", 12 + 2 * i, i) for i in range(2)] + [("gate", 16 + 2 * i, i) for i in range(4)]

        with nc.Block(no_gpsimd_drain=True) as block:
            @block.sync
            def _(sp):
                sp.dma_start(gate_up, io["gate_up"]).then_inc(gates_loaded, 16)
                load_ahead(sp, G_FFN + FT, G_OUT1)

            @block.tensor
            def _(pe):
                norm_sum(pe, 2, squares2)
                pe.wait_ge(xn_ready, 3 * KT)
                for k in range(KT):
                    last = nc.tensor.matmul(ps[4][0:GRANK, 0:S], sml("w_gd")[:, k * GRANK:(k + 1) * GRANK], xn[:, k],
                                            start=(k == 0), stop=(k == KT - 1))
                last.then_inc(low1_ready, 1)
                for j, (kind, first, _) in enumerate(fills):
                    if j >= 4:
                        pe.wait_ge(proj1_copied, j - 3)
                    if kind == "v":
                        g = G_IN1 + first // GROUP
                        tile_ready(pe, g, 1)
                        w = tuple(v[:, g % 2, 0:2 * D].rearrange("p (i k n) -> p k i n", i=2, k=KT) for v in w_split)
                        if j == 0:
                            pe.wait_ge(x_split_ready, 4 * 3 + 4)
                        for t in range(TT):
                            for k in range(KT):
                                tokens = tuple(v[:, k, t * P:(t + 1) * P] for v in x_split)
                                last = split_product(ps[j % 4][:, t * S:(t + 1) * S], tokens, (w[0][:, k], w[1][:, k]), k == 0, k == KT - 1)
                            last.then_inc(tile_done, 1)
                    else:
                        for i in range(first, first + (1 if kind == "q" else 2)):
                            g, n = G_IN1 + i // GROUP, i % GROUP
                            tile_ready(pe, g, n)
                            w = tile_parts(g, n)
                            for k in range(KT):
                                last = split_product(ps[j % 4][:, (i - first) * S:(i - first + 1) * S], (w[0][:, k], w[1][:, k]), x_parts(k),
                                               k == 0, k == KT - 1)
                            last.then_inc(tile_done, 1)
                    if 1 <= j <= 4:
                        pe.wait_ge(low1_copied, 1)
                        pe.wait_ge(gates_loaded, 16)
                        if j >= 3:
                            pe.wait_ge(z_copied, 2 * (j - 2))
                        d, n = (j - 1) // 2, (j - 1) % 2
                        for h in (2 * n, 2 * n + 1):
                            last = nc.tensor.matmul(ps[5 + n][:, (h % 2) * S:(h % 2 + 1) * S],
                                                    gate_up[:, d * RW + h * P:d * RW + (h + 1) * P], low1[0:GRANK, :], start=True, stop=True)
                        last.then_inc(z_ready, 1)

            @block.scalar
            def _(act):
                split_high(act, G_IN1)
                norm_rstd(act, 2)
                x_high(act, 3, xn, 2 * KT)
                split_high(act, G_IN1 + 1)
                act.wait_ge(low1_ready, 1)
                nc.scalar.activation(low1[0:GRANK, :], ps[4][0:GRANK, 0:S], ACT.Copy).then_inc(low1_copied, 1)

                def z_copy(m):
                    d, n = m // 2, m % 2
                    act.wait_ge(z_ready, m + 1)
                    for h in (2 * n, 2 * n + 1):
                        nc.scalar.activation(G[:, d, h], ps[5 + n][:, (h % 2) * S:(h % 2 + 1) * S], ACT.Identity,
                                             bias=par("bias_b" if d else "bias_f", h)).then_inc(z_copied, 1)

                split = 2
                for j, (kind, first, i) in enumerate(fills):
                    end = first + (1 if kind == "q" else 2)
                    if (end - 1) // GROUP + 2 == split < N_IN1:
                        split_high(act, G_IN1 + split, T_IN1 + GROUP * (split - 1))
                        split += 1
                    act.wait_ge(tile_done, T_IN1 + end)
                    func = ACT.Copy
                    if kind == "v":
                        dst, src = v1[:, :, i * S:(i + 1) * S], two(j % 4)
                    elif kind == "q":
                        dst, src = q1[:, i], ps[j % 4][:, 0:S]
                    elif kind == "k":
                        dst, src = k1[:, 2 * i:2 * i + 2], two(j % 4)
                    else:
                        dst, src, func = swish[:, 2 * i:2 * i + 2], two(j % 4), ACT.Silu
                    nc.scalar.activation(dst, src, func).then_inc(proj1_copied, 1)
                    if 1 <= j <= 4:
                        z_copy(j - 1)
                    if j == 6:
                        act.wait_ge(abs_ready, 1)
                        act_then(act, nc.scalar.activation(run8, run8, ACT.Exp))
                        nc.scalar.activation(run8, run8, ACT.Ln, bias=par("one")).then_inc(log_ready, 1)
                    if j == 9:
                        act.wait_ge(run1_ready, 3)
                        for out, src, s in ((Q1[:, 0], run1[:, 0], GS), (K1[:, 0], run1[:, 0], -GS), (Q1[:, 1], G[:, 1], -GS),
                                            (K1[:, 1], G[:, 1], GS)):
                            nc.scalar.activation(flat(out), flat(src), ACT.Exp, scale=s).then_inc(scales1_ready, 1)
                        nc.scalar.activation(factor, factor, ACT.Exp, scale=GS).then_inc(scales1_ready, 1)

            @block.vector
            def _(dve):
                dve.wait_ge(out_added, 8)
                norm_squares(dve, 2, squares2)
                split_low(dve, G_IN1)
                norm_scale(dve, 2, "o_norm1")
                x_low(dve, 3, xn)
                nc.vector.tensor_copy(reset1.rearrange("p (a b) -> p a b", b=C), cst("reset").unsqueeze(1).to_broadcast([P, GH * NCH, C]))
                for g in range(1, 5):
                    split_low(dve, G_IN1 + g)
                dve.wait_ge(z_copied, 8)
                dve_then(dve, nc.vector.tensor_scalar(run8, G8, -1.0, None, mul))
                nc.vector.tensor_tensor(run8, run8, G8, ALU.min).then_inc(abs_ready, 1)
                split_low(dve, G_IN1 + 5)
                dve.wait_ge(log_ready, 1)
                dve_then(dve, nc.vector.scalar_tensor_tensor(G8, G8, 0.0, run8, ALU.min, sub))
                for d in range(2):
                    dve_then(dve, nc.vector.tensor_tensor_scan(flat(run1[:, d]), reset1, flat(G[:, d]), 0.0, mul, add))
                split_low(dve, G_IN1 + 6)
                nc.vector.tensor_tensor(G8, run8, G8, sub).then_inc(run1_ready, 1)
                dve.wait_ge(run1_ready, 1)
                L = run1.rearrange("p d t (c n) -> p d t c n", n=C)
                X = G.rearrange("p d t (c n) -> p d t c n", n=C)
                dve_then(dve, nc.vector.tensor_copy(mid[:, 0], L[:, 0, :, :, C // 2]))
                dve_then(dve, nc.vector.tensor_copy(mid[:, 1], X[:, 1, :, :, C // 2 - 1]))
                dve_then(dve, nc.vector.tensor_tensor(tail, L[:, :, :, :, C - 1], mid, sub))
                for s in range(3):
                    dve_then(dve, nc.vector.tensor_tensor(factor[:, s, 0], tail[:, 0, :, s], mid[:, 0, :, s + 1], add))
                    dve_then(dve, nc.vector.tensor_tensor(factor[:, s, 1], mid[:, 1, :, 3 - s], tail[:, 1, :, 2 - s], add))
                for d, v in ((0, run1), (1, G)):
                    w = v[:, d].rearrange("p t (c n) -> p (t c) n", n=C)
                    nc.vector.tensor_tensor(w, w, mid[:, d].rearrange("p t c -> p (t c)").unsqueeze(2).to_broadcast([P, 16, C]), sub)\
                        .then_inc(run1_ready, 1)
                split_low(dve, G_IN1 + 7)
                dve.wait_ge(scales1_ready, 5)
                dve.wait_ge(proj1_copied, 10)
                for d in range(2):
                    dve_then(dve, nc.vector.scalar_tensor_tensor(flat(Q1[:, d]), flat(Q1[:, d]), P ** -0.5, flat(q1), mul, mul))
                    nc.vector.tensor_tensor(flat(K1[:, d]), flat(K1[:, d]), flat(k1), mul).then_inc(qk1_ready, 1)
        if stop <= 7:
            return

        states = area(14336, 3, 2, GH, 2 * P)
        K_tok = area(6144, TT, 2, GH, P)
        att = area(8192, TT, 2, GH, C)
        o_sq, o_rstd = area(0, KT, S), area(2048, GH, S)
        (k1_turned, k1_copied, att_ready, att_masked, add1_ready,
         states_ready, o_ready, o_copied, o_sq_ready, o_sum_ready, o_rstd_ready, mixed1) = (
            sem(n) for n in ("k1_turned", "k1_copied", "att_ready",
                             "att_masked", "add1_ready", "states_ready", "o_ready", "o_copied", "o_sq_ready", "o_sum_ready",
                             "o_rstd_ready", "mixed1"))

        with nc.Block(no_gpsimd_drain=True) as block:
            @block.vector
            def _(dve):
                dve_then(dve, nc.vector.memset(area(8192, 1024), 0.0))
                for t in range(TT):
                    dve.wait_ge(att_ready, t + 1)
                    for d in range(2):
                        last = nc.vector.copy_predicated(att[:, t, d], cst("read")[:, d * C:(d + 1) * C].bitcast(u32).unsqueeze(1).to_broadcast([P, GH, C]),
                                                         bank8(t)[:, GH * d:GH * (d + 1)])
                    last.then_inc(att_masked, 1)
                for s in range(3):
                    for n in range(4):
                        d, h = n // 2, 2 * (n % 2)
                        dve.wait_ge(add1_ready, 4 * s + n + 1)
                        new = states[:, s, d, h:h + 2]
                        scale = factor[:, s, d, h:h + 2].unsqueeze(2).to_broadcast([P, 2, 2 * P])
                        if s == 0:
                            nc.vector.tensor_tensor(new, two(4 + n), scale, mul).then_inc(states_ready, 1)
                        else:
                            dve_then(dve, nc.vector.tensor_tensor(new, two(4 + n), states[:, s - 1, d, h:h + 2], add))
                            nc.vector.tensor_tensor(new, new, scale, mul).then_inc(states_ready, 1)
                for n in range(4):
                    dve.wait_ge(o_copied, 4)
                    o = yT[:, 2 * n:2 * n + 2]
                    nc.vector.tensor_tensor(o_sq[:, 2 * n:2 * n + 2], o, o, mul).then_inc(o_sq_ready, 1)
                for h in range(GH):
                    dve.wait_ge(o_rstd_ready, h // 2 + 1)
                    for v in range(2):
                        dve_then(dve, nc.vector.scalar_tensor_tensor(yT[:, 2 * h + v], yT[:, 2 * h + v], par("out_norm", v), o_rstd[:, h], mul, mul))
                    o = yT[:, 2 * h:2 * h + 2]
                    nc.vector.tensor_tensor(o, o, swish[:, 2 * h:2 * h + 2], mul).then_inc(mixed1, 1)

            @block.scalar
            def _(act):
                for n in range(4):
                    act.wait_ge(k1_turned, n + 1)
                    nc.scalar.activation(K_tok[:, n // 2, n % 2], ps[2 + n][:, :].rearrange("p (h n) -> p h n", h=GH), ACT.Copy)\
                        .then_inc(k1_copied, 1)
                for n in range(4):
                    act.wait_ge(o_ready, n + 1)
                    dst = yT[:, 4 * (n % 2):4 * (n % 2) + 4].rearrange("p i (t b n) -> p i t b n", t=2, b=2)[:, :, :, n // 2]
                    nc.scalar.activation(dst, ps[n][:, :].rearrange("p (i t n) -> p i t n", i=4, t=2), ACT.Copy).then_inc(o_copied, 1)
                for n in range(2):
                    act.wait_ge(o_sum_ready, n + 1)
                    act_then(act, nc.scalar.activation(o_rstd[:, 2 * n:2 * n + 2], two(4 + n), ACT.Ln, scale=1.0 / (2 * P), bias=par("eps")))
                for n in range(2):
                    nc.scalar.activation(o_rstd[:, 2 * n:2 * n + 2], o_rstd[:, 2 * n:2 * n + 2], ACT.Exp, scale=-0.5).then_inc(o_rstd_ready, 1)

            @block.tensor
            def _(pe):
                pe.wait_ge(qk1_ready, 2)
                for t in range(TT):
                    for d in range(2):
                        for h in range(GH):
                            for b in range(2):
                                c = slice((2 * t + b) * C, (2 * t + b + 1) * C)
                                last = nc.tensor.matmul(bank8(t)[C * b:C * (b + 1), GH * d + h], K1[:, d, h, c], Q1[:, d, h, c], start=True, stop=True)
                    last.then_inc(att_ready, 1)
                for n in range(4):
                    for h in range(GH):
                        last = nc.tensor.transpose(ps[2 + n][:, h * P:(h + 1) * P], K1[:, n % 2, h, (n // 2) * P:(n // 2 + 1) * P], ident)
                    last.then_inc(k1_turned, 1)
                pe.wait_ge(k1_copied, 4)
                for s in range(3):
                    for n in range(4):
                        d = n // 2
                        c = s if d == 0 else NCH - 1 - s
                        rows = slice(C * (c % 2), C * (c % 2 + 1))
                        if s:
                            pe.wait_ge(states_ready, 4 * (s - 1) + n + 1)
                        for h in (2 * (n % 2), 2 * (n % 2) + 1):
                            last = nc.tensor.matmul(ps[4 + n][:, (h % 2) * S:(h % 2 + 1) * S], K_tok[rows, c // 2, d, h],
                                                    v1[rows, c // 2, h * 2 * P:(h + 1) * 2 * P], start=True, stop=True)
                        last.then_inc(add1_ready, 1)
                pe.wait_ge(att_masked, 2)
                pe.wait_ge(states_ready, 12)
                for n in range(4):
                    parity = n // 2
                    rows = slice(C * parity, C * (parity + 1))
                    for i in range(4 * (n % 2), 4 * (n % 2) + 4):
                        h, vt = i // 2, i % 2
                        for t in range(TT):
                            c = 2 * t + parity
                            out = ps[n][:, (i % 4) * P + t * C:(i % 4) * P + (t + 1) * C]
                            vs = slice(h * 2 * P + vt * P, h * 2 * P + (vt + 1) * P)
                            terms = [(v1[rows, t, vs], att[rows, t, d, h]) for d in range(2)]
                            if c:
                                terms.append((states[:, c - 1, 0, h, vt * P:(vt + 1) * P], Q1[:, 0, h, c * C:(c + 1) * C]))
                            if c < NCH - 1:
                                terms.append((states[:, NCH - 2 - c, 1, h, vt * P:(vt + 1) * P], Q1[:, 1, h, c * C:(c + 1) * C]))
                            for m, (left, right) in enumerate(terms):
                                last = nc.tensor.matmul(out, left, right, start=(m == 0), stop=(m == len(terms) - 1))
                    last.then_inc(o_ready, 1)
                for h in range(GH):
                    pe.wait_ge(o_sq_ready, h + 1)
                    for v in range(2):
                        last = nc.tensor.matmul(ps[4 + h // 2][:, (h % 2) * S:(h % 2 + 1) * S], cst("ones"), o_sq[:, 2 * h + v],
                                                start=(v == 0), stop=(v == 1))
                    if h % 2:
                        last.then_inc(o_sum_ready, 1)
        if stop <= 8:
            return

        w_moe = io["w_moe"].rearrange("e t p n -> (e t) p n")
        N_MOE = E * FET

        def load_front(sp, tile, g, split):
            sp.wait_ge(front_split, split)
            sp.dma_start(ring[:, g % RING, 0:2 * D], w_moe[bass.ds(tile, 1), :, 0:2 * D].rearrange("a p n -> (a p) n"))\
                .then_inc(slot_loaded[g % RING], 16)

        def load_back(sp, tile, g, split):
            sp.wait_ge(back_split, split)
            sp.dma_start(ring[:, g % RING, 2 * D:], w_moe[bass.ds(tile, 1), :, 2 * D:].rearrange("a p n -> (a p) n"))\
                .then_inc(back_loaded[g % RING], 16)

        def front_high_part(act, g, n, turns):
            if n == 0:
                act.wait_ge(slot_loaded[g % RING], (turns + (g // RING + 1)) * 16)
            high_part(piece(w_split[0], g % 2, n), piece(ring, g % RING, n)).then_inc(front_high, 1)

        def back_high_part(act, g, turns):
            act.wait_ge(back_loaded[g % RING], (turns + ((g - G_MOE) // RING + 1)) * 16)
            high_part(piece(w_split[0], g % 2, 2), piece(ring, g % RING, 2)).then_inc(back_high, 1)

        def front_low_part(dve, g, n, tiles):
            dve.wait_ge(front_high, tiles * 2 + (2 * g + n + 1))
            last = low_part(piece(w_split[1], g % 2, n), piece(ring, g % RING, n), piece(w_split[0], g % 2, n))
            if n:
                last.then_inc(front_split, 1)

        def back_low_part(dve, g, tiles):
            dve.wait_ge(back_high, tiles + (g + 1))
            low_part(piece(w_split[1], g % 2, 2), piece(ring, g % RING, 2), piece(w_split[0], g % 2, 2)).then_inc(back_split, 1)

        squares3 = area(0, KT, S)
        x_tok1 = area(0, TT, D)
        logits, top_idx_f = area(11264, TT, E), area(11280, TT, E)
        top = area(11296, TT, E)
        top_idx = sb("top_idx", [P, TT, E], u32)
        gap = area(11312, 4, TT)
        chosen, weight, hot = area(11328, TT, E), area(11344, TT, E), area(11360, 2, TT, E)
        rank, counts = area(11392, TT, E), area(11408, E)
        most = area(11416, 1)
        more = sb("more", [P, PASSES], i32)
        (logits_ready, turned1, tok1_copied, gap_ready, gap_exp, chosen_ready, ranks1_ready, routed) = (
            sem(n) for n in ("logits_ready", "turned1", "tok1_copied", "gap_ready", "gap_exp", "chosen_ready", "ranks1_ready", "routed"))

        with nc.Block(no_gpsimd_drain=True) as block:
            @block.sync
            def _(sp):
                load_ahead(sp, G_OUT1, G_MOE)
                load_front(sp, RING, G_MOE + RING, G_MOE + 1)
                load_front(sp, RING + 1, G_MOE + RING + 1, G_MOE + 2)
                load_back(sp, RING, G_MOE + RING, G_MOE + 1)

            @block.tensor
            def _(pe):
                project_out(pe, G_OUT1, T_OUT1, 4)
                norm_sum(pe, 3, squares3)
                for t in range(TT):
                    for k in range(KT):
                        pe.wait_ge(xn_ready, 3 * KT + k + 1)
                        last = nc.tensor.matmul(ps[4][:, t * E:(t + 1) * E], xn[:, k, t * P:(t + 1) * P], sml("router")[:, k * E:(k + 1) * E],
                                                start=(k == 0), stop=(k == KT - 1))
                last.then_inc(logits_ready, 1)
                for n in range(4):
                    for k in range(4 * (n % 2), 4 * (n % 2) + 4):
                        last = nc.tensor.transpose(ps[n][:, (k % 4) * P:(k % 4 + 1) * P], xn[:, k, (n // 2) * P:(n // 2 + 1) * P], ident)
                    last.then_inc(turned1, 1)
                pe.wait_ge(chosen_ready, 1)
                nc.tensor.matmul(ps[5][:, 0:E], cst("before"), chosen[:, 0], start=True, stop=True)
                nc.tensor.matmul(ps[5][:, E:2 * E], cst("ones"), chosen[:, 0], start=True, stop=False)
                nc.tensor.matmul(ps[5][:, E:2 * E], cst("before"), chosen[:, 1], start=False, stop=True)
                nc.tensor.matmul(ps[5][:, 2 * E:3 * E], cst("ones"), chosen[:, 0], start=True, stop=False)
                nc.tensor.matmul(ps[5][:, 2 * E:3 * E], cst("ones"), chosen[:, 1], start=False, stop=True).then_inc(ranks1_ready, 1)

            @block.scalar
            def _(act):
                x_high(act, 4, yT)
                split_high(act, G_OUT1)
                split_high(act, G_OUT1 + 1)
                split_high(act, G_OUT1 + 2, T_OUT1 + 3)
                act.wait_ge(tile_done, T_OUT1 + 2 * GROUP)
                for n in range(2):
                    front_high_part(act, G_MOE, n, 0)
                back_high_part(act, G_MOE, 0)
                norm_rstd(act, 3)
                for n in range(2):
                    front_high_part(act, G_MOE + 1, n, 0)
                act.wait_ge(gap_ready, 1)
                nc.scalar.activation(gap[:, 1], gap[:, 0], ACT.Exp).then_inc(gap_exp, 1)
                for n in range(4):
                    act.wait_ge(turned1, n + 1)
                    nc.scalar.activation(x_tok1[:, n // 2, (n % 2) * 512:(n % 2 + 1) * 512], ps[n][:, :], ACT.Copy).then_inc(tok1_copied, 1)

            @block.vector
            def _(dve):
                x_low(dve, 4, yT)
                for n in range(N_OUT1):
                    split_low(dve, G_OUT1 + n)
                add_out(dve, 1, T_OUT1, squares3)
                for n in range(2):
                    front_low_part(dve, G_MOE, n, 0)
                norm_scale(dve, 3, "o_norm2")
                back_low_part(dve, G_MOE, 0)
                for n in range(2):
                    front_low_part(dve, G_MOE + 1, n, 0)
                dve.wait_ge(logits_ready, 1)
                dve_then(dve, nc.vector.tensor_copy(logits.rearrange("p t e -> p (t e)"), ps[4][:, 0:TT * E]))
                for t in range(TT):
                    dve_then(dve, nc.vector.max(top[:, t], logits[:, t]))
                    dve_then(dve, nc.vector.max_index(top_idx[:, t], top[:, t], logits[:, t]))
                dve_then(dve, nc.vector.tensor_copy(top_idx_f, top_idx[:, :, :]))
                nc.vector.tensor_tensor(gap[:, 0], top[:, :, 1], top[:, :, 0], sub).then_inc(gap_ready, 1)
                for n in range(2):
                    for t in range(TT):
                        dve_then(dve, nc.vector.tensor_scalar(hot[:, n, t], cst("experts"), top_idx_f[:, t, n:n + 1], None, ALU.is_equal))
                nc.vector.tensor_tensor(chosen, hot[:, 0], hot[:, 1], add).then_inc(chosen_ready, 1)
                dve.wait_ge(gap_exp, 1)
                dve_then(dve, nc.vector.tensor_scalar(gap[:, 2], gap[:, 1], 1.0, None, add))
                dve_then(dve, nc.vector.reciprocal(gap[:, 2], gap[:, 2]))
                dve_then(dve, nc.vector.tensor_tensor(gap[:, 3], gap[:, 1], gap[:, 2], mul))
                for t in range(TT):
                    dve_then(dve, nc.vector.tensor_scalar(weight[:, t], hot[:, 0, t], gap[:, 2, t:t + 1], None, mul))
                    dve_then(dve, nc.vector.scalar_tensor_tensor(weight[:, t], hot[:, 1, t], gap[:, 3, t:t + 1], weight[:, t], mul, add))
                dve.wait_ge(ranks1_ready, 1)
                dve_then(dve, nc.vector.tensor_copy(rank.rearrange("p t e -> p (t e)"), ps[5][:, 0:2 * E]))
                dve_then(dve, nc.vector.tensor_copy(counts, ps[5][:, 2 * E:3 * E]))
                dve_then(dve, nc.vector.tensor_reduce(most, counts, AX, ALU.max))
                for p in range(PASSES):
                    last = nc.vector.tensor_scalar(more[:, p:p + 1], most, float(CAP * p), None, ALU.is_gt)
                last.then_inc(routed, 1)
        if stop <= 9:
            return

        place = area(2048, TT, E, CAP)
        placed_weight = area(3584, TT, E, CAP)
        back = area(5120, E, S)
        silu_e, hidden_e = area(7168, 2, P), area(7168 + 2 * P, 2, P)
        y_slot = area(7680, D)
        slots_split = parts("slots", (9216, 9216 + KT * CAP), [KT, CAP])
        turned_split = parts("turned", (9216 + 2 * KT * CAP, 9216 + (2 * KT + 2) * CAP), [2, CAP])
        place_flat, back_flat = area(2048, TT * E, CAP), area(5120, E * S)
        rank_p = area(11424, TT, E)
        (placed, back_turned, back_copied, gathered, slots_high, slots_ready, pair_e_done, silu_e_ready, hidden_e_ready, turned_e,
         turned_high, turned_ready, down_e_done, y_copied, acc_zeroed, scattered, x_added) = (
            sem(n) for n in ("placed", "back_turned", "back_copied", "gathered", "slots_high", "slots_ready", "pair_e_done",
                             "silu_e_ready", "hidden_e_ready", "turned_e", "turned_high", "turned_ready", "down_e_done", "y_copied",
                             "acc_zeroed", "scattered", "x_added"))
        TURNS = FET // RING - 1
        LEAD = 1
        SCATTER_BANK = [6, 7, 2, 3]

        class Pass:

            def __init__(self, p):
                self.p, self.tiles0, self.e0 = p, N_MOE * p, E * p
                self.g0 = G_MOE + self.tiles0

        def all_passes(eng, body):
            body(eng, Pass(0))
            for p in range(1, PASSES):
                with eng.If(eng.value_load(more[0:1, p:p + 1], min_val=0, max_val=1) > 0):
                    body(eng, Pass(p))

        def moe_loads(sp, at):
            def turn(i, j):
                load_front(sp, i * RING + (j + 1), at.g0 + j + 1, i * RING + (at.g0 + j - RING + 2))
                load_back(sp, i * RING + j, at.g0 + j, i * RING + (at.g0 + j - RING + 1))

            if at.p == 0:
                for j in range(1, RING):
                    turn(1, j)
            else:
                load_front(sp, 0, at.g0, at.g0 - RING + 1)
            with sp.Fori(2 if at.p == 0 else 0, N_MOE // RING - 1) as i:
                for j in range(RING):
                    turn(i, j)
            for j in range(RING - 1):
                turn(N_MOE // RING - 1, j)
            load_back(sp, N_MOE - 1, at.g0 + RING - 1, at.g0 + N_MOE - RING)

        def moe_products(pe, at):
            p, tiles0, e0, g0 = at.p, at.tiles0, at.e0, at.g0
            for n in range(4):
                pe.wait_ge(placed, TT * (p + 1))
                if p:
                    pe.wait_ge(x_added, 4 * e0 + LEAD)
                for e in (2 * n, 2 * n + 1):
                    for t in range(TT):
                        last = nc.tensor.transpose(ps[2 + n][0:CAP, (e % 2) * S + t * P:(e % 2) * S + (t + 1) * P],
                                                   placed_weight[:, t, e], ident)
                last.then_inc(back_turned, 1)
            pe.wait_ge(back_copied, 4 * (p + 1))

            def gather(e, n):
                for k in range(4 * n, 4 * n + 4):
                    for t in range(TT):
                        last = nc.tensor.matmul(ps[2 + n][:, (k % 4) * CAP:(k % 4 + 1) * CAP], x_tok1[:, t, k * P:(k + 1) * P],
                                                place_flat[:, bass.ds(e + t * E, 1)].rearrange("p a n -> p (a n)"),
                                                start=(t == 0), stop=(t == TT - 1))
                last.then_inc(gathered, 1)

            def pair_rows(t, rows):
                g = g0 + t
                w = tile_pair(g)
                for k in rows:
                    last = split_product(ps[4 + t % 2][0:CAP, 0:2 * P],  (slots_split[0][:, k], slots_split[1][:, k]),
                                   (w[0][:, k].rearrange("p m n -> p (m n)"), w[1][:, k].rearrange("p m n -> p (m n)")),
                                   k == 0, k == KT - 1)
                return last

            def pair(e, at_tile, t, turned=True):
                pe.wait_ge(front_split, e * FET + at_tile + (g0 + t + 1))
                pair_rows(t, range(3))
                if turned:
                    turn(e, at_tile, t - 1)
                pair_rows(t, range(3, KT)).then_inc(pair_e_done, 1)

            def turn(e, at_tile, t):
                pe.wait_ge(hidden_e_ready, e * FET + at_tile + (tiles0 + t + 1))
                nc.tensor.transpose(ps[6 + t % 2][:, 0:CAP], hidden_e[0:CAP, t % 2], ident[0:CAP, 0:CAP]).then_inc(turned_e, 1)

            def down(e, at_tile, t):
                w = [piece(v, (g0 + t) % 2, 2) for v in w_split]
                pe.wait_ge(back_split, e * FET + at_tile + (g0 + t + 1))
                pe.wait_ge(turned_ready, e * FET + at_tile + (tiles0 + t + 1))
                for n in range(2):
                    last = split_product(ps[n][0:CAP, :], (turned_split[0][:, t % 2], turned_split[1][:, t % 2]),
                                   (w[0][:, n * 512:(n + 1) * 512], w[1][:, n * 512:(n + 1) * 512]), False, False, skip_group_check=True)
                last.then_inc(down_e_done, 1)

            def scatter(e):
                pe.wait_ge(y_copied, e * 2 + (2 * e0 + 2))
                for r in range(4):
                    if r == 2:
                        pe.wait_ge(acc_zeroed, e + (e0 + 2))
                    for k in (2 * r, 2 * r + 1):
                        last = nc.tensor.matmul(ps[SCATTER_BANK[r]][:, (k % 2) * S:(k % 2 + 1) * S], y_slot[0:CAP, k * P:(k + 1) * P],
                                                back_flat[0:CAP, bass.ds(e * S, S)], start=True, stop=True)
                    last.then_inc(scattered, 1)

            def expert(e, last):
                with pe.Fori(0, TURNS) as i:
                    for t in range(RING):
                        pair(e, i * RING, t + 1)
                        down(e, i * RING, t)
                for t in range(FET - RING, FET - 1):
                    pair(e, 0, t + 1)
                    down(e, 0, t)
                if not last:
                    pe.wait_ge(x_added, e * 4 + (4 * e0 + LEAD))
                    gather(e + 1, 0)
                turn(e, 0, FET - 1)
                if not last:
                    gather(e + 1, 1)
                down(e, 0, FET - 1)
                if not last:
                    pe.wait_ge(slots_ready, e * 2 + (2 * e0 + 4))
                    pair(e + 1, 0, 0, turned=False)
                scatter(e)

            for n in range(2):
                gather(0, n)
            pe.wait_ge(slots_ready, 2 * e0 + 2)
            pe.wait_ge(acc_zeroed, e0 + 1)
            pair(0, 0, 0, turned=False)
            with pe.Fori(0, E - 1) as e:
                expert(e, False)
            expert(E - 1, True)

        def moe_activations(act, at):
            p, tiles0, e0, g0 = at.p, at.tiles0, at.e0, at.g0

            def gathered_high(e):
                for n in range(2):
                    act.wait_ge(gathered, e * 2 + (2 * e0 + n + 1))
                    high_part(slots_split[0][:, 4 * n:4 * n + 4], ps[2 + n][:, 0:4 * CAP].rearrange("p (a b) -> p a b", a=4))\
                        .then_inc(slots_high, 1)

            def step(e, i, t, front=True, back=True, gather=False):
                done = e * FET + i * RING + (tiles0 + t + 1)
                act.wait_ge(pair_e_done, done)
                nc.scalar.activation(silu_e[0:CAP, t % 2], ps[4 + t % 2][0:CAP, 0:P], ACT.Silu).then_inc(silu_e_ready, 1)
                turns = e * (FET // RING) + i
                if front:
                    front_high_part(act, g0 + t + 2, 0, turns)
                act.wait_ge(turned_e, done)
                high_part(turned_split[0][:, t % 2], ps[6 + t % 2][:, 0:CAP]).then_inc(turned_high, 1)
                if gather:
                    gathered_high(e + 1)
                if front:
                    front_high_part(act, g0 + t + 2, 1, turns)
                if back:
                    act.wait_ge(down_e_done, done)
                    back_high_part(act, g0 + t + 1, turns)

            def expert(e, last):
                with act.Fori(0, TURNS) as i:
                    for t in range(RING):
                        step(e, i, t)
                for t in range(RING):
                    end = t == RING - 1
                    step(e, TURNS, t, front=not (last and t >= RING - 2), back=not (last and end), gather=end and not last)
                act.wait_ge(down_e_done, e * FET + (tiles0 + FET + 1))
                nc.scalar.activation(y_slot[0:CAP, 512:1024], ps[1][0:CAP, :], ACT.Copy).then_inc(y_copied, 1)

            if p:
                act.wait_ge(down_e_done, tiles0 + 1)
                for n in range(2):
                    front_high_part(act, g0, n, 0)
                back_high_part(act, g0, 0)
                for n in range(2):
                    front_high_part(act, g0 + 1, n, 0)
            for n in range(4):
                act.wait_ge(back_turned, 4 * p + n + 1)
                nc.scalar.activation(back[0:CAP, 2 * n:2 * n + 2], ps[2 + n][0:CAP, :].rearrange("p (a b) -> p a b", a=2), ACT.Copy)\
                    .then_inc(back_copied, 1)
            gathered_high(0)
            with act.Fori(0, E - 1) as e:
                expert(e, False)
            expert(E - 1, True)

        def moe_elementwise(dve, at):
            p, tiles0, e0, g0 = at.p, at.tiles0, at.e0, at.g0
            dve_then(dve, nc.vector.tensor_scalar(rank_p, rank, float(CAP * p), None, sub))
            for t in range(TT):
                slots_b = cst("slots").unsqueeze(1).to_broadcast([P, E, CAP])
                dve_then(dve, nc.vector.tensor_tensor(place[:, t], slots_b, rank_p[:, t].unsqueeze(2).to_broadcast([P, E, CAP]), ALU.is_equal))
                dve_then(dve, nc.vector.tensor_tensor(place[:, t], place[:, t], chosen[:, t].unsqueeze(2).to_broadcast([P, E, CAP]), mul))
                nc.vector.tensor_tensor(placed_weight[:, t], place[:, t], weight[:, t].unsqueeze(2).to_broadcast([P, E, CAP]), mul)\
                    .then_inc(placed, 1)
            if p == 0:
                for n in range(2):
                    nc.vector.memset(ps[n][:, :], 0.0).then_inc(acc_zeroed if n else down_e_done, 1)
                for n in range(LEAD):
                    nc.vector.memset(area(11440 + n, 1), 0.0).then_inc(x_added, 1)

            def gathered_low(e):
                for n in range(2):
                    dve.wait_ge(slots_high, e * 2 + (2 * e0 + n + 1))
                    low_part(slots_split[1][:, 4 * n:4 * n + 4], ps[2 + n][:, 0:4 * CAP].rearrange("p (a b) -> p a b", a=4),
                             slots_split[0][:, 4 * n:4 * n + 4]).then_inc(slots_ready, 1)

            def step(e, at_tile, t, front=True, back=True, gather=False):
                count = e * FET + at_tile + (tiles0 + t + 1)
                dve.wait_ge(silu_e_ready, count)
                nc.vector.tensor_tensor(hidden_e[0:CAP, t % 2], silu_e[0:CAP, t % 2], ps[4 + t % 2][0:CAP, P:2 * P], mul)\
                    .then_inc(hidden_e_ready, 1)
                if front:
                    front_low_part(dve, g0 + t + 2, 0, e * FET + at_tile)
                dve.wait_ge(turned_high, count)
                low_part(turned_split[1][:, t % 2], ps[6 + t % 2][:, 0:CAP], turned_split[0][:, t % 2]).then_inc(turned_ready, 1)
                if gather:
                    gathered_low(e + 1)
                if front:
                    front_low_part(dve, g0 + t + 2, 1, e * FET + at_tile)
                if back:
                    back_low_part(dve, g0 + t + 1, e * FET + at_tile)

            def expert(e, last):
                with dve.Fori(0, TURNS) as i:
                    for t in range(RING):
                        step(e, i * RING, t)
                for t in range(RING):
                    end = t == RING - 1
                    step(e, TURNS * RING, t, front=not (last and t >= RING - 2), back=not (last and end), gather=end and not last)
                dve.wait_ge(down_e_done, e * FET + (tiles0 + FET + 1))
                nc.vector.tensor_copy(y_slot[0:CAP, 0:512], ps[0][0:CAP, :]).then_inc(y_copied, 1)
                dve.wait_ge(y_copied, e * 2 + (2 * e0 + 2))
                nc.vector.memset(ps[0][:, :], 0.0)
                nc.vector.memset(ps[1][:, :], 0.0).then_inc(acc_zeroed, 1)
                for r in range(4):
                    dve.wait_ge(scattered, e * 4 + (4 * e0 + r + 1))
                    x = xT[:, 2 * r:2 * r + 2]
                    nc.vector.tensor_tensor(x, x, two(SCATTER_BANK[r]), add).then_inc(x_added, 1)

            if p:
                for n in range(2):
                    front_low_part(dve, g0, n, 0)
                back_low_part(dve, g0, 0)
                for n in range(2):
                    front_low_part(dve, g0 + 1, n, 0)
            gathered_low(0)
            with dve.Fori(0, E - 1) as e:
                expert(e, False)
            expert(E - 1, True)

        with nc.Block(no_gpsimd_drain=True) as block:
            @block.sync
            def _(sp):
                all_passes(sp, moe_loads)

            @block.tensor
            def _(pe):
                all_passes(pe, moe_products)

            @block.scalar
            def _(act):
                all_passes(act, moe_activations)

            @block.vector
            def _(dve):
                all_passes(dve, moe_elementwise)

        if stop <= 10:
            return

        y_tok = area(0, TT, D)
        (result_turned, result_copied, stored) = (sem(n) for n in ("result_turned", "result_copied", "stored"))
        with nc.Block(no_gpsimd_drain=True) as block:
            @block.tensor
            def _(pe):
                for n in range(4):
                    for k in range(4 * (n % 2), 4 * (n % 2) + 4):
                        last = nc.tensor.transpose(ps[n][:, (k % 4) * P:(k % 4 + 1) * P], xT[:, k, (n // 2) * P:(n // 2 + 1) * P], ident)
                    last.then_inc(result_turned, 1)

            @block.vector
            def _(dve):
                for n in range(4):
                    dve.wait_ge(result_turned, n + 1)
                    nc.vector.tensor_copy(y_tok[:, n // 2, (n % 2) * 512:(n % 2 + 1) * 512], ps[n][:, :]).then_inc(result_copied, 1)

            @block.sync
            def _(sp):
                for t in range(TT):
                    sp.wait_ge(result_copied, 2 * (t + 1))
                    sp.dma_start(io["out"][t * P:(t + 1) * P, :], y_tok[:, t]).then_inc(stored, 16)
                sp.wait_ge(stored, 32)


def _const():
    out = np.zeros((P, N_CONST), np.float32)

    def put(name, v):
        a, b = CONST[name]
        out[:, a:b] = v

    p = np.arange(P)
    put("ident", np.eye(P))
    put("headsum", (p[:, None] // HD == p[None] // HD))
    put("ones", 1.0)
    rot = np.zeros((P, P))
    even = p[::2]
    rot[even + 1, even] = -1.0
    rot[even, even + 1] = 1.0
    put("rot", rot)
    put("before", p[:, None] < p[None])
    t = np.arange(S)
    freq = (np.float32(10000.0) ** (-np.arange(0, HD // 2, 2, dtype=np.float32) / np.float32(HD // 2))).astype(np.float32)
    row, col = (t // 64).astype(np.float32), (t % 64).astype(np.float32)
    ang = np.concatenate([row[:, None] * freq, col[:, None] * freq], -1)
    ang = ang[:, (p % HD) // 2].T.astype(np.float64)
    put("cos", np.cos(ang))
    put("sin", np.sin(ang))
    r, c = (p % C)[:, None], np.arange(C)[None]
    low, up = r > c, r < c
    for b in LEVELS:
        pair = (r // (2 * b) == c // (2 * b)) & (r // b != c // b)
        put(f"level{b}", np.concatenate([pair & low, pair & up], 1))
        if b == 1:
            put("level1_t", np.concatenate([pair & up, pair & low], 1))
    put("strict", np.concatenate([up, low], 1))
    put("read", np.concatenate([r <= c, low], 1))
    put("ident64", r == c)
    put("slots", np.arange(CAP)[None])
    put("experts", np.arange(E)[None])
    put("reset", (c > 0) * np.ones((P, 1)))
    return out


def _tiles(w, size=P):
    k, n = w.shape
    return np.ascontiguousarray(w.reshape(k // P, P, n // P, P).transpose(2, 1, 0, 3)).reshape(n // P, P, k)


def _groups(tiles):
    n = -(-len(tiles) // GROUP)
    out = np.zeros((n * GROUP,) + tiles.shape[1:], tiles.dtype)
    out[:len(tiles)] = tiles
    return np.ascontiguousarray(out.reshape(n, GROUP, P, D).transpose(0, 2, 1, 3)).reshape(n, P, GROUP * D)


def _hidden_groups(gate, up, down):
    n = gate.shape[1] // P
    pairs = np.stack([_tiles(gate).reshape(n, P, KT, P), _tiles(up).reshape(n, P, KT, P)], 3)
    return np.concatenate([pairs.reshape(n, P, 2 * D), down.reshape(n, P, D)], 2)


def _arrays(i):
    def col(v):
        return np.asarray(v).reshape(-1, P).T

    i = {k: np.asarray(v) for k, v in i.items()}
    param = np.zeros((P, N_PARAM), np.float32)

    def put(name, v):
        a, b = PARAM[name]
        param[:, a:b] = v

    for name, key in [("e_norm1", "e_norm1"), ("mu", "e_shift_mu"), ("w0_f", "e_w0_f"), ("w0_b", "e_w0_b"), ("a0_f", "e_a0_f"),
                      ("a0_b", "e_a0_b"), ("k_k", "e_k_k"), ("k_a", "e_k_a"), ("r_k", "e_r_k"), ("gn_w", "e_gn_w"), ("gn_b", "e_gn_b"),
                      ("e_norm2", "e_norm2"), ("o_norm1", "o_norm1"), ("bias_f", "o_gate_bias_f"), ("bias_b", "o_gate_bias_b"),
                      ("out_norm", "o_out_norm"), ("o_norm2", "o_norm2")]:
        put(name, col(i[key]))
    for name, key in [("q_norm", "e_q_norm"), ("k_norm", "e_k_norm")]:
        put(name, np.concatenate([i[key][0], i[key][0]])[:, None])
    put("eps", EPS)
    put("gn_eps", GN_EPS)
    put("kk_bias", 0.5 * np.log(KK_SCALE))
    put("one", 1.0)

    small = np.zeros((P, N_SMALL), np.float32)

    def puts(name, v):
        a, b = SMALL[name]
        small[:v.shape[0], a:b] = v

    puts("up_f", np.concatenate([i["e_w_up_f"][0], i["e_a_up_f"][0]]))
    puts("up_b", np.concatenate([i["e_w_up_b"][0], i["e_a_up_b"][0]]))
    puts("g_up", i["e_g_up"][0])
    puts("router", i["o_router"][0].reshape(KT, P, E).transpose(1, 0, 2).reshape(P, KT * E))
    w1 = i["o_w_in"][0]
    puts("w_gd", w1[:, 2048:2064].reshape(KT, P, GRANK).transpose(1, 0, 2).reshape(P, KT * GRANK))

    w0 = i["e_w_in"][0]
    q = w0[:, RW_IN:RW_IN + ATT].reshape(D, 2, 4, HD).transpose(0, 2, 1, 3).reshape(D, ATT)
    w0 = np.concatenate([w0[:, :RW_IN], q, w0[:, RW_IN + ATT:]], 1)
    wo0 = i["e_w_out"][0]
    att = wo0[RW:].reshape(2, 4, HD, D).transpose(1, 0, 2, 3).reshape(ATT, D)
    wo0 = np.concatenate([wo0[:RW], att], 0)
    w1 = np.concatenate([w1[:, :2048], w1[:, 2064:]], 1)
    t1 = _tiles(w1)
    order = [n for g in range(4) for n in (8 + 2 * g, 9 + 2 * g, g)] + list(range(4, 8)) + list(range(16, 24))
    moe = np.stack([_hidden_groups(i["o_exp_gate"][0, e], i["o_exp_up"][0, e], i["o_exp_down"][0, e]) for e in range(E)])
    return {"x": np.ascontiguousarray(i["x"][0]), "const": _const(), "param": param, "small": small,
            "gate_up": np.concatenate([i["o_gate_up_f"][0], i["o_gate_up_b"][0]], 1),
            "w_in0": _groups(_tiles(w0)), "w_out0": _groups(_tiles(wo0)),
            "w_ffn": _hidden_groups(i["e_ffn_gate"][0], i["e_ffn_up"][0], i["e_ffn_down"][0]),
            "w_in1": _groups(t1[order]), "w_out1": _groups(_tiles(i["o_w_out"][0])), "w_moe": moe}


def kernel(**inputs):
    import concourse.bacc as _bacc
    from concourse.bass_utils import run_bass_kernel_spmd as _run

    nc = _bacc.Bacc("TRN2", target_bir_lowering=False, num_devices=1)
    arrays = _arrays(inputs)
    io = {n: nc.dram_tensor(f"in_{n}", a.shape, mybir.dt.float32, kind="ExternalInput").ap() for n, a in arrays.items()}
    io["out"] = nc.dram_tensor("out_y", (S, D), mybir.dt.float32, kind="ExternalOutput").ap()
    program(nc, io)
    r = _run(nc, [{f"in_{n}": a for n, a in arrays.items()}], core_ids=[0])
    return np.asarray(r.results[0]["out_y"]).reshape(1, S, D)
```

```python
import concourse.bass as bass
from concourse import mybir
from contextlib import ExitStack
import numpy as np

D, S = 1024, 256
P = 128
KT = D // P
TT = S // P
HD = 64
RW = 512
RT = RW // P
C = 64
NCH = S // C
RW_IN = 3 * RW + 64 + 64 + 128
ATT = 512
FF = 2816
FT = FF // P
E = 8
FE = 3584
FET = FE // P
CAP = 96
PASSES = -(-S // CAP)
GH = 4
GRANK = 16
RING = 4
GROUP = 3
EPS = 1e-6
GN_EPS = 64e-5
DECAY_C = float(np.exp(-0.5))
KK_SCALE = float(2.0 ** 20)

G_IN0 = 0
N_IN0 = 7
G_OUT0 = G_IN0 + N_IN0
N_OUT0 = 3
G_FFN = G_OUT0 + N_OUT0
G_IN1 = G_FFN + FT
N_IN1 = 8
G_OUT1 = G_IN1 + N_IN1
N_OUT1 = 3
G_MOE = G_OUT1 + N_OUT1

LEVELS = [1, 2, 4, 8, 16, 32]


def layout(parts):
    at, out = 0, {}
    for name, n in parts:
        out[name] = (at, at + n)
        at += n
    return out, at


CONST, N_CONST = layout(
    [("ident", P), ("headsum", P), ("ones", P), ("rot", P), ("before", P), ("cos", S), ("sin", S)]
    + [(f"level{b}", 2 * C) for b in LEVELS]
    + [("level1_t", 2 * C), ("strict", 2 * C), ("read", 2 * C), ("ident64", C), ("slots", CAP), ("experts", E), ("reset", C)]
)
PARAM, N_PARAM = layout(
    [("e_norm1", KT), ("mu", 14), ("w0_f", RT), ("w0_b", RT), ("a0_f", RT), ("a0_b", RT), ("k_k", RT), ("k_a", RT),
     ("r_k", RT), ("gn_w", RT), ("gn_b", RT), ("q_norm", 1), ("k_norm", 1), ("e_norm2", KT), ("o_norm1", KT),
     ("bias_f", GH), ("bias_b", GH), ("out_norm", 2), ("o_norm2", KT), ("eps", 1), ("gn_eps", 1), ("kk_bias", 1), ("one", 1)]
)
SMALL, N_SMALL = layout(
    [("up_f", RW), ("up_b", RW), ("g_up", RW), ("router", KT * E), ("w_gd", KT * GRANK)]
)
A_, R_, B_, K_ = 0, 2048, 4096, 6144
V_, GATE_, BONUS_, TEMP_ = 8192, 9216, 10240, 11264
X_HI, X_LO = 15360, 17408
W_HI = 19456
W_LO = W_HI + 2 * GROUP * D
N_SCRATCH = W_LO + 2 * GROUP * D
TOP = 229344

T_IN0 = 0
T_OUT0 = T_IN0 + 20
T_IN1 = T_OUT0 + KT
T_OUT1 = T_IN1 + 24


def program(nc, io):
    f32, i32, u32, f32r = mybir.dt.float32, mybir.dt.int32, mybir.dt.uint32, mybir.dt.float32r
    ACT = mybir.ActivationFunctionType
    ALU = mybir.AluOpType
    AX = mybir.AxisListType.X
    mul, add, sub = ALU.mult, ALU.add, ALU.subtract
    ctx = ExitStack()

    def sb(name, shape, dt=f32):
        return ctx.enter_context(nc.sbuf_tensor(name, shape, dt))

    def sem(name):
        return ctx.enter_context(nc.semaphore(name))

    with ctx:
        ring = sb("ring", [P, RING, GROUP * D])
        xT = sb("xT", [P, KT, S])
        xn = sb("xn", [P, KT, S])
        const = sb("const", [P, N_CONST])
        param = sb("param", [P, N_PARAM])
        small = sb("small", [P, N_SMALL])
        rstd = sb("rstd", [P, S])
        scratch = nc.alloc_sbuf_tensor_at("scratch", [P, N_SCRATCH], f32, offset=TOP - 4 * N_SCRATCH)
        ps = [ctx.enter_context(nc.psum_tensor(f"bank{i}", [P, 512], f32)) for i in range(8)]

        def cst(name):
            a, b = CONST[name]
            return const[:, a:b]

        def par(name, i=0):
            a = PARAM[name][0] + i
            return param[:, a:a + 1]

        def sml(name):
            a, b = SMALL[name]
            return small[:, a:b]

        def area(at, *shape):
            n = int(np.prod(shape))
            v = scratch[:, at:at + n]
            if len(shape) == 1:
                return v
            names = "abcde"[:len(shape)]
            return v.rearrange(f"p ({' '.join(names)}) -> p {' '.join(names)}", **dict(zip(names, shape)))

        def two(b, n=2):
            return ps[b][:, :].rearrange("p (a b) -> p a b", a=n)

        def parts(name, at, shape):
            return tuple(nc.alloc_sbuf_tensor_at(f"{name}_{part}", [P] + shape, f32r, offset=TOP - 4 * (N_SCRATCH - a))
                         for part, a in zip(("high", "low"), at))

        x_split = parts("x", (X_HI, X_LO), [KT, S])
        w_split = parts("w", (W_HI, W_LO), [2, GROUP * D])

        def high_part(dst, src):
            return nc.scalar.activation(dst, src, ACT.Copy)

        def low_part(dst, src, high):
            return nc.vector.tensor_tensor(dst, src, high.bitcast(f32), sub)

        def split_product(out, left, right, start, stop, **flags):
            nc.tensor.matmul(out, left[0], right[0], start=start, stop=False, **flags)
            nc.tensor.matmul(out, left[0], right[1], start=False, stop=False, **flags)
            return nc.tensor.matmul(out, left[1], right[0], start=False, stop=stop, **flags)

        ident = cst("ident")

        consts_loaded, rest_loaded, x_loaded = sem("consts_loaded"), sem("rest_loaded"), sem("x_loaded")
        slot_loaded = [sem(f"slot_loaded{i}") for i in range(RING)]
        back_loaded = [sem(f"back_loaded{i}") for i in range(RING)]
        front_high, back_high, front_split, back_split = (sem(n) for n in ("front_high", "back_high", "front_split", "back_split"))
        tile_done = sem("tile_done")
        x_high_ready, x_split_ready = sem("x_high_ready"), sem("x_split_ready")
        dve_order, act_order = sem("dve_order"), sem("act_order")
        squares_ready, sum_ready, rstd_ready, xn_ready = (sem(n) for n in ("squares_ready", "sum_ready", "rstd_ready", "xn_ready"))

        dve_steps, act_steps = [0], [0]

        def dve_then(dve, instruction):
            instruction.then_inc(dve_order, 1)
            dve_steps[0] += 1
            dve.wait_ge(dve_order, dve_steps[0])

        def act_then(act, instruction):
            instruction.then_inc(act_order, 1)
            act_steps[0] += 1
            act.wait_ge(act_order, act_steps[0])

        def load_group(sp, g, src):
            if g >= RING:
                sp.wait_ge(back_split, g - RING + 1)
            if g < G_MOE:
                sp.dma_start(ring[:, g % RING], src).then_inc(slot_loaded[g % RING], 16)
            else:
                sp.dma_start(ring[:, g % RING, 0:2 * D], src[:, 0:2 * D]).then_inc(slot_loaded[g % RING], 16)
                sp.dma_start(ring[:, g % RING, 2 * D:], src[:, 2 * D:]).then_inc(back_loaded[g % RING], 16)

        stream = ([io["w_in0"][i] for i in range(N_IN0)] + [io["w_out0"][i] for i in range(N_OUT0)]
                  + [io["w_ffn"][i] for i in range(FT)] + [io["w_in1"][i] for i in range(N_IN1)]
                  + [io["w_out1"][i] for i in range(N_OUT1)] + [io["w_moe"][0, i] for i in range(RING)])

        def load_ahead(sp, first, last):
            for g in range(first + RING, last + RING):
                load_group(sp, g, stream[g])

        def piece(v, slot, n):
            return v[:, slot, n * D:(n + 1) * D]

        def tile_parts(g, n):
            return tuple(piece(v, g % 2, n).rearrange("p (k n) -> p k n", k=KT) for v in w_split)

        def tile_pair(g):
            return tuple(v[:, g % 2, 0:2 * D].rearrange("p (k m n) -> p k m n", k=KT, m=2) for v in w_split)

        def split_high(act, g, free=None):
            act.wait_ge(slot_loaded[g % RING], 16 * (g // RING + 1))
            if free:
                act.wait_ge(tile_done, free)
            for n in range(GROUP):
                high_part(piece(w_split[0], g % 2, n), piece(ring, g % RING, n)).then_inc(back_high if n == 2 else front_high, 1)

        def split_low(dve, g):
            for n in range(GROUP):
                if n < 2:
                    dve.wait_ge(front_high, 2 * g + n + 1)
                else:
                    dve.wait_ge(back_high, g + 1)
                last = low_part(piece(w_split[1], g % 2, n), piece(ring, g % RING, n), piece(w_split[0], g % 2, n))
                if n:
                    last.then_inc(back_split if n == 2 else front_split, 1)

        def tile_ready(pe, g, n):
            pe.wait_ge(back_split if n == 2 else front_split, g + 1)

        def x_high(act, src, pairs=range(4), ready=None):
            for j in pairs:
                if ready:
                    ready(j)
                high_part(x_split[0][:, 2 * j:2 * j + 2], src[:, 2 * j:2 * j + 2]).then_inc(x_high_ready, 1)

        def x_low(dve, m, src, pairs=range(4), before=0):
            for i, j in enumerate(pairs):
                dve.wait_ge(x_high_ready, 4 * m + before + i + 1)
                two_tiles = slice(2 * j, 2 * j + 2)
                low_part(x_split[1][:, two_tiles], src[:, two_tiles], x_split[0][:, two_tiles]).then_inc(x_split_ready, 1)

        def x_parts(k):
            return tuple(v[:, k] for v in x_split)

        def norm_squares(dve, n, squares):
            for j in range(4):
                nc.vector.tensor_tensor(squares[:, 2 * j:2 * j + 2], xT[:, 2 * j:2 * j + 2], xT[:, 2 * j:2 * j + 2], mul)\
                    .then_inc(squares_ready, 1)

        def norm_sum(pe, n, squares):
            for k in range(KT):
                if k % 2 == 0:
                    pe.wait_ge(squares_ready, 4 * n + k // 2 + 1)
                last = nc.tensor.matmul(ps[7][:, 0:S], cst("ones"), squares[:, k], start=(k == 0), stop=(k == KT - 1))
            last.then_inc(sum_ready, 1)

        def norm_rstd(act, n):
            act.wait_ge(sum_ready, n + 1)
            act_then(act, nc.scalar.activation(rstd[:, :], ps[7][:, 0:S], ACT.Ln, scale=1.0 / D, bias=par("eps")))
            nc.scalar.activation(rstd[:, :], rstd[:, :], ACT.Exp, scale=-0.5).then_inc(rstd_ready, 1)

        def norm_scale(dve, n, gain):
            dve.wait_ge(rstd_ready, n + 1)
            for k in range(KT):
                nc.vector.scalar_tensor_tensor(xn[:, k], xT[:, k], par(gain, k), rstd[:, :], mul, mul).then_inc(xn_ready, 1)

        def norm_scale_split(dve, n, gain, m):
            dve.wait_ge(rstd_ready, n + 1)
            for j in range(4):
                for k in (2 * j, 2 * j + 1):
                    nc.vector.scalar_tensor_tensor(xn[:, k], xT[:, k], par(gain, k), rstd[:, :], mul, mul).then_inc(xn_ready, 1)
                if j:
                    x_low(dve, m, xn, (j - 1,), j - 1)
            x_low(dve, m, xn, (3,), 3)

        def xn_pair(act, n):
            return lambda j: act.wait_ge(xn_ready, n * KT + 2 * j + 2)

        x_tok = area(0, TT, D)
        squares0 = area(2048, KT, S)
        proj = area(0, 14, S + 2)
        qk = area(3616, 5, S)
        v_tok = area(28672, TT, P)
        shift_sum = area(5152, 2, S)
        r_in, k_in, v_in = area(TEMP_, RT, S), area(TEMP_ + 1024, RT, S), area(V_, RT, S)
        low = area(TEMP_ + 2048, S)
        gate_low = area(TEMP_ + 2304, S)
        shifted = [r_in[:, i] for i in range(4)] + [k_in[:, i] for i in range(4)] + [v_in[:, i] for i in range(4)] + [low, gate_low]
        x_transposed, xT_ready, proj_copied = (sem(n) for n in ("x_transposed", "xT_ready", "proj_copied"))

        with nc.Block(no_gpsimd_drain=True) as block:
            @block.sync
            def _(sp):
                for t in range(TT):
                    sp.dma_start(x_tok[:, t], io["x"][t * P:(t + 1) * P, :]).then_inc(x_loaded, 16)
                first = CONST["cos"][0]
                sp.dma_start(const[:, 0:first], io["const"][:, 0:first]).then_inc(consts_loaded, 16)
                sp.dma_start(param[:, :], io["param"]).then_inc(consts_loaded, 16)
                for g in range(RING):
                    load_group(sp, g, stream[g])
                    if g == 1:
                        sp.dma_start(const[:, first:], io["const"][:, first:]).then_inc(rest_loaded, 16)
                        sp.dma_start(small[:, :], io["small"]).then_inc(rest_loaded, 16)
                load_ahead(sp, G_IN0, G_IN0 + N_IN0 - 1)

            @block.tensor
            def _(pe):
                pe.wait_ge(consts_loaded, 32)
                pe.wait_ge(x_loaded, 32)
                for k in range(KT):
                    for t in range(TT):
                        last = nc.tensor.transpose(ps[k // 2][:, (k % 2) * S + t * P:(k % 2) * S + (t + 1) * P],
                                                   x_tok[:, t, k * P:(k + 1) * P], ident)
                    if k % 2:
                        last.then_inc(x_transposed, 1)
                norm_sum(pe, 0, squares0)
                for i in range(20):
                    j, g, n = i // 2, i // GROUP, i % GROUP
                    if j >= 4 and i % 2 == 0:
                        pe.wait_ge(proj_copied, j - 3)
                    out = ps[j % 4][:, (i % 2) * S:(i % 2 + 1) * S]
                    if n != 1:
                        tile_ready(pe, g, n)
                    if i < 19:
                        w = tile_parts(g, n)
                        for k in range(KT):
                            if i == 0 and k % 2 == 0:
                                pe.wait_ge(x_split_ready, k // 2 + 1)
                            last = split_product(out, (w[0][:, k], w[1][:, k]), x_parts(k), k == 0, k == KT - 1)
                    else:
                        w = piece(ring, g % RING, n).rearrange("p (k n) -> p k n", k=KT)
                        for t in range(TT):
                            for k in range(KT):
                                last = nc.tensor.matmul(out[:, t * P:(t + 1) * P], xn[:, k, t * P:(t + 1) * P], w[:, k],
                                                        start=(k == 0), stop=(k == KT - 1))
                    last.then_inc(tile_done, 1)

            @block.scalar
            def _(act):
                act.wait_ge(consts_loaded, 32)
                split_high(act, 0)
                norm_rstd(act, 0)
                x_high(act, xn, ready=xn_pair(act, 0))
                split_high(act, 1)
                for j in range(10):
                    g = (2 * j + 1) // GROUP + 2
                    if g < N_IN0 and g > (2 * j - 1) // GROUP + 2:
                        split_high(act, g, GROUP * (g - 1))
                    act.wait_ge(tile_done, 2 * j + 2)
                    if j < 7:
                        dst = proj[:, 2 * j:2 * j + 2, 1:S + 1]
                    elif j < 9:
                        dst = qk[:, 2 * (j - 7):2 * (j - 7) + 2]
                    else:
                        nc.scalar.activation(qk[:, 4], ps[j % 4][:, 0:S], ACT.Copy)
                        nc.scalar.activation(v_tok.rearrange("p t n -> p (t n)"), ps[j % 4][:, S:2 * S], ACT.Copy)
                        break
                    nc.scalar.activation(dst, two(j % 4), ACT.Copy).then_inc(proj_copied, 1)

            @block.vector
            def _(dve):
                dve.wait_ge(consts_loaded, 32)
                for j in range(4):
                    dve.wait_ge(x_transposed, j + 1)
                    nc.vector.tensor_copy(xT[:, 2 * j:2 * j + 2], two(j)).then_inc(xT_ready, 1)
                dve.wait_ge(xT_ready, 4)
                norm_squares(dve, 0, squares0)
                split_low(dve, 0)
                norm_scale_split(dve, 0, "e_norm1", 0)
                split_low(dve, 1)
                dve_then(dve, nc.vector.memset(proj[:, :, 0:1], 0.0))
                dve_then(dve, nc.vector.memset(proj[:, :, S + 1:S + 2], 0.0))
                for j in range(7):
                    g = (2 * j + 1) // GROUP + 2
                    if g < N_IN0 and g > (2 * j - 1) // GROUP + 2:
                        split_low(dve, g)
                    dve.wait_ge(proj_copied, j + 1)
                    pair = proj[:, 2 * j:2 * j + 2]
                    dve_then(dve, nc.vector.tensor_tensor(shift_sum, pair[:, :, 0:S], pair[:, :, 2:S + 2], add))
                    dve_then(dve, nc.vector.scalar_tensor_tensor(shift_sum, shift_sum, 0.5, pair[:, :, 1:S + 1], mul, sub))
                    for i in range(2):
                        dve_then(dve, nc.vector.scalar_tensor_tensor(shifted[2 * j + i], shift_sum[:, i], par("mu", 2 * j + i),
                                                                     pair[:, i, 1:S + 1], mul, add))


        sq_qk, rstd_qk, rope = area(22528, 5 * S), area(22528 + 5 * S, 5 * S), area(22528 + 10 * S, 5, S)
        probs, probs_t = area(26368, 2, 2, S), area(27392, 2, 2, S)
        stats = area(28416, 3, 16)
        yT = xn
        (qk_sq_ready, qk_sum_ready, qk_rstd_ready, qk_normed, rotated, rope_ready, scores_ready, max_ready, exp_ready,
         probs_ready, probs_turned, turned_copied, heads_ready, heads_copied) = (
            sem(n) for n in ("qk_sq_ready", "qk_sum_ready", "qk_rstd_ready", "qk_normed", "rotated", "rope_ready", "scores_ready",
                             "max_ready", "exp_ready", "probs_ready", "probs_turned", "turned_copied", "heads_ready", "heads_copied"))
        UNITS = 8
        QK_SPANS = [(0, 512), (512, 1024), (1024, 1280)]
        qk_flat, rope_flat = area(3616, 5 * S), area(22528 + 10 * S, 5 * S)


        A, R, B, K = (area(at, 2, RT, S) for at in (A_, R_, B_, K_))
        gate, bonus = area(GATE_, RT, S), area(BONUS_, RT, S)
        rate = area(TEMP_ + 3072, 2, RT, S)
        sig = area(TEMP_ + 5120, 2, RT, S)
        run = area(TEMP_ + 7168, 2, RT, S)
        kk = area(TEMP_ + 9216, RT, S)
        reset = area(TEMP_ + 10240, RT * S)
        cols = sb("cols", [P, 4, 2, RT, NCH])
        mid, tail = cols[:, 0], cols[:, 1]
        factor = cols[:, 2].rearrange("p d t c -> p (d t c)")[:, 0:24].rearrange("p (s d t) -> p s d t", s=3, d=2)
        one_less_ka = cols[:, 3, 0, 0]

        def flat(v):
            return v.rearrange("p a b -> p (a b)")

        def halves(v, n):
            return v[:, 2 * n:2 * n + 2]

        def chunks(v):
            return v.rearrange("p d t (c n) -> p (d t c) n", n=C)

        (low_ready, ranks_ready, sig_ready, kk_sq_ready, kk_sum_ready, kk_floor_ready, kk_scale_ready, gate_done, gate_copied,
         run_ready, scales_ready, bonus_in, bonus_sum) = (
            sem(n) for n in ("low_ready", "ranks_ready", "sig_ready", "kk_sq_ready", "kk_sum_ready", "kk_floor_ready",
                             "kk_scale_ready", "gate_done", "gate_copied", "run_ready", "scales_ready", "bonus_in", "bonus_sum"))
        kk_sq, kk_scale = run[:, 0], run[:, 1]

        with nc.Block(no_gpsimd_drain=True) as block:
            @block.vector
            def _(dve):
                nc.vector.tensor_tensor(sq_qk, qk_flat, qk_flat, mul).then_inc(qk_sq_ready, 1)
                for i in range(RT):
                    dve_then(dve, nc.vector.tensor_scalar(kk[:, i], k_in[:, i], par("k_k", i), None, mul))
                nc.vector.tensor_tensor(flat(kk_sq), flat(kk), flat(kk), mul).then_inc(kk_sq_ready, 1)
                dve.wait_ge(qk_rstd_ready, 3)
                for i in range(5):
                    nc.vector.scalar_tensor_tensor(qk[:, i], qk[:, i], par("q_norm" if i < 4 else "k_norm"),
                                                   rstd_qk[:, i * S:(i + 1) * S], mul, mul).then_inc(qk_normed, 1)
                dve.wait_ge(qk_normed, 5)
                dve.wait_ge(rest_loaded, 32)
                dve_then(dve, nc.vector.tensor_tensor(rope, qk, cst("cos").unsqueeze(1).to_broadcast([P, 5, S]), mul))
                for n, (a, b) in enumerate(QK_SPANS):
                    dve.wait_ge(rotated, n + 1)
                    w = (b - a) // S
                    dve_then(dve, nc.vector.tensor_tensor(sq_qk[:, a:b].rearrange("p (a b) -> p a b", b=S),
                                                          ps[n][:, 0:b - a].rearrange("p (a b) -> p a b", b=S),
                                                          cst("sin").unsqueeze(1).to_broadcast([P, w, S]), mul))
                nc.vector.tensor_tensor(rope_flat, rope_flat, sq_qk, add).then_inc(rope_ready, 1)
                dve.wait_ge(kk_sum_ready, 1)
                for n in range(2):
                    last = nc.vector.tensor_scalar(halves(kk_scale, n), two(4 + n), 1e-24, None, ALU.max)
                last.then_inc(kk_floor_ready, 1)

                def maximum(u):
                    dve.wait_ge(scores_ready, u + 1)
                    dve_then(dve, nc.vector.tensor_reduce(stats[:, 0, 2 * u:2 * u + 2], two(u % 4), AX, ALU.max))
                    nc.vector.tensor_scalar(stats[:, 0, 2 * u:2 * u + 2], stats[:, 0, 2 * u:2 * u + 2], -HD ** -0.5, None, mul)\
                        .then_inc(max_ready, 1)

                def normalise(u):
                    dve.wait_ge(exp_ready, 2 * u + 2)
                    dve_then(dve, nc.vector.reciprocal(stats[:, 2, 2 * u:2 * u + 2], stats[:, 1, 2 * u:2 * u + 2]))
                    for q in range(2):
                        nc.vector.tensor_scalar(probs[:, u % 2, q], probs[:, u % 2, q], stats[:, 2, 2 * u + q:2 * u + q + 1], None, mul)\
                            .then_inc(probs_ready, 1)

                def attend(u):
                    if u < UNITS:
                        maximum(u)
                    if u >= 1:
                        normalise(u - 1)

                def keys(d):
                    for i in range(RT):
                        dve_then(dve, nc.vector.tensor_scalar(K[:, d, i], rate[:, d, i], par("k_a", i), one_less_ka[:, i:i + 1], mul, add))
                    dve_then(dve, nc.vector.tensor_tensor(flat(K[:, d]), flat(K[:, d]), flat(k_in), mul))

                a = PARAM["k_a"][0]
                dve_then(dve, nc.vector.tensor_scalar(one_less_ka, param[:, a:a + RT], -1.0, 1.0, mul, add))
                attend(0)
                dve_then(dve, nc.vector.tensor_copy(reset.rearrange("p (a b) -> p a b", b=C),
                                                    cst("reset").unsqueeze(1).to_broadcast([P, RT * NCH, C])))
                dve.wait_ge(sig_ready, 16)
                keys(0)
                attend(1)
                keys(1)
                for i in range(RT):
                    nc.vector.scalar_tensor_tensor(bonus[:, i], r_in[:, i], par("r_k", i), K[:, 0, i], mul, mul).then_inc(bonus_in, 1)
                attend(2)
                dve.wait_ge(kk_scale_ready, 1)
                dve_then(dve, nc.vector.tensor_tensor(flat(kk), flat(kk), flat(kk_scale), mul))
                for d in range(2):
                    dve_then(dve, nc.vector.tensor_tensor_scan(flat(run[:, d]), reset, flat(sig[:, d]), 0.0, mul, add))
                attend(3)
                ends = run.rearrange("p d t (c n) -> p d t c n", n=C)
                dve_then(dve, nc.vector.tensor_copy(mid, ends[:, :, :, :, C // 2 - 1]))
                dve_then(dve, nc.vector.tensor_tensor(tail, ends[:, :, :, :, C - 1], mid, sub))
                for s in range(3):
                    dve_then(dve, nc.vector.tensor_tensor(factor[:, s, 0], tail[:, 0, :, s], mid[:, 0, :, s + 1], add))
                    dve_then(dve, nc.vector.tensor_tensor(factor[:, s, 1], mid[:, 1, :, 3 - s], tail[:, 1, :, 2 - s], add))
                attend(4)
                dve_then(dve, nc.vector.tensor_tensor(chunks(run), chunks(run),
                                                      mid.rearrange("p d t c -> p (d t c)").unsqueeze(2).to_broadcast([P, 32, C]), sub))
                attend(5)
                nc.vector.tensor_tensor(chunks(sig), chunks(run), chunks(sig), sub).then_inc(run_ready, 1)
                attend(6)
                for d in range(2):
                    dve_then(dve, nc.vector.tensor_tensor(flat(B[:, d]), flat(kk), flat(rate[:, d]), mul))
                attend(7)
                dve.wait_ge(scales_ready, 3)
                dve_then(dve, nc.vector.tensor_tensor(flat(R[:, 0]), flat(R[:, 0]), flat(r_in), mul))
                dve_then(dve, nc.vector.tensor_tensor(flat(R[:, 1]), flat(A[:, 1]), flat(r_in), mul))
                attend(8)
                for d in range(2):
                    dve_then(dve, nc.vector.scalar_tensor_tensor(flat(A[:, d]), flat(A[:, d]), -1.0, flat(kk), mul, mul))
                dve.wait_ge(scales_ready, 5)
                for d, scale in ((0, run[:, 0]), (1, sig[:, 1])):
                    dve_then(dve, nc.vector.tensor_tensor(flat(B[:, d]), flat(B[:, d]), flat(scale), mul))
                    dve_then(dve, nc.vector.tensor_tensor(flat(K[:, d]), flat(K[:, d]), flat(scale), mul))
                for n in range(2):
                    dve.wait_ge(bonus_sum, n + 1)
                    dve_then(dve, nc.vector.tensor_tensor(halves(bonus, n), two(4 + n), halves(v_in, n), mul))

            @block.scalar
            def _(act):
                nc.scalar.activation(low[0:64, :], low[0:64, :], ACT.Tanh).then_inc(low_ready, 1)
                nc.scalar.activation(gate_low, gate_low, ACT.Sigmoid).then_inc(low_ready, 1)
                for n, (a, b) in enumerate(QK_SPANS):
                    act.wait_ge(qk_sum_ready, n + 1)
                    act_then(act, nc.scalar.activation(rstd_qk[:, a:b], ps[4 + n][:, 0:b - a], ACT.Ln, scale=1.0 / HD, bias=par("eps")))
                for n, (a, b) in enumerate(QK_SPANS):
                    nc.scalar.activation(rstd_qk[:, a:b], rstd_qk[:, a:b], ACT.Exp, scale=-0.5).then_inc(qk_rstd_ready, 1)
                act.wait_ge(ranks_ready, 1)
                for d in range(2):
                    for i in range(RT):
                        nc.scalar.activation(sig[:, d, i], ps[2 * d + i // 2][:, (i % 2) * S:(i % 2 + 1) * S], ACT.Sigmoid,
                                             bias=par("w0_b" if d else "w0_f", i)).then_inc(sig_ready, 1)
                act.wait_ge(ranks_ready, 2)
                for d in range(2):
                    for i in range(RT):
                        nc.scalar.activation(rate[:, d, i], ps[4 + 2 * d + i // 2][:, (i % 2) * S:(i % 2 + 1) * S], ACT.Sigmoid,
                                             bias=par("a0_b" if d else "a0_f", i)).then_inc(sig_ready, 1)
                act.wait_ge(gate_done, 1)
                for n in range(2):
                    nc.scalar.activation(halves(gate, n), two(6 + n), ACT.Copy).then_inc(gate_copied, 1)

                def exponentials(u):
                    act.wait_ge(max_ready, u + 1)
                    if u >= 2:
                        act.wait_ge(probs_turned, u - 1)
                    for q in range(2):
                        nc.scalar.activation(probs[:, u % 2, q], ps[u % 4][:, q * S:(q + 1) * S], ACT.Exp, scale=HD ** -0.5,
                                             bias=stats[:, 0, 2 * u + q:2 * u + q + 1],
                                             accum_out=stats[:, 1, 2 * u + q:2 * u + q + 1]).then_inc(exp_ready, 1)

                def copy_turned(u):
                    act.wait_ge(probs_turned, u + 1)
                    if u >= 2:
                        act.wait_ge(heads_ready, u - 1)
                    nc.scalar.activation(probs_t[:, u % 2], two(4 + u % 2), ACT.Copy).then_inc(turned_copied, 1)

                def copy_heads(i):
                    act.wait_ge(heads_ready, 2 * i + 2)
                    nc.scalar.activation(yT[:, 4 + i], ps[6 + i % 2][:, 0:S], ACT.Copy).then_inc(heads_copied, 1)

                for u in range(UNITS + 2):
                    if u < UNITS:
                        exponentials(u)
                    if 1 <= u <= UNITS:
                        copy_turned(u - 1)
                    if u >= 3 and u % 2:
                        copy_heads((u - 3) // 2)
                    if u == 0:
                        act.wait_ge(kk_floor_ready, 1)
                        act_then(act, nc.scalar.activation(flat(kk_scale), flat(kk_scale), ACT.Ln, scale=KK_SCALE))
                        nc.scalar.activation(flat(kk_scale), flat(kk_scale), ACT.Exp, scale=-0.5, bias=par("kk_bias")).then_inc(kk_scale_ready, 1)
                    if u == 6:
                        act.wait_ge(run_ready, 1)
                        for out, src, s in ((R[:, 0], run[:, 0], -DECAY_C), (A[:, 1], run[:, 1], DECAY_C), (A[:, 0], sig[:, 0], -DECAY_C)):
                            nc.scalar.activation(flat(out), flat(src), ACT.Exp, scale=s).then_inc(scales_ready, 1)
                    if u == 7:
                        act.wait_ge(scales_ready, 3)
                        nc.scalar.activation(flat(run[:, 0]), flat(run[:, 0]), ACT.Exp, scale=DECAY_C).then_inc(scales_ready, 1)
                        nc.scalar.activation(flat(sig[:, 1]), flat(sig[:, 1]), ACT.Exp, scale=-DECAY_C).then_inc(scales_ready, 1)
                        nc.scalar.activation(factor, factor, ACT.Exp, scale=-DECAY_C).then_inc(scales_ready, 1)

            @block.tensor
            def _(pe):
                def ranks(rows, bank):
                    for d in range(2):
                        up = sml("up_b" if d else "up_f")
                        for i in range(RT):
                            last = nc.tensor.matmul(ps[bank + 2 * d + i // 2][:, (i % 2) * S:(i % 2 + 1) * S], up[rows, i * P:(i + 1) * P],
                                                    low[rows, :], start=True, stop=True)
                    last.then_inc(ranks_ready, 1)

                pe.wait_ge(rest_loaded, 32)
                pe.wait_ge(qk_sq_ready, 1)
                for n, (a, b) in enumerate(QK_SPANS):
                    nc.tensor.matmul(ps[4 + n][:, 0:b - a], cst("headsum"), sq_qk[:, a:b], start=True, stop=True).then_inc(qk_sum_ready, 1)
                pe.wait_ge(low_ready, 2)
                ranks(slice(0, 64), 0)
                pe.wait_ge(qk_rstd_ready, 1)
                ranks(slice(64, 128), 4)
                pe.wait_ge(sig_ready, 8)
                pe.wait_ge(qk_normed, 5)
                for n, (a, b) in enumerate(QK_SPANS):
                    nc.tensor.matmul(ps[n][:, 0:b - a], cst("rot"), qk_flat[:, a:b], start=True, stop=True).then_inc(rotated, 1)
                pe.wait_ge(sig_ready, 16)
                pe.wait_ge(kk_sq_ready, 1)
                for n in range(2):
                    last = nc.tensor.matmul(ps[4 + n][:, :], cst("headsum"), halves(kk_sq, n), start=True, stop=True)
                last.then_inc(kk_sum_ready, 1)
                for i in range(RT):
                    last = nc.tensor.matmul(ps[6 + i // 2][:, (i % 2) * S:(i % 2 + 1) * S], sml("g_up")[:, i * P:(i + 1) * P], gate_low,
                                            start=True, stop=True)
                last.then_inc(gate_done, 1)
                pe.wait_ge(rope_ready, 1)

                def scores(u):
                    i, h = u // 2, u % 2
                    if u >= 4:
                        pe.wait_ge(exp_ready, 2 * (u - 3))
                    for q in range(2):
                        last = nc.tensor.matmul(ps[u % 4][:, q * S:(q + 1) * S], rope[HD * h:HD * (h + 1), i, q * P:(q + 1) * P],
                                                rope[HD * h:HD * (h + 1), 4], start=True, stop=True)
                    last.then_inc(scores_ready, 1)

                def turn(u):
                    pe.wait_ge(probs_ready, 2 * u + 2)
                    if u >= 2:
                        pe.wait_ge(turned_copied, u - 1)
                    for q in range(2):
                        for t in range(TT):
                            last = nc.tensor.transpose(ps[4 + u % 2][:, t * S + q * P:t * S + (q + 1) * P],
                                                       probs[:, u % 2, q, t * P:(t + 1) * P], ident)
                    last.then_inc(probs_turned, 1)

                def weigh(u):
                    i, h = u // 2, u % 2
                    pe.wait_ge(turned_copied, u + 1)
                    if i >= 2 and h == 0:
                        pe.wait_ge(heads_copied, i - 1)
                    for t in range(TT):
                        last = nc.tensor.matmul(ps[6 + i % 2][HD * h:HD * (h + 1), 0:S], v_tok[:, t, HD * h:HD * (h + 1)],
                                                probs_t[:, u % 2, t], start=(t == 0), stop=(t == TT - 1))
                    last.then_inc(heads_ready, 1)

                for u in range(UNITS + 2):
                    if u < UNITS:
                        scores(u)
                    if u == 1:
                        pe.wait_ge(kk_floor_ready, 1)
                    if u == 2:
                        pe.wait_ge(gate_copied, 2)
                    if 1 <= u <= UNITS:
                        turn(u - 1)
                    if u >= 2:
                        weigh(u - 2)
                pe.wait_ge(turned_copied, UNITS)
                pe.wait_ge(bonus_in, 4)
                for n in range(2):
                    nc.tensor.matmul(ps[4 + n][:, :], cst("headsum"), halves(bonus, n), start=True, stop=True).then_inc(bonus_sum, 1)

        def tile8(at):
            return area(at, 8, C)

        slots = []
        for q in range(2):
            at = TEMP_ + q * 3 * 1024
            slots.append({n: area(at + 1024 * j, 8, 2 * C) for j, n in enumerate(("X", "XT", "MT"))})
            at = TEMP_ + 8192 + q * 6 * 512
            slots[q].update({n: tile8(at + 512 * j) for j, n in enumerate(("AK", "RB", "RK", "Bt", "Kt", "Vt"))})
        product = [area(TEMP_ + 6144, 8, 2 * C), area(TEMP_ + 7168, 8, 2 * C)]
        state = [tile8(TEMP_ + 14336), tile8(TEMP_ + 14848)]
        W, U = tile8(TEMP_ + 15360), tile8(TEMP_ + 15872)
        yA = yT[:, 0:RT]
        SYSTEMS = [(d, t, h) for d in range(2) for t in range(RT) for h in range(2)]
        names = ("grams_ready", "grams_taken_dve", "grams_taken_act", "w_ready", "w_copied", "u_ready", "u_copied", "y_ready",
                 "y_taken", "s_ready", "state_ready")
        (grams_ready, grams_taken_dve, grams_taken_act, w_ready, w_copied, u_ready, u_copied, y_ready, y_taken, s_ready,
         state_ready) = (sem(n) for n in names)
        inverse_ready = [sem(f"inverse_ready{q}") for q in range(2)]
        product_ready = [sem(f"product_ready{q}") for q in range(2)]
        product_masked = [sem(f"product_masked{q}") for q in range(2)]
        blocks_ready = [sem(f"blocks_ready{q}") for q in range(2)]

        def both(name):
            return cst(name).rearrange("p (d n) -> p d n", d=2).unsqueeze(2).to_broadcast([P, 2, RT, C])

        def head_blocks(v, h):
            return v[HD * h:HD * (h + 1), :, C * h:C * (h + 1)]

        def dirs(v):
            return v.rearrange("p (d t) n -> p d t n", d=2)

        def bank8(b):
            return ps[b][:, :].rearrange("p (a n) -> p a n", n=C)

        def by_direction(v):
            return v.rearrange("p (d t) (h n) -> p d (t h) n", d=2, h=2)

        def both_heads(name):
            return cst(name).rearrange("p (d n) -> p d n", d=2).unsqueeze(2).to_broadcast([P, 2, 2 * RT, C])

        def gram_groups(s):
            return 8 * min(s, 2) + 7 * max(s - 2, 0)

        def act_groups(s):
            return 4 * min(s, 2) + 3 * max(s - 2, 0)

        def turned_v(s, p, d, t):
            if s < 2:
                return slots[s]["Vt"][p, RT * d + t]
            return slots[NCH - 1 - s]["Vt"][p, RT * (1 - d) + t]

        def side_by_side(b):
            return ps[b][:, :].rearrange("p (t x n) -> p t x n", t=RT, x=2)

        eye = ident.unsqueeze(1).to_broadcast([P, 8, 2 * C])
        zeroed = sem("zeroed")

        with nc.Block(no_gpsimd_drain=True) as block:
            @block.tensor
            def _(pe):
                def chunk(v, s, d, t, h):
                    c = s if d == 0 else NCH - 1 - s
                    return v[HD * h:HD * (h + 1), d, t, c * C:(c + 1) * C]

                def v_chunk(s, d, t, h):
                    c = s if d == 0 else NCH - 1 - s
                    return v_in[HD * h:HD * (h + 1), t, c * C:(c + 1) * C]

                def grams(s):
                    a_and_r = area(A_, 2, 2, RT, S)

                    def wait_for_bank(dve_count, act_count):
                        if s % 2:
                            if dve_count:
                                pe.wait_ge(grams_taken_dve, 4 * (s - 1) + dve_count)
                            if act_count:
                                pe.wait_ge(grams_taken_act, act_groups(s - 1) + act_count)

                    wait_for_bank(1, 0)
                    for d, t, h in SYSTEMS:
                        last = nc.tensor.matmul(bank8(0)[HD * h:HD * (h + 1), RT * d + t], chunk(A, s, d, t, h), chunk(B, s, d, t, h),
                                                start=True, stop=True)
                    last.then_inc(grams_ready, 1)
                    for bank, left, dve_count, act_count in ((1, B, (2, 2), 1), (3, K, (3, 4), 0)):
                        for d in range(2):
                            wait_for_bank(dve_count[d], act_count)
                            c = s if d == 0 else NCH - 1 - s
                            for t in range(RT):
                                for h in range(2):
                                    rows = slice(HD * h, HD * (h + 1))
                                    last = nc.tensor.matmul(ps[bank + d][rows, t * 2 * C:(t + 1) * 2 * C], chunk(left, s, d, t, h),
                                                            a_and_r[rows, :, d, t, c * C:(c + 1) * C], start=True, stop=True)
                            last.then_inc(grams_ready, 1)
                    for n, v in enumerate((B, K, None) if s < 2 else (B, K)):
                        wait_for_bank(0, n + 2)
                        for d, t, h in SYSTEMS:
                            left = v_chunk(s, d, t, h) if v is None else chunk(v, s, d, t, h)
                            last = nc.tensor.matmul(bank8(5 + n)[HD * h:HD * (h + 1), RT * d + t], left,
                                                    ident[HD * h:HD * (h + 1), HD * h:HD * (h + 1)], start=True, stop=True)
                        last.then_inc(grams_ready, 1)

                def pairs_product(bank, left, right):
                    for d in range(2):
                        for t in range(RT):
                            last = nc.tensor.matmul(ps[bank + d][:, t * 2 * C:(t + 1) * 2 * C], left[:, RT * d + t], right[:, RT * d + t],
                                                    start=True, stop=True)
                    return last

                def levels(s):
                    pe.wait_ge(grams_taken_dve, 4 * (s + 2))
                    pe.wait_ge(grams_taken_act, act_groups(s + 2))
                    for n in range(1, len(LEVELS)):
                        done = len(LEVELS) * (s // 2)
                        for q in range(2):
                            o = slots[q]
                            pe.wait_ge(inverse_ready[q], done + n)
                            pairs_product(4 * q, o["MT"], o["X"]).then_inc(product_ready[q], 1)
                        for q in range(2):
                            o = slots[q]
                            pe.wait_ge(product_masked[q], (len(LEVELS) - 1) * (s // 2) + n)
                            last = pairs_product(4 * q + 2, product[q], o["XT"])
                            if n < len(LEVELS) - 1:
                                last = pairs_product(4 * q, o["XT"], product[q])
                            last.then_inc(blocks_ready[q], 1)

                def recur(s):
                    o, now = slots[s % 2], state[s % 2]
                    pe.wait_ge(inverse_ready[s % 2], len(LEVELS) * (s // 2 + 1))
                    if s:
                        pe.wait_ge(state_ready, s)
                    for d, t, h in SYSTEMS:
                        p, j = slice(HD * h, HD * (h + 1)), RT * d + t
                        if s:
                            nc.tensor.matmul(bank8(4)[p, j], chunk(A, s, d, t, h), now[p, j], start=True, stop=False)
                        last = nc.tensor.matmul(bank8(4)[p, j], o["AK"][p, j], turned_v(s, p, d, t), start=(s == 0), stop=True)
                    last.then_inc(w_ready, 1)
                    pe.wait_ge(w_copied, s + 1)
                    for d, t, h in SYSTEMS:
                        p, j = slice(HD * h, HD * (h + 1)), RT * d + t
                        last = nc.tensor.matmul(bank8(5)[p, j], o["XT"][p, j, C * h:C * (h + 1)], W[p, j], start=True, stop=True)
                    last.then_inc(u_ready, 1)
                    pe.wait_ge(u_copied, s + 1)
                    if s < NCH - 1:
                        for d, t, h in SYSTEMS:
                            p, j = slice(HD * h, HD * (h + 1)), RT * d + t
                            nc.tensor.matmul(bank8(1)[p, j], o["Bt"][p, j], U[p, j], start=True, stop=False)
                            last = nc.tensor.matmul(bank8(1)[p, j], o["Kt"][p, j], turned_v(s, p, d, t), start=False, stop=True)
                        last.then_inc(s_ready, 1)
                    if s:
                        pe.wait_ge(y_taken, s)
                    for d, t, h in SYSTEMS:
                        p, j = slice(HD * h, HD * (h + 1)), RT * d + t
                        if s:
                            nc.tensor.matmul(bank8(0)[p, j], now[p, j], chunk(R, s, d, t, h), start=True, stop=False)
                        nc.tensor.matmul(bank8(0)[p, j], U[p, j], o["RB"][p, j], start=(s == 0), stop=False)
                        last = nc.tensor.matmul(bank8(0)[p, j], turned_v(s, p, d, t), o["RK"][p, j], start=False, stop=True)
                    last.then_inc(y_ready, 1)

                for s in range(0, NCH, 2):
                    if s:
                        pe.wait_ge(y_taken, s)
                        pe.wait_ge(state_ready, s)
                    grams(s)
                    grams(s + 1)
                    levels(s)
                    recur(s)
                    recur(s + 1)

            @block.scalar
            def _(act):
                for s in range(0, NCH, 2):
                    for q in range(2):
                        o = slots[q]
                        for n, (name, bank) in enumerate((("MT", 1), ("Bt", 5), ("Kt", 6), ("Vt", 7))):
                            if name == "Vt" and s + q >= 2:
                                continue
                            act.wait_ge(grams_ready, gram_groups(s + q) + bank + 1)
                            if name == "MT":
                                act.wait_ge(grams_ready, gram_groups(s + q) + 3)
                                if s + q < 1:
                                    act.wait_ge(zeroed, 2)
                                for d in range(2):
                                    for h in range(2):
                                        rows = slice(HD * h, HD * (h + 1))
                                        last = nc.scalar.activation(head_blocks(o[name], h)[:, RT * d:RT * (d + 1)],
                                                                    side_by_side(1 + d)[rows, :, 0], ACT.Copy)
                            else:
                                last = nc.scalar.activation(o[name], bank8(bank), ACT.Copy)
                            last.then_inc(grams_taken_act, 1)
                    for r in (s, s + 1):
                        act.wait_ge(w_ready, r + 1)
                        nc.scalar.activation(W, bank8(4), ACT.Copy).then_inc(w_copied, 1)
                        act.wait_ge(u_ready, r + 1)
                        nc.scalar.activation(U, bank8(5), ACT.Copy).then_inc(u_copied, 1)

            @block.vector
            def _(dve):
                def y_out(s):
                    dve.wait_ge(y_ready, s + 1)
                    for d, c in ((0, s), (1, NCH - 1 - s)):
                        out, src = yA[:, :, c * C:(c + 1) * C], bank8(0)[:, RT * d:RT * (d + 1)]
                        if s < 2:
                            last = nc.vector.tensor_copy(out, src)
                        else:
                            last = nc.vector.tensor_tensor(out, out, src, add)
                    last.then_inc(y_taken, 1)

                def masked_product(q, d, name):
                    mask = cst(name)[:, d * C:(d + 1) * C].unsqueeze(1).to_broadcast([P, 2 * RT, C])
                    return nc.vector.tensor_tensor(product[q][:, RT * d:RT * (d + 1)].rearrange("p t (h n) -> p (t h) n", h=2),
                                                   bank8(4 * q + d), mask, mul)

                def add_pairs(v, bank):
                    for d in range(2):
                        w = v[:, RT * d:RT * (d + 1)].rearrange("p t n -> p (t n)")
                        last = nc.vector.tensor_tensor(w, w, ps[bank + d][:, :], add)
                    return last

                for q in range(2):
                    nc.vector.memset(area(TEMP_ + q * 3 * 1024, 3 * 1024), 0.0).then_inc(zeroed, 1)
                dve.wait_ge(zeroed, 2)
                for s in range(0, NCH, 2):
                    for q in range(2):
                        o = slots[q]
                        base = gram_groups(s + q)
                        dve.wait_ge(grams_ready, base + 1)
                        for h in range(2):
                            p = slice(HD * h, HD * (h + 1))
                            last = nc.vector.tensor_tensor(dirs(head_blocks(o["X"], h)), dirs(bank8(0)[p]), both("level1")[p], mul)
                        last.then_inc(grams_taken_dve, 1)
                        def masked(name, bank, x, mask, d):
                            m = cst(mask)[:, d * C:(d + 1) * C].unsqueeze(1).to_broadcast([P, RT, C])
                            return nc.vector.tensor_tensor(o[name][:, RT * d:RT * (d + 1)], side_by_side(bank + d)[:, :, x], m, mul)

                        dve.wait_ge(grams_taken_dve, 4 * (s + q) + 1)
                        dve_then(dve, nc.vector.tensor_tensor(o["X"], o["X"], eye, add))
                        dve.wait_ge(grams_taken_act, act_groups(s + q) + 1)
                        dve_then(dve, nc.vector.tensor_tensor(by_direction(o["XT"]), by_direction(o["MT"]), both_heads("level1_t"), mul))
                        nc.vector.tensor_tensor(o["XT"], o["XT"], eye, add).then_inc(inverse_ready[q], 1)
                        for d in range(2):
                            last = masked("RB", 1, 1, "read", d)
                        last.then_inc(grams_taken_dve, 1)
                        for d in range(2):
                            dve.wait_ge(grams_ready, base + 4 + d)
                            masked("AK", 3, 0, "strict", d)
                            masked("RK", 3, 1, "read", d).then_inc(grams_taken_dve, 1)
                    for n in range(1, len(LEVELS)):
                        done = (len(LEVELS) - 1) * (s // 2)
                        for q in range(2):
                            dve.wait_ge(product_ready[q], done + n)
                            for d in range(2):
                                last = masked_product(q, d, f"level{LEVELS[n]}")
                            last.then_inc(product_masked[q], 1)
                        for q in range(2):
                            o = slots[q]
                            dve.wait_ge(blocks_ready[q], done + n)
                            if n < len(LEVELS) - 1:
                                add_pairs(o["X"], 4 * q)
                            add_pairs(o["XT"], 4 * q + 2).then_inc(inverse_ready[q], 1)
                    for r in (s, s + 1):
                        if r < NCH - 1:
                            dve.wait_ge(s_ready, r + 1)
                            scale = factor[:, r].rearrange("p d t -> p (d t)").unsqueeze(2).to_broadcast([P, 8, C])
                            new = state[(r + 1) % 2]
                            if r == 0:
                                nc.vector.tensor_tensor(new, bank8(1), scale, mul).then_inc(state_ready, 1)
                            else:
                                dve_then(dve, nc.vector.tensor_tensor(new, bank8(1), state[r % 2], add))
                                nc.vector.tensor_tensor(new, new, scale, mul).then_inc(state_ready, 1)
                        y_out(r)

        y_sq, y_rstd = area(A_, RT, S), area(R_, RT, S)
        (mean_ready, centred, var_ready, y_rstd_ready, gated) = (
            sem(n) for n in ("mean_ready", "centred", "var_ready", "y_rstd_ready", "gated"))
        with nc.Block(no_gpsimd_drain=True) as block:
            @block.tensor
            def _(pe):
                for n in range(2):
                    nc.tensor.matmul(ps[n][:, :], cst("headsum"), halves(yA, n), start=True, stop=True).then_inc(mean_ready, 1)
                for n in range(2):
                    pe.wait_ge(centred, n + 1)
                    nc.tensor.matmul(ps[2 + n][:, :], cst("headsum"), halves(y_sq, n), start=True, stop=True).then_inc(var_ready, 1)

            @block.scalar
            def _(act):
                split_high(act, G_OUT0)
                x_high(act, yT, (2, 3))
                for n in range(2):
                    act.wait_ge(var_ready, n + 1)
                    act_then(act, nc.scalar.activation(halves(y_rstd, n), two(2 + n), ACT.Ln, scale=1.0 / HD, bias=par("gn_eps")))
                for n in range(2):
                    nc.scalar.activation(halves(y_rstd, n), halves(y_rstd, n), ACT.Exp, scale=-0.5).then_inc(y_rstd_ready, 1)
                x_high(act, yT, (0, 1), lambda j: act.wait_ge(gated, j + 1))

            @block.vector
            def _(dve):
                for n in range(2):
                    dve.wait_ge(mean_ready, n + 1)
                    dve_then(dve, nc.vector.scalar_tensor_tensor(halves(yA, n), two(n), -1.0 / HD, halves(yA, n), mul, add))
                    nc.vector.tensor_tensor(halves(y_sq, n), halves(yA, n), halves(yA, n), mul).then_inc(centred, 1)
                split_low(dve, G_OUT0)
                x_low(dve, 1, yT, (2, 3))
                for n in range(2):
                    dve.wait_ge(y_rstd_ready, n + 1)
                    y = halves(yA, n)
                    dve_then(dve, nc.vector.tensor_tensor(y, y, halves(y_rstd, n), mul))
                    for i in (2 * n, 2 * n + 1):
                        dve_then(dve, nc.vector.tensor_scalar(yA[:, i], yA[:, i], par("gn_w", i), par("gn_b", i), mul, add))
                    dve_then(dve, nc.vector.tensor_tensor(y, y, halves(bonus, n), add))
                    nc.vector.tensor_tensor(y, y, halves(gate, n), mul).then_inc(gated, 1)
                for n in range(2):
                    x_low(dve, 1, yT, (n,), 2 + n)

        out_added = sem("out_added")

        def project_out(pe, first_group, first_tile, m):
            for j in range(KT):
                g, n = first_group + j // GROUP, j % GROUP
                if n != 1:
                    tile_ready(pe, g, n)
                w = tile_parts(g, n)
                for k in range(KT):
                    if j == 0 and k % 2 == 0:
                        pe.wait_ge(x_split_ready, 4 * m + k // 2 + 1)
                    last = split_product(ps[j // 2][:, (j % 2) * S:(j % 2 + 1) * S], (w[0][:, k], w[1][:, k]), x_parts(k), k == 0, k == KT - 1)
                last.then_inc(tile_done, 1)

        def add_out(dve, use, first_tile, squares):
            for n in range(4):
                dve.wait_ge(tile_done, first_tile + 2 * n + 2)
                x = xT[:, 2 * n:2 * n + 2]
                nc.vector.tensor_tensor(x, x, two(n), add).then_inc(out_added, 1)
                dve.wait_ge(out_added, 8 * use + n + 1)
                nc.vector.tensor_tensor(squares[:, 2 * n:2 * n + 2], x, x, mul).then_inc(squares_ready, 1)

        PAIR_BANK = [4, 5, 6, 7]
        squares1 = area(0, KT, S)
        silu_f, hidden_f = area(2048, 2, S), area(2048 + 2 * S, 2, S)
        hidden_split = parts("hidden", (4096, 4096 + 2 * S), [2, S])
        (acc_zero, pair_done, silu_ready, product_done, hidden_high, hidden_ready, down_done) = (
            sem(n) for n in ("acc_zero", "pair_done", "silu_ready", "product_done", "hidden_high", "hidden_ready", "down_done"))

        with nc.Block(no_gpsimd_drain=True) as block:
            @block.sync
            def _(sp):
                load_ahead(sp, G_IN0 + N_IN0 - 1, G_FFN + FT)

            @block.tensor
            def _(pe):
                project_out(pe, G_OUT0, T_OUT0, 1)
                norm_sum(pe, 1, squares1)

                def pair(t, j, first=False):
                    w = tile_pair(G_FFN + j)
                    pe.wait_ge(front_split, t + (G_FFN + 1))
                    for m in range(2):
                        for k in range(KT):
                            if first and m == 0 and k % 2 == 0:
                                pe.wait_ge(x_split_ready, 4 * 2 + k // 2 + 1)
                            last = split_product(ps[PAIR_BANK[j % 4]][:, m * S:(m + 1) * S], (w[0][:, k, m], w[1][:, k, m]), x_parts(k),
                                           k == 0, k == KT - 1)
                    last.then_inc(pair_done, 1)

                def down(t, j):
                    w = tile_parts(G_FFN + j, 2)
                    pe.wait_ge(back_split, t + (G_FFN + 1))
                    pe.wait_ge(hidden_ready, t + 1)
                    for k in range(KT):
                        last = split_product(ps[k // 2][:, (k % 2) * S:(k % 2 + 1) * S], (w[0][:, k], w[1][:, k]),
                                       (hidden_split[0][:, j % 2], hidden_split[1][:, j % 2]), False, False, skip_group_check=True)
                    last.then_inc(down_done, 1)

                pair(0, 0, first=True)
                pe.wait_ge(acc_zero, 3)
                with pe.Fori(0, FT // 4) as i:
                    for j in range(4):
                        pair(i * 4 + (j + 1), j + 1)
                        down(i * 4 + j, j)
                pair(FT - 1, 1)
                down(FT - 2, 0)
                down(FT - 1, 1)

            @block.scalar
            def _(act):
                split_high(act, G_OUT0 + 1)
                split_high(act, G_OUT0 + 2, T_OUT0 + 3)

                def pair_high(j, i=0):
                    g = G_FFN + j
                    act.wait_ge(slot_loaded[g % RING], i * 16 + 16 * (g // RING + 1))
                    for n in range(2):
                        high_part(piece(w_split[0], g % 2, n), piece(ring, g % RING, n)).then_inc(front_high, 1)

                def down_high(j):
                    g = G_FFN + j
                    high_part(piece(w_split[0], g % 2, 2), piece(ring, g % RING, 2)).then_inc(back_high, 1)

                def hidden(t, j):
                    act.wait_ge(pair_done, t + 1)
                    nc.scalar.activation(silu_f[:, j % 2], ps[PAIR_BANK[j % 4]][:, 0:S], ACT.Silu).then_inc(silu_ready, 1)
                    act.wait_ge(product_done, t + 1)
                    high_part(hidden_split[0][:, j % 2], hidden_f[:, j % 2]).then_inc(hidden_high, 1)

                act.wait_ge(tile_done, T_OUT0 + 2 * GROUP)
                pair_high(0)
                down_high(0)
                act.wait_ge(tile_done, T_OUT0 + KT)
                pair_high(1)
                norm_rstd(act, 1)
                x_high(act, xn, ready=xn_pair(act, 1))
                act.wait_ge(back_split, G_FFN)
                with act.Fori(0, FT // 4) as i:
                    for j in range(4):
                        t = i * 4 + j
                        hidden(t, j)
                        pair_high(j + 2, i)
                        act.wait_ge(down_done, t + 1)
                        down_high(j + 1)
                hidden(FT - 2, 0)
                act.wait_ge(down_done, FT - 1)
                down_high(1)
                hidden(FT - 1, 1)

            @block.vector
            def _(dve):
                for n in range(1, N_OUT0):
                    split_low(dve, G_OUT0 + n)
                add_out(dve, 0, T_OUT0, squares1)

                def pair_low(t, j):
                    g = G_FFN + j
                    for n in range(2):
                        dve.wait_ge(front_high, t * 2 + (2 * G_FFN + n + 1))
                        last = low_part(piece(w_split[1], g % 2, n), piece(ring, g % RING, n), piece(w_split[0], g % 2, n))
                    last.then_inc(front_split, 1)

                def down_low(t, j):
                    g = G_FFN + j
                    dve.wait_ge(back_high, t + (G_FFN + 1))
                    low_part(piece(w_split[1], g % 2, 2), piece(ring, g % RING, 2), piece(w_split[0], g % 2, 2)).then_inc(back_split, 1)

                def hidden(t, j):
                    dve.wait_ge(silu_ready, t + 1)
                    nc.vector.tensor_tensor(hidden_f[:, j % 2], silu_f[:, j % 2], ps[PAIR_BANK[j % 4]][:, S:2 * S], mul)                        .then_inc(product_done, 1)
                    dve.wait_ge(hidden_high, t + 1)
                    low_part(hidden_split[1][:, j % 2], hidden_f[:, j % 2], hidden_split[0][:, j % 2]).then_inc(hidden_ready, 1)

                pair_low(0, 0)
                norm_scale_split(dve, 1, "e_norm2", 2)
                down_low(0, 0)
                pair_low(1, 1)
                dve.wait_ge(out_added, 4)
                for n in range(4):
                    nc.vector.memset(ps[n][:, :], 0.0).then_inc(acc_zero if n else down_done, 1)
                with dve.Fori(0, FT // 4) as i:
                    for j in range(4):
                        t = i * 4 + j
                        hidden(t, j)
                        pair_low(t + 2, j + 2)
                        down_low(t + 1, j + 1)
                hidden(FT - 2, 0)
                down_low(FT - 1, 1)
                hidden(FT - 1, 1)
                dve.wait_ge(down_done, FT + 1)
                for n in range(4):
                    x = xT[:, 2 * n:2 * n + 2]
                    nc.vector.tensor_tensor(x, x, two(n), add).then_inc(out_added, 1)

        q1, k1 = area(0, GH, S), area(1024, GH, S)
        v1 = area(2048, TT, D)
        swish = area(4096, KT, S)
        G = area(6144, 2, GH, S)
        run1 = area(8192, 2, GH, S)
        squares2 = area(10240, KT, S)
        reset1, low1 = area(12288, GH * S), area(13312, S)
        gate_up = small[0:GRANK, 0:2 * RW]
        (gates_loaded, low1_ready, proj1_copied, low1_copied, z_ready, z_copied) = (
            sem(n) for n in ("gates_loaded", "low1_ready", "proj1_copied", "low1_copied", "z_ready", "z_copied"))

        Q1, K1 = area(10240, 2, GH, S), area(12288, 2, GH, S)
        G8, run8 = area(6144, 2 * GH * S), area(8192, 2 * GH * S)
        GS = 1.0 / 16
        abs_ready, log_ready, run1_ready, scales1_ready, qk1_ready = (
            sem(n) for n in ("abs_ready", "log_ready", "run1_ready", "scales1_ready", "qk1_ready"))
        fills = []
        for i in range(4):
            fills += [("v", 3 * i, i), ("q", 3 * i + 2, i)]
        fills += [("k", 12 + 2 * i, i) for i in range(2)] + [("gate", 16 + 2 * i, i) for i in range(4)]

        with nc.Block(no_gpsimd_drain=True) as block:
            @block.sync
            def _(sp):
                sp.dma_start(gate_up, io["gate_up"]).then_inc(gates_loaded, 16)
                load_ahead(sp, G_FFN + FT, G_OUT1)

            @block.tensor
            def _(pe):
                norm_sum(pe, 2, squares2)
                for j, (kind, first, _) in enumerate(fills):
                    if j >= 4:
                        pe.wait_ge(proj1_copied, j - 3)
                    if kind == "v":
                        g = G_IN1 + first // GROUP
                        tile_ready(pe, g, 1)
                        w = tuple(v[:, g % 2, 0:2 * D].rearrange("p (i k n) -> p k i n", i=2, k=KT) for v in w_split)
                        for t in range(TT):
                            for k in range(KT):
                                if j == 0 and t == 0 and k % 2 == 0:
                                    pe.wait_ge(x_split_ready, 4 * 3 + k // 2 + 1)
                                tokens = tuple(v[:, k, t * P:(t + 1) * P] for v in x_split)
                                last = split_product(ps[j % 4][:, t * S:(t + 1) * S], tokens, (w[0][:, k], w[1][:, k]), k == 0, k == KT - 1)
                            last.then_inc(tile_done, 1)
                        if j == 0:
                            pe.wait_ge(xn_ready, 3 * KT)
                            for k in range(KT):
                                last = nc.tensor.matmul(ps[4][0:GRANK, 0:S], sml("w_gd")[:, k * GRANK:(k + 1) * GRANK], xn[:, k],
                                                        start=(k == 0), stop=(k == KT - 1))
                            last.then_inc(low1_ready, 1)
                    else:
                        for i in range(first, first + (1 if kind == "q" else 2)):
                            g, n = G_IN1 + i // GROUP, i % GROUP
                            tile_ready(pe, g, n)
                            w = tile_parts(g, n)
                            for k in range(KT):
                                last = split_product(ps[j % 4][:, (i - first) * S:(i - first + 1) * S], (w[0][:, k], w[1][:, k]), x_parts(k),
                                               k == 0, k == KT - 1)
                            last.then_inc(tile_done, 1)
                    if 1 <= j <= 4:
                        pe.wait_ge(low1_copied, 1)
                        pe.wait_ge(gates_loaded, 16)
                        if j >= 3:
                            pe.wait_ge(z_copied, 2 * (j - 2))
                        d, n = (j - 1) // 2, (j - 1) % 2
                        for h in (2 * n, 2 * n + 1):
                            last = nc.tensor.matmul(ps[5 + n][:, (h % 2) * S:(h % 2 + 1) * S],
                                                    gate_up[:, d * RW + h * P:d * RW + (h + 1) * P], low1[0:GRANK, :], start=True, stop=True)
                        last.then_inc(z_ready, 1)

            @block.scalar
            def _(act):
                split_high(act, G_IN1)
                norm_rstd(act, 2)
                x_high(act, xn, ready=xn_pair(act, 2))
                split_high(act, G_IN1 + 1)
                act.wait_ge(low1_ready, 1)
                nc.scalar.activation(low1[0:GRANK, :], ps[4][0:GRANK, 0:S], ACT.Copy).then_inc(low1_copied, 1)

                def z_copy(m):
                    d, n = m // 2, m % 2
                    act.wait_ge(z_ready, m + 1)
                    for h in (2 * n, 2 * n + 1):
                        nc.scalar.activation(G[:, d, h], ps[5 + n][:, (h % 2) * S:(h % 2 + 1) * S], ACT.Identity,
                                             bias=par("bias_b" if d else "bias_f", h)).then_inc(z_copied, 1)

                split = 2
                for j, (kind, first, i) in enumerate(fills):
                    end = first + (1 if kind == "q" else 2)
                    if (end - 1) // GROUP + 2 == split < N_IN1:
                        split_high(act, G_IN1 + split, T_IN1 + GROUP * (split - 1))
                        split += 1
                    act.wait_ge(tile_done, T_IN1 + end)
                    func = ACT.Copy
                    if kind == "v":
                        dst, src = v1[:, :, i * S:(i + 1) * S], two(j % 4)
                    elif kind == "q":
                        dst, src = q1[:, i], ps[j % 4][:, 0:S]
                    elif kind == "k":
                        dst, src = k1[:, 2 * i:2 * i + 2], two(j % 4)
                    else:
                        dst, src, func = swish[:, 2 * i:2 * i + 2], two(j % 4), ACT.Silu
                    nc.scalar.activation(dst, src, func).then_inc(proj1_copied, 1)
                    if 1 <= j <= 4:
                        z_copy(j - 1)
                    if j == 6:
                        act.wait_ge(abs_ready, 1)
                        act_then(act, nc.scalar.activation(run8, run8, ACT.Exp))
                        nc.scalar.activation(run8, run8, ACT.Ln, bias=par("one")).then_inc(log_ready, 1)
                    if j == 9:
                        act.wait_ge(run1_ready, 3)
                        for out, src, s in ((Q1[:, 0], run1[:, 0], GS), (K1[:, 0], run1[:, 0], -GS), (Q1[:, 1], G[:, 1], -GS),
                                            (K1[:, 1], G[:, 1], GS)):
                            nc.scalar.activation(flat(out), flat(src), ACT.Exp, scale=s).then_inc(scales1_ready, 1)
                        nc.scalar.activation(factor, factor, ACT.Exp, scale=GS).then_inc(scales1_ready, 1)

            @block.vector
            def _(dve):
                dve.wait_ge(out_added, 8)
                norm_squares(dve, 2, squares2)
                split_low(dve, G_IN1)
                norm_scale_split(dve, 2, "o_norm1", 3)
                nc.vector.tensor_copy(reset1.rearrange("p (a b) -> p a b", b=C), cst("reset").unsqueeze(1).to_broadcast([P, GH * NCH, C]))
                for g in range(1, 5):
                    split_low(dve, G_IN1 + g)
                dve.wait_ge(z_copied, 8)
                dve_then(dve, nc.vector.tensor_scalar(run8, G8, -1.0, None, mul))
                nc.vector.tensor_tensor(run8, run8, G8, ALU.min).then_inc(abs_ready, 1)
                split_low(dve, G_IN1 + 5)
                dve.wait_ge(log_ready, 1)
                dve_then(dve, nc.vector.scalar_tensor_tensor(G8, G8, 0.0, run8, ALU.min, sub))
                for d in range(2):
                    dve_then(dve, nc.vector.tensor_tensor_scan(flat(run1[:, d]), reset1, flat(G[:, d]), 0.0, mul, add))
                split_low(dve, G_IN1 + 6)
                nc.vector.tensor_tensor(G8, run8, G8, sub).then_inc(run1_ready, 1)
                dve.wait_ge(run1_ready, 1)
                L = run1.rearrange("p d t (c n) -> p d t c n", n=C)
                X = G.rearrange("p d t (c n) -> p d t c n", n=C)
                dve_then(dve, nc.vector.tensor_copy(mid[:, 0], L[:, 0, :, :, C // 2]))
                dve_then(dve, nc.vector.tensor_copy(mid[:, 1], X[:, 1, :, :, C // 2 - 1]))
                dve_then(dve, nc.vector.tensor_tensor(tail, L[:, :, :, :, C - 1], mid, sub))
                for s in range(3):
                    dve_then(dve, nc.vector.tensor_tensor(factor[:, s, 0], tail[:, 0, :, s], mid[:, 0, :, s + 1], add))
                    dve_then(dve, nc.vector.tensor_tensor(factor[:, s, 1], mid[:, 1, :, 3 - s], tail[:, 1, :, 2 - s], add))
                for d, v in ((0, run1), (1, G)):
                    w = v[:, d].rearrange("p t (c n) -> p (t c) n", n=C)
                    nc.vector.tensor_tensor(w, w, mid[:, d].rearrange("p t c -> p (t c)").unsqueeze(2).to_broadcast([P, 16, C]), sub)\
                        .then_inc(run1_ready, 1)
                split_low(dve, G_IN1 + 7)
                dve.wait_ge(scales1_ready, 5)
                dve.wait_ge(proj1_copied, 10)
                for d in range(2):
                    dve_then(dve, nc.vector.scalar_tensor_tensor(flat(Q1[:, d]), flat(Q1[:, d]), P ** -0.5, flat(q1), mul, mul))
                    nc.vector.tensor_tensor(flat(K1[:, d]), flat(K1[:, d]), flat(k1), mul).then_inc(qk1_ready, 1)

        states = area(14336, 3, 2, GH, 2 * P)
        K_tok = area(6144, TT, 2, GH, P)
        att = area(8192, TT, 2, GH, C)
        both_att = area(9216, TT, GH, 2 * C)
        o_tok = area(0, TT, GH, 2 * P)
        o_stats = sb("o_stats", [P, 2, TT, GH])
        (outputs_zero, k1_turned, k1_copied, att_ready, att_taken, att_masked, add1_ready, states_ready, o_ready, o_sq_ready, o_rstd_ready,
         o_scaled, o_turned, mixed1) = (
            sem(n) for n in ("outputs_zero", "k1_turned", "k1_copied", "att_ready", "att_taken", "att_masked", "add1_ready", "states_ready", "o_ready",
                             "o_sq_ready", "o_rstd_ready", "o_scaled", "o_turned", "mixed1"))

        with nc.Block(no_gpsimd_drain=True) as block:
            @block.vector
            def _(dve):
                dve_then(dve, nc.vector.memset(area(8192, 2048), 0.0))
                for t in range(TT):
                    dve.wait_ge(att_ready, t + 1)
                    for d in range(2):
                        last = nc.vector.copy_predicated(att[:, t, d], cst("read")[:, d * C:(d + 1) * C].bitcast(u32).unsqueeze(1).to_broadcast([P, GH, C]),
                                                         bank8(t)[:, GH * d:GH * (d + 1)])
                    last.then_inc(att_taken, 1)
                    dve.wait_ge(att_taken, t + 1)
                    for b in range(2):
                        rows = slice(C * b, C * (b + 1))
                        last = nc.vector.tensor_tensor(both_att[rows, t, :, rows], att[rows, t, 0], att[rows, t, 1], add)
                    last.then_inc(att_masked, 1)
                for n in range(4):
                    if n >= 2:
                        dve.wait_ge(k1_copied, n - 1)
                    nc.vector.memset(ps[n][:, :], 0.0).then_inc(outputs_zero, 1)
                for s in range(3):
                    for n in range(4):
                        d, h = n // 2, 2 * (n % 2)
                        dve.wait_ge(add1_ready, 4 * s + n + 1)
                        new = states[:, s, d, h:h + 2]
                        scale = factor[:, s, d, h:h + 2].unsqueeze(2).to_broadcast([P, 2, 2 * P])
                        if s == 0:
                            nc.vector.tensor_tensor(new, two(4 + n), scale, mul).then_inc(states_ready, 1)
                        else:
                            dve_then(dve, nc.vector.tensor_tensor(new, two(4 + n), states[:, s - 1, d, h:h + 2], add))
                            nc.vector.tensor_tensor(new, new, scale, mul).then_inc(states_ready, 1)
                for t in range(TT):
                    dve.wait_ge(o_rstd_ready, t + 1)
                    for h in range(GH):
                        nc.vector.tensor_scalar(o_tok[:, t, h], ps[2 * t + h // 2][:, (h % 2) * S:(h % 2 + 1) * S],
                                                o_stats[:, 1, t, h:h + 1], None, mul).then_inc(o_scaled, 1)
                for j in range(GH):
                    dve.wait_ge(o_turned, j + 1)
                    for v in range(2):
                        i = 2 * j + v
                        last = nc.vector.scalar_tensor_tensor(yT[:, i], ps[4 + j][:, v * S:(v + 1) * S], par("out_norm", v), swish[:, i], mul, mul)
                    last.then_inc(mixed1, 1)
                    if j:
                        x_low(dve, 4, yT, (j - 1,), j - 1)
                x_low(dve, 4, yT, (3,), 3)
                split_low(dve, G_OUT1)

            @block.scalar
            def _(act):
                for n in range(4):
                    act.wait_ge(k1_turned, n + 1)
                    nc.scalar.activation(K_tok[:, n // 2, n % 2], ps[2 + n][:, :].rearrange("p (h n) -> p h n", h=GH), ACT.Copy)\
                        .then_inc(k1_copied, 1)
                for t in range(TT):
                    for h in range(GH):
                        act.wait_ge(o_ready, 2 * t + h // 2 + 1)
                        nc.scalar.activation(o_tok[:, t, h], ps[2 * t + h // 2][:, (h % 2) * S:(h % 2 + 1) * S], ACT.Square,
                                             accum_out=o_stats[:, 0, t, h:h + 1]).then_inc(o_sq_ready, 1)
                for t in range(TT):
                    act.wait_ge(o_sq_ready, GH * TT)
                    act_then(act, nc.scalar.activation(o_stats[:, 1, t], o_stats[:, 0, t], ACT.Ln, scale=1.0 / (2 * P), bias=par("eps")))
                for t in range(TT):
                    nc.scalar.activation(o_stats[:, 1, t], o_stats[:, 1, t], ACT.Exp, scale=-0.5).then_inc(o_rstd_ready, 1)
                split_high(act, G_OUT1)
                x_high(act, yT, ready=lambda j: act.wait_ge(mixed1, j + 1))

            @block.tensor
            def _(pe):
                pe.wait_ge(qk1_ready, 2)
                for t in range(TT):
                    for d in range(2):
                        for h in range(GH):
                            for b in range(2):
                                c = slice((2 * t + b) * C, (2 * t + b + 1) * C)
                                last = nc.tensor.matmul(bank8(t)[C * b:C * (b + 1), GH * d + h], K1[:, d, h, c], Q1[:, d, h, c], start=True, stop=True)
                    last.then_inc(att_ready, 1)
                for n in range(4):
                    for h in range(GH):
                        last = nc.tensor.transpose(ps[2 + n][:, h * P:(h + 1) * P], K1[:, n % 2, h, (n // 2) * P:(n // 2 + 1) * P], ident)
                    last.then_inc(k1_turned, 1)
                pe.wait_ge(k1_copied, 4)

                def output(t, h):
                    return ps[2 * t + h // 2][:, (h % 2) * S:(h % 2 + 1) * S]

                def chunk_terms():
                    pe.wait_ge(att_masked, TT)
                    pe.wait_ge(outputs_zero, 4)
                    for t in range(TT):
                        for h in range(GH):
                            nc.tensor.matmul(output(t, h), both_att[:, t, h], v1[:, t, h * 2 * P:(h + 1) * 2 * P],
                                             start=False, stop=False, skip_group_check=True)

                def state_terms(s):
                    pe.wait_ge(states_ready, 4 * (s + 1))
                    for d, c in ((1, NCH - 2 - s), (0, s + 1)):
                        for h in range(GH):
                            last = nc.tensor.matmul(output(c // 2, h)[C * (c % 2):C * (c % 2 + 1)], Q1[:, d, h, c * C:(c + 1) * C],
                                                    states[:, s, d, h], start=False, stop=False, skip_group_check=True)
                            if s == 2 and h % 2:
                                last.then_inc(o_ready, 1)

                for s in range(3):
                    for n in range(4):
                        d = n // 2
                        c = s if d == 0 else NCH - 1 - s
                        rows = slice(C * (c % 2), C * (c % 2 + 1))
                        if s:
                            pe.wait_ge(states_ready, 4 * (s - 1) + n + 1)
                        for h in (2 * (n % 2), 2 * (n % 2) + 1):
                            last = nc.tensor.matmul(ps[4 + n][:, (h % 2) * S:(h % 2 + 1) * S], K_tok[rows, c // 2, d, h],
                                                    v1[rows, c // 2, h * 2 * P:(h + 1) * 2 * P], start=True, stop=True)
                        last.then_inc(add1_ready, 1)
                    if s == 0:
                        chunk_terms()
                    else:
                        state_terms(s - 1)
                state_terms(2)
                for t in range(TT):
                    for j in range(GH):
                        pe.wait_ge(o_scaled, GH * t + j + 1)
                        for v in range(2):
                            last = nc.tensor.transpose(ps[4 + j][:, v * S + t * P:v * S + (t + 1) * P], o_tok[:, t, j, v * P:(v + 1) * P], ident)
                        if t:
                            last.then_inc(o_turned, 1)

        w_moe = io["w_moe"].rearrange("e t p n -> (e t) p n")
        N_MOE = E * FET

        def load_front(sp, tile, g, split):
            sp.wait_ge(front_split, split)
            sp.dma_start(ring[:, g % RING, 0:2 * D], w_moe[bass.ds(tile, 1), :, 0:2 * D].rearrange("a p n -> (a p) n"))\
                .then_inc(slot_loaded[g % RING], 16)

        def load_back(sp, tile, g, split):
            sp.wait_ge(back_split, split)
            sp.dma_start(ring[:, g % RING, 2 * D:], w_moe[bass.ds(tile, 1), :, 2 * D:].rearrange("a p n -> (a p) n"))\
                .then_inc(back_loaded[g % RING], 16)

        def front_high_part(act, g, n, turns):
            if n == 0:
                act.wait_ge(slot_loaded[g % RING], (turns + (g // RING + 1)) * 16)
            high_part(piece(w_split[0], g % 2, n), piece(ring, g % RING, n)).then_inc(front_high, 1)

        def back_high_part(act, g, turns):
            act.wait_ge(back_loaded[g % RING], (turns + ((g - G_MOE) // RING + 1)) * 16)
            high_part(piece(w_split[0], g % 2, 2), piece(ring, g % RING, 2)).then_inc(back_high, 1)

        def front_low_part(dve, g, n, tiles):
            dve.wait_ge(front_high, tiles * 2 + (2 * g + n + 1))
            last = low_part(piece(w_split[1], g % 2, n), piece(ring, g % RING, n), piece(w_split[0], g % 2, n))
            if n:
                last.then_inc(front_split, 1)

        def back_low_part(dve, g, tiles):
            dve.wait_ge(back_high, tiles + (g + 1))
            low_part(piece(w_split[1], g % 2, 2), piece(ring, g % RING, 2), piece(w_split[0], g % 2, 2)).then_inc(back_split, 1)

        squares3 = area(0, KT, S)
        x_tok1 = area(0, TT, D)
        logits, top_idx_f = area(11264, TT, E), area(11280, TT, E)
        top = area(11296, TT, E)
        top_idx = sb("top_idx", [P, TT, E], u32)
        gap = area(11312, 4, TT)
        chosen, weight, hot = area(11328, TT, E), area(11344, TT, E), area(11360, 2, TT, E)
        rank, counts = area(11392, TT, E), area(11408, E)
        most = area(11416, 1)
        more = sb("more", [P, PASSES], i32)
        (logits_ready, turned1, tok1_copied, gap_ready, gap_exp, chosen_ready, ranks1_ready, routed) = (
            sem(n) for n in ("logits_ready", "turned1", "tok1_copied", "gap_ready", "gap_exp", "chosen_ready", "ranks1_ready", "routed"))

        with nc.Block(no_gpsimd_drain=True) as block:
            @block.sync
            def _(sp):
                load_ahead(sp, G_OUT1, G_MOE)
                load_front(sp, RING, G_MOE + RING, G_MOE + 1)
                load_front(sp, RING + 1, G_MOE + RING + 1, G_MOE + 2)
                load_back(sp, RING, G_MOE + RING, G_MOE + 1)

            @block.tensor
            def _(pe):
                project_out(pe, G_OUT1, T_OUT1, 4)
                norm_sum(pe, 3, squares3)
                for t in range(TT):
                    for k in range(KT):
                        pe.wait_ge(xn_ready, 3 * KT + k + 1)
                        last = nc.tensor.matmul(ps[4][:, t * E:(t + 1) * E], xn[:, k, t * P:(t + 1) * P], sml("router")[:, k * E:(k + 1) * E],
                                                start=(k == 0), stop=(k == KT - 1))
                last.then_inc(logits_ready, 1)
                for n in range(4):
                    for k in range(4 * (n % 2), 4 * (n % 2) + 4):
                        last = nc.tensor.transpose(ps[n][:, (k % 4) * P:(k % 4 + 1) * P], xn[:, k, (n // 2) * P:(n // 2 + 1) * P], ident)
                    last.then_inc(turned1, 1)
                pe.wait_ge(chosen_ready, 1)
                nc.tensor.matmul(ps[5][:, 0:E], cst("before"), chosen[:, 0], start=True, stop=True)
                nc.tensor.matmul(ps[5][:, E:2 * E], cst("ones"), chosen[:, 0], start=True, stop=False)
                nc.tensor.matmul(ps[5][:, E:2 * E], cst("before"), chosen[:, 1], start=False, stop=True)
                nc.tensor.matmul(ps[5][:, 2 * E:3 * E], cst("ones"), chosen[:, 0], start=True, stop=False)
                nc.tensor.matmul(ps[5][:, 2 * E:3 * E], cst("ones"), chosen[:, 1], start=False, stop=True).then_inc(ranks1_ready, 1)

            @block.scalar
            def _(act):
                split_high(act, G_OUT1 + 1)
                split_high(act, G_OUT1 + 2, T_OUT1 + 3)
                act.wait_ge(tile_done, T_OUT1 + 2 * GROUP)
                for n in range(2):
                    front_high_part(act, G_MOE, n, 0)
                back_high_part(act, G_MOE, 0)
                norm_rstd(act, 3)
                for n in range(2):
                    front_high_part(act, G_MOE + 1, n, 0)
                act.wait_ge(gap_ready, 1)
                nc.scalar.activation(gap[:, 1], gap[:, 0], ACT.Exp).then_inc(gap_exp, 1)
                for n in range(4):
                    act.wait_ge(turned1, n + 1)
                    nc.scalar.activation(x_tok1[:, n // 2, (n % 2) * 512:(n % 2 + 1) * 512], ps[n][:, :], ACT.Copy).then_inc(tok1_copied, 1)

            @block.vector
            def _(dve):
                for n in range(1, N_OUT1):
                    split_low(dve, G_OUT1 + n)
                add_out(dve, 1, T_OUT1, squares3)
                for n in range(2):
                    front_low_part(dve, G_MOE, n, 0)
                norm_scale(dve, 3, "o_norm2")
                back_low_part(dve, G_MOE, 0)
                for n in range(2):
                    front_low_part(dve, G_MOE + 1, n, 0)
                dve.wait_ge(logits_ready, 1)
                dve_then(dve, nc.vector.tensor_copy(logits.rearrange("p t e -> p (t e)"), ps[4][:, 0:TT * E]))
                for t in range(TT):
                    dve_then(dve, nc.vector.max(top[:, t], logits[:, t]))
                    dve_then(dve, nc.vector.max_index(top_idx[:, t], top[:, t], logits[:, t]))
                dve_then(dve, nc.vector.tensor_copy(top_idx_f, top_idx[:, :, :]))
                nc.vector.tensor_tensor(gap[:, 0], top[:, :, 1], top[:, :, 0], sub).then_inc(gap_ready, 1)
                for n in range(2):
                    for t in range(TT):
                        dve_then(dve, nc.vector.tensor_scalar(hot[:, n, t], cst("experts"), top_idx_f[:, t, n:n + 1], None, ALU.is_equal))
                nc.vector.tensor_tensor(chosen, hot[:, 0], hot[:, 1], add).then_inc(chosen_ready, 1)
                dve.wait_ge(gap_exp, 1)
                dve_then(dve, nc.vector.tensor_scalar(gap[:, 2], gap[:, 1], 1.0, None, add))
                dve_then(dve, nc.vector.reciprocal(gap[:, 2], gap[:, 2]))
                dve_then(dve, nc.vector.tensor_tensor(gap[:, 3], gap[:, 1], gap[:, 2], mul))
                for t in range(TT):
                    dve_then(dve, nc.vector.tensor_scalar(weight[:, t], hot[:, 0, t], gap[:, 2, t:t + 1], None, mul))
                    dve_then(dve, nc.vector.scalar_tensor_tensor(weight[:, t], hot[:, 1, t], gap[:, 3, t:t + 1], weight[:, t], mul, add))
                dve.wait_ge(ranks1_ready, 1)
                dve_then(dve, nc.vector.tensor_copy(rank.rearrange("p t e -> p (t e)"), ps[5][:, 0:2 * E]))
                dve_then(dve, nc.vector.tensor_copy(counts, ps[5][:, 2 * E:3 * E]))
                dve_then(dve, nc.vector.tensor_reduce(most, counts, AX, ALU.max))
                for p in range(PASSES):
                    last = nc.vector.tensor_scalar(more[:, p:p + 1], most, float(CAP * p), None, ALU.is_gt)
                last.then_inc(routed, 1)

        place = area(2048, TT, E, CAP)
        placed_weight = area(3584, TT, E, CAP)
        back = area(5120, E, S)
        silu_e, hidden_e = area(7168, 2, P), area(7168 + 2 * P, 2, P)
        y_slot = area(7680, D)
        slots_split = parts("slots", (9216, 9216 + KT * CAP), [KT, CAP])
        turned_split = parts("turned", (9216 + 2 * KT * CAP, 9216 + (2 * KT + 2) * CAP), [2, CAP])
        place_flat, back_flat = area(2048, TT * E, CAP), area(5120, E * S)
        rank_p = area(11424, TT, E)
        (placed, weights_placed, back_turned, back_copied, gathered, slots_high, slots_ready, pair_e_done, silu_e_ready, hidden_e_ready, turned_e,
         turned_high, turned_ready, down_e_done, y_copied, scattered, x_added) = (
            sem(n) for n in ("placed", "weights_placed", "back_turned", "back_copied", "gathered", "slots_high", "slots_ready", "pair_e_done",
                             "silu_e_ready", "hidden_e_ready", "turned_e", "turned_high", "turned_ready", "down_e_done", "y_copied",
                             "scattered", "x_added"))
        TURNS = FET // RING - 1
        SCATTER_BANK = [2, 3, 7, 2]

        class Pass:

            def __init__(self, p):
                self.p, self.tiles0, self.e0 = p, N_MOE * p, E * p
                self.g0 = G_MOE + self.tiles0

        def all_passes(eng, body):
            body(eng, Pass(0))
            for p in range(1, PASSES):
                with eng.If(eng.value_load(more[0:1, p:p + 1], min_val=0, max_val=1) > 0):
                    body(eng, Pass(p))

        def moe_loads(sp, at):
            def turn(i, j):
                load_front(sp, i * RING + (j + 1), at.g0 + j + 1, i * RING + (at.g0 + j - RING + 2))
                load_back(sp, i * RING + j, at.g0 + j, i * RING + (at.g0 + j - RING + 1))

            if at.p == 0:
                for j in range(1, RING):
                    turn(1, j)
            else:
                load_front(sp, 0, at.g0, at.g0 - RING + 1)
            with sp.Fori(2 if at.p == 0 else 0, N_MOE // RING - 1) as i:
                for j in range(RING):
                    turn(i, j)
            for j in range(RING - 1):
                turn(N_MOE // RING - 1, j)
            load_back(sp, N_MOE - 1, at.g0 + RING - 1, at.g0 + N_MOE - RING)

        def moe_products(pe, at):
            p, tiles0, e0, g0 = at.p, at.tiles0, at.e0, at.g0
            def turn_weights(n):
                pe.wait_ge(weights_placed, TT * (p + 1))
                if n >= 2:
                    pe.wait_ge(back_copied, 4 * p + n - 1)
                for e in (2 * n, 2 * n + 1):
                    for t in range(TT):
                        last = nc.tensor.transpose(ps[2 + n % 2][0:CAP, (e % 2) * S + t * P:(e % 2) * S + (t + 1) * P],
                                                   placed_weight[:, t, e], ident)
                last.then_inc(back_turned, 1)

            def gather(e, n):
                for k in range(4 * n, 4 * n + 4):
                    for t in range(TT):
                        last = nc.tensor.matmul(ps[2 + n][:, (k % 4) * CAP:(k % 4 + 1) * CAP], x_tok1[:, t, k * P:(k + 1) * P],
                                                place_flat[:, bass.ds(e + t * E, 1)].rearrange("p a n -> p (a n)"),
                                                start=(t == 0), stop=(t == TT - 1))
                last.then_inc(gathered, 1)

            def pair_rows(t, rows):
                g = g0 + t
                w = tile_pair(g)
                for k in rows:
                    last = split_product(ps[4 + t % 2][0:CAP, 0:2 * P],  (slots_split[0][:, k], slots_split[1][:, k]),
                                   (w[0][:, k].rearrange("p m n -> p (m n)"), w[1][:, k].rearrange("p m n -> p (m n)")),
                                   k == 0, k == KT - 1)
                return last

            def pair(e, at_tile, t, turned=True):
                pe.wait_ge(front_split, e * FET + at_tile + (g0 + t + 1))
                pair_rows(t, range(3))
                if turned:
                    turn(e, at_tile, t - 1)
                pair_rows(t, range(3, KT)).then_inc(pair_e_done, 1)

            def turn(e, at_tile, t):
                pe.wait_ge(hidden_e_ready, e * FET + at_tile + (tiles0 + t + 1))
                nc.tensor.transpose(ps[6 + t % 2][:, 0:CAP], hidden_e[0:CAP, t % 2], ident[0:CAP, 0:CAP]).then_inc(turned_e, 1)

            def down(e, at_tile, t, first=False):
                w = [piece(v, (g0 + t) % 2, 2) for v in w_split]
                pe.wait_ge(back_split, e * FET + at_tile + (g0 + t + 1))
                pe.wait_ge(turned_ready, e * FET + at_tile + (tiles0 + t + 1))
                for n in range(2):
                    last = split_product(ps[n][0:CAP, :], (turned_split[0][:, t % 2], turned_split[1][:, t % 2]),
                                   (w[0][:, n * 512:(n + 1) * 512], w[1][:, n * 512:(n + 1) * 512]), first, False, skip_group_check=True)
                last.then_inc(down_e_done, 1)

            def scatter(e, pieces):
                for r in pieces:
                    if r == 3:
                        pe.wait_ge(x_added, e * 4 + (4 * e0 + 1))
                    for k in (2 * r, 2 * r + 1):
                        last = nc.tensor.matmul(ps[SCATTER_BANK[r]][:, (k % 2) * S:(k % 2 + 1) * S], y_slot[0:CAP, k * P:(k + 1) * P],
                                                back_flat[0:CAP, bass.ds(e * S, S)], start=True, stop=True)
                    last.then_inc(scattered, 1)

            def expert(e, last):
                with pe.Fori(0, TURNS) as i:
                    for t in range(1, RING + 1):
                        pair(e, i * RING, t + 1)
                        down(e, i * RING, t)
                for t in range(FET - RING + 1, FET - 1):
                    pair(e, 0, t + 1)
                    down(e, 0, t)
                if not last:
                    pe.wait_ge(back_copied, 4 * (p + 1))
                    gather(e + 1, 0)
                turn(e, 0, FET - 1)
                if not last:
                    gather(e + 1, 1)
                down(e, 0, FET - 1)
                if not last:
                    pe.wait_ge(slots_ready, e * 2 + (2 * e0 + 4))
                    pair(e + 1, 0, 0, turned=False)
                pe.wait_ge(y_copied, e * 2 + (2 * e0 + 2))
                scatter(e, (0, 1))
                if not last:
                    pair(e + 1, 0, 1)
                scatter(e, (2, 3))
                if not last:
                    down(e + 1, 0, 0, first=True)

            pe.wait_ge(placed, TT * (p + 1))
            if p:
                pe.wait_ge(x_added, 4 * e0)
            for n in range(2):
                gather(0, n)
            pe.wait_ge(slots_ready, 2 * e0 + 2)
            pair(0, 0, 0, turned=False)
            for n in range(2):
                turn_weights(n)
            pair(0, 0, 1)
            for n in range(2, 4):
                turn_weights(n)
            down(0, 0, 0, first=True)
            with pe.Fori(0, E - 1) as e:
                expert(e, False)
            expert(E - 1, True)

        def moe_activations(act, at):
            p, tiles0, e0, g0 = at.p, at.tiles0, at.e0, at.g0

            def gathered_high(e):
                for n in range(2):
                    act.wait_ge(gathered, e * 2 + (2 * e0 + n + 1))
                    high_part(slots_split[0][:, 4 * n:4 * n + 4], ps[2 + n][:, 0:4 * CAP].rearrange("p (a b) -> p a b", a=4))\
                        .then_inc(slots_high, 1)

            def step(e, i, t, front=True, back=True, gather=False):
                done = e * FET + i * RING + (tiles0 + t + 1)
                act.wait_ge(pair_e_done, done)
                nc.scalar.activation(silu_e[0:CAP, t % 2], ps[4 + t % 2][0:CAP, 0:P], ACT.Silu).then_inc(silu_e_ready, 1)
                turns = e * (FET // RING) + i
                if front:
                    front_high_part(act, g0 + t + 2, 0, turns)
                act.wait_ge(turned_e, done)
                high_part(turned_split[0][:, t % 2], ps[6 + t % 2][:, 0:CAP]).then_inc(turned_high, 1)
                if gather:
                    gathered_high(e + 1)
                if front:
                    front_high_part(act, g0 + t + 2, 1, turns)
                if back:
                    act.wait_ge(down_e_done, done)
                    back_high_part(act, g0 + t + 1, turns)

            def expert(e, last):
                with act.Fori(0, TURNS) as i:
                    for t in range(1, RING + 1):
                        step(e, i, t)
                for t in range(1, RING):
                    end = t == RING - 1
                    step(e, TURNS, t, front=not (last and t >= RING - 2), back=not (last and end), gather=end and not last)
                act.wait_ge(down_e_done, e * FET + (tiles0 + FET + 1))
                nc.scalar.activation(y_slot[0:CAP, 512:1024], ps[1][0:CAP, :], ACT.Copy).then_inc(y_copied, 1)
                if not last:
                    step(e + 1, 0, 0)

            if p:
                act.wait_ge(down_e_done, tiles0 + 1)
                for n in range(2):
                    front_high_part(act, g0, n, 0)
                back_high_part(act, g0, 0)
                for n in range(2):
                    front_high_part(act, g0 + 1, n, 0)
            def back_copy(n):
                act.wait_ge(back_turned, 4 * p + n + 1)
                nc.scalar.activation(back[0:CAP, 2 * n:2 * n + 2], ps[2 + n % 2][0:CAP, :].rearrange("p (a b) -> p a b", a=2), ACT.Copy)\
                    .then_inc(back_copied, 1)

            gathered_high(0)
            for n in range(2):
                back_copy(n)
            step(0, 0, 0)
            for n in range(2, 4):
                back_copy(n)
            with act.Fori(0, E - 1) as e:
                expert(e, False)
            expert(E - 1, True)

        def moe_elementwise(dve, at):
            p, tiles0, e0, g0 = at.p, at.tiles0, at.e0, at.g0
            dve_then(dve, nc.vector.tensor_scalar(rank_p, rank, float(CAP * p), None, sub))
            for t in range(TT):
                slots_b = cst("slots").unsqueeze(1).to_broadcast([P, E, CAP])
                dve_then(dve, nc.vector.tensor_tensor(place[:, t], slots_b, rank_p[:, t].unsqueeze(2).to_broadcast([P, E, CAP]), ALU.is_equal))
                nc.vector.tensor_tensor(place[:, t], place[:, t], chosen[:, t].unsqueeze(2).to_broadcast([P, E, CAP]), mul)\
                    .then_inc(placed, 1)
            dve.wait_ge(placed, TT * (p + 1))
            for t in range(TT):
                nc.vector.tensor_tensor(placed_weight[:, t], place[:, t], weight[:, t].unsqueeze(2).to_broadcast([P, E, CAP]), mul)\
                    .then_inc(weights_placed, 1)
            if p == 0:
                nc.vector.memset(area(11440, 1), 0.0).then_inc(down_e_done, 1)

            def gathered_low(e):
                for n in range(2):
                    dve.wait_ge(slots_high, e * 2 + (2 * e0 + n + 1))
                    low_part(slots_split[1][:, 4 * n:4 * n + 4], ps[2 + n][:, 0:4 * CAP].rearrange("p (a b) -> p a b", a=4),
                             slots_split[0][:, 4 * n:4 * n + 4]).then_inc(slots_ready, 1)

            def add_scattered(e, pieces):
                for r in pieces:
                    dve.wait_ge(scattered, e * 4 + (4 * e0 + r + 1))
                    x = xT[:, 2 * r:2 * r + 2]
                    nc.vector.tensor_tensor(x, x, two(SCATTER_BANK[r]), add).then_inc(x_added, 1)

            def step(e, at_tile, t, front=True, back=True, gather=False, added=None):
                count = e * FET + at_tile + (tiles0 + t + 1)
                dve.wait_ge(silu_e_ready, count)
                nc.vector.tensor_tensor(hidden_e[0:CAP, t % 2], silu_e[0:CAP, t % 2], ps[4 + t % 2][0:CAP, P:2 * P], mul)\
                    .then_inc(hidden_e_ready, 1)
                if front:
                    front_low_part(dve, g0 + t + 2, 0, e * FET + at_tile)
                if added is not None:
                    add_scattered(added, (0, 1))
                dve.wait_ge(turned_high, count)
                low_part(turned_split[1][:, t % 2], ps[6 + t % 2][:, 0:CAP], turned_split[0][:, t % 2]).then_inc(turned_ready, 1)
                if gather:
                    gathered_low(e + 1)
                if front:
                    front_low_part(dve, g0 + t + 2, 1, e * FET + at_tile)
                if back:
                    back_low_part(dve, g0 + t + 1, e * FET + at_tile)

            def expert(e, last):
                with dve.Fori(0, TURNS) as i:
                    for t in range(1, RING + 1):
                        step(e, i * RING, t)
                for t in range(1, RING):
                    end = t == RING - 1
                    step(e, TURNS * RING, t, front=not (last and t >= RING - 2), back=not (last and end), gather=end and not last)
                dve.wait_ge(down_e_done, e * FET + (tiles0 + FET + 1))
                nc.vector.tensor_copy(y_slot[0:CAP, 0:512], ps[0][0:CAP, :]).then_inc(y_copied, 1)
                if last:
                    add_scattered(e, (0, 1))
                else:
                    step(e + 1, 0, 0, added=e)
                add_scattered(e, (2, 3))

            if p:
                for n in range(2):
                    front_low_part(dve, g0, n, 0)
                back_low_part(dve, g0, 0)
                for n in range(2):
                    front_low_part(dve, g0 + 1, n, 0)
            gathered_low(0)
            step(0, 0, 0)
            with dve.Fori(0, E - 1) as e:
                expert(e, False)
            expert(E - 1, True)

        with nc.Block(no_gpsimd_drain=True) as block:
            @block.sync
            def _(sp):
                all_passes(sp, moe_loads)

            @block.tensor
            def _(pe):
                all_passes(pe, moe_products)

            @block.scalar
            def _(act):
                all_passes(act, moe_activations)

            @block.vector
            def _(dve):
                all_passes(dve, moe_elementwise)


        y_tok = area(0, TT, D)
        (result_turned, result_copied, stored) = (sem(n) for n in ("result_turned", "result_copied", "stored"))
        with nc.Block(no_gpsimd_drain=True) as block:
            @block.tensor
            def _(pe):
                for n in range(4):
                    for k in range(4 * (n % 2), 4 * (n % 2) + 4):
                        last = nc.tensor.transpose(ps[n][:, (k % 4) * P:(k % 4 + 1) * P], xT[:, k, (n // 2) * P:(n // 2 + 1) * P], ident)
                    last.then_inc(result_turned, 1)

            @block.vector
            def _(dve):
                for n in range(4):
                    dve.wait_ge(result_turned, n + 1)
                    nc.vector.tensor_copy(y_tok[:, n // 2, (n % 2) * 512:(n % 2 + 1) * 512], ps[n][:, :]).then_inc(result_copied, 1)

            @block.sync
            def _(sp):
                for t in range(TT):
                    sp.wait_ge(result_copied, 2 * (t + 1))
                    sp.dma_start(io["out"][t * P:(t + 1) * P, :], y_tok[:, t]).then_inc(stored, 16)
                sp.wait_ge(stored, 32)


def _const():
    out = np.zeros((P, N_CONST), np.float32)

    def put(name, v):
        a, b = CONST[name]
        out[:, a:b] = v

    p = np.arange(P)
    put("ident", np.eye(P))
    put("headsum", (p[:, None] // HD == p[None] // HD))
    put("ones", 1.0)
    rot = np.zeros((P, P))
    even = p[::2]
    rot[even + 1, even] = -1.0
    rot[even, even + 1] = 1.0
    put("rot", rot)
    put("before", p[:, None] < p[None])
    t = np.arange(S)
    freq = (np.float32(10000.0) ** (-np.arange(0, HD // 2, 2, dtype=np.float32) / np.float32(HD // 2))).astype(np.float32)
    row, col = (t // 64).astype(np.float32), (t % 64).astype(np.float32)
    ang = np.concatenate([row[:, None] * freq, col[:, None] * freq], -1)
    ang = ang[:, (p % HD) // 2].T.astype(np.float64)
    put("cos", np.cos(ang))
    put("sin", np.sin(ang))
    r, c = (p % C)[:, None], np.arange(C)[None]
    low, up = r > c, r < c
    for b in LEVELS:
        pair = (r // (2 * b) == c // (2 * b)) & (r // b != c // b)
        put(f"level{b}", np.concatenate([pair & low, pair & up], 1))
        if b == 1:
            put("level1_t", np.concatenate([pair & up, pair & low], 1))
    put("strict", np.concatenate([up, low], 1))
    put("read", np.concatenate([r <= c, low], 1))
    put("ident64", r == c)
    put("slots", np.arange(CAP)[None])
    put("experts", np.arange(E)[None])
    put("reset", (c > 0) * np.ones((P, 1)))
    return out


def _tiles(w, size=P):
    k, n = w.shape
    return np.ascontiguousarray(w.reshape(k // P, P, n // P, P).transpose(2, 1, 0, 3)).reshape(n // P, P, k)


def _groups(tiles):
    n = -(-len(tiles) // GROUP)
    out = np.zeros((n * GROUP,) + tiles.shape[1:], tiles.dtype)
    out[:len(tiles)] = tiles
    return np.ascontiguousarray(out.reshape(n, GROUP, P, D).transpose(0, 2, 1, 3)).reshape(n, P, GROUP * D)


def _hidden_groups(gate, up, down):
    n = gate.shape[1] // P
    pairs = np.stack([_tiles(gate).reshape(n, P, KT, P), _tiles(up).reshape(n, P, KT, P)], 3)
    return np.concatenate([pairs.reshape(n, P, 2 * D), down.reshape(n, P, D)], 2)


def _arrays(i):
    def col(v):
        return np.asarray(v).reshape(-1, P).T

    i = {k: np.asarray(v) for k, v in i.items()}
    param = np.zeros((P, N_PARAM), np.float32)

    def put(name, v):
        a, b = PARAM[name]
        param[:, a:b] = v

    for name, key in [("e_norm1", "e_norm1"), ("mu", "e_shift_mu"), ("w0_f", "e_w0_f"), ("w0_b", "e_w0_b"), ("a0_f", "e_a0_f"),
                      ("a0_b", "e_a0_b"), ("k_k", "e_k_k"), ("k_a", "e_k_a"), ("r_k", "e_r_k"), ("gn_w", "e_gn_w"), ("gn_b", "e_gn_b"),
                      ("e_norm2", "e_norm2"), ("o_norm1", "o_norm1"), ("bias_f", "o_gate_bias_f"), ("bias_b", "o_gate_bias_b"),
                      ("out_norm", "o_out_norm"), ("o_norm2", "o_norm2")]:
        put(name, col(i[key]))
    for name, key in [("q_norm", "e_q_norm"), ("k_norm", "e_k_norm")]:
        put(name, np.concatenate([i[key][0], i[key][0]])[:, None])
    put("eps", EPS)
    put("gn_eps", GN_EPS)
    put("kk_bias", 0.5 * np.log(KK_SCALE))
    put("one", 1.0)

    small = np.zeros((P, N_SMALL), np.float32)

    def puts(name, v):
        a, b = SMALL[name]
        small[:v.shape[0], a:b] = v

    puts("up_f", np.concatenate([i["e_w_up_f"][0], i["e_a_up_f"][0]]))
    puts("up_b", np.concatenate([i["e_w_up_b"][0], i["e_a_up_b"][0]]))
    puts("g_up", i["e_g_up"][0])
    puts("router", i["o_router"][0].reshape(KT, P, E).transpose(1, 0, 2).reshape(P, KT * E))
    w1 = i["o_w_in"][0]
    puts("w_gd", w1[:, 2048:2064].reshape(KT, P, GRANK).transpose(1, 0, 2).reshape(P, KT * GRANK))

    w0 = i["e_w_in"][0]
    q = w0[:, RW_IN:RW_IN + ATT].reshape(D, 2, 4, HD).transpose(0, 2, 1, 3).reshape(D, ATT)
    w0 = np.concatenate([w0[:, :RW_IN], q, w0[:, RW_IN + ATT:]], 1)
    wo0 = i["e_w_out"][0]
    att = wo0[RW:].reshape(2, 4, HD, D).transpose(1, 0, 2, 3).reshape(ATT, D)
    wo0 = np.concatenate([wo0[:RW], att], 0)
    w1 = np.concatenate([w1[:, :2048], w1[:, 2064:]], 1)
    t1 = _tiles(w1)
    order = [n for g in range(4) for n in (8 + 2 * g, 9 + 2 * g, g)] + list(range(4, 8)) + list(range(16, 24))
    moe = np.stack([_hidden_groups(i["o_exp_gate"][0, e], i["o_exp_up"][0, e], i["o_exp_down"][0, e]) for e in range(E)])
    return {"x": np.ascontiguousarray(i["x"][0]), "const": _const(), "param": param, "small": small,
            "gate_up": np.concatenate([i["o_gate_up_f"][0], i["o_gate_up_b"][0]], 1),
            "w_in0": _groups(_tiles(w0)), "w_out0": _groups(_tiles(wo0)),
            "w_ffn": _hidden_groups(i["e_ffn_gate"][0], i["e_ffn_up"][0], i["e_ffn_down"][0]),
            "w_in1": _groups(t1[order]), "w_out1": _groups(_tiles(i["o_w_out"][0])), "w_moe": moe}


def kernel(**inputs):
    import concourse.bacc as _bacc
    from concourse.bass_utils import run_bass_kernel_spmd as _run

    nc = _bacc.Bacc("TRN2", target_bir_lowering=False, num_devices=1)
    arrays = _arrays(inputs)
    io = {n: nc.dram_tensor(f"in_{n}", a.shape, mybir.dt.float32, kind="ExternalInput").ap() for n, a in arrays.items()}
    io["out"] = nc.dram_tensor("out_y", (S, D), mybir.dt.float32, kind="ExternalOutput").ap()
    program(nc, io)
    r = _run(nc, [{f"in_{n}": a for n, a in arrays.items()}], core_ids=[0])
    return np.asarray(r.results[0]["out_y"]).reshape(1, S, D)
```
